# Optimizing a Trainium2 kernel written in Bass

```python
import math
import jax, jax.numpy as jnp
from jax import lax
import numpy as np

D_MODEL = 2048
BATCH = 1
SEQ = 256
DEPTH = 2

SSM_GROUP = 16
SSM_STATE = 64
SSM_GROUPS = D_MODEL // SSM_GROUP
HEAD_DIM = 128
N_HEADS = D_MODEL // HEAD_DIM
D_FF = 11 * D_MODEL // 4
CONV_WIDTH = 3
BLOCK_Q = 128
N_A_LAYERS = max(1, DEPTH // 2)
N_B_LAYERS = DEPTH - N_A_LAYERS
N_MOD = 6
NORM_EPS = 1e-6
STEP_MIN = 1e-3
STEP_MAX = 1e-1
FORGET_BIAS_MEAN = 3.0

kernel_name = "yoco_s5_fox_convffn_adaln"

def rms_norm(x, g):
    x32 = x.astype(jnp.float32)
    y = x32 * lax.rsqrt(jnp.mean(x32 * x32, axis=-1, keepdims=True) + NORM_EPS)
    return (y * g.astype(jnp.float32)).astype(x.dtype)

def modulate(h, shift, scale):
    return h * (1 + scale[:, None, :]) + shift[:, None, :]

def _complex_affine_combine(e1, e2):
    a1r, a1i, b1r, b1i = e1
    a2r, a2i, b2r, b2i = e2
    ar = a2r * a1r - a2i * a1i
    ai = a2r * a1i + a2i * a1r
    br = a2r * b1r - a2i * b1i + b2r
    bi = a2r * b1i + a2i * b1r + b2i
    return (ar, ai, br, bi)

def s5_ssm(u, log_step, a_re, a_im, b_re, b_im, c_re, c_im, d):
    bsz, seq, _ = u.shape
    f32 = jnp.float32
    ug = u.astype(f32).reshape(bsz, seq, SSM_GROUPS, SSM_GROUP)
    lam_re = a_re.astype(f32)
    lam_im = a_im.astype(f32)
    step = jnp.exp(log_step.astype(f32))[:, None]
    mag = jnp.exp(lam_re * step)
    abar_re = mag * jnp.cos(lam_im * step)
    abar_im = mag * jnp.sin(lam_im * step)
    den = lam_re * lam_re + lam_im * lam_im
    nr = abar_re - 1.0
    fr = (nr * lam_re + abar_im * lam_im) / den
    fi = (abar_im * lam_re - nr * lam_im) / den
    br = b_re.astype(f32)
    bi = b_im.astype(f32)
    bbar_re = fr[..., None] * br - fi[..., None] * bi
    bbar_im = fr[..., None] * bi + fi[..., None] * br
    bu_re = jnp.einsum('blgh,gph->blgp', ug, bbar_re)
    bu_im = jnp.einsum('blgh,gph->blgp', ug, bbar_im)
    shape = bu_re.shape
    elems = (jnp.broadcast_to(abar_re, shape), jnp.broadcast_to(abar_im, shape), bu_re, bu_im)
    _, _, s_re, s_im = lax.associative_scan(_complex_affine_combine, elems, axis=1)
    y = (jnp.einsum('blgp,ghp->blgh', s_re, c_re.astype(f32))
         - jnp.einsum('blgp,ghp->blgh', s_im, c_im.astype(f32))
         + d.astype(f32) * ug)
    return y.reshape(bsz, seq, D_MODEL).astype(u.dtype)

def s5_mixer(h, w_in, log_step, a_re, a_im, b_re, b_im, c_re, c_im, d, glu_w, glu_b, w_out):
    u = h @ w_in
    y = s5_ssm(u, log_step, a_re, a_im, b_re, b_im, c_re, c_im, d)
    g = jax.nn.gelu(y)
    z = g * jax.nn.sigmoid(g @ glu_w + glu_b)
    return z @ w_out

def forgetting_attention(q, k, v, f_cum):
    seq = q.shape[1]
    scale = HEAD_DIM ** -0.5
    outs = []
    for start in range(0, seq, BLOCK_Q):
        end = start + BLOCK_Q
        qb = q[:, start:end]
        kb = k[:, :end]
        vb = v[:, :end]
        s = jnp.einsum('bqhd,bkhd->bhqk', qb, kb).astype(jnp.float32) * scale
        s = s + f_cum[:, :, start:end, None] - f_cum[:, :, None, :end]
        q_pos = start + jnp.arange(BLOCK_Q)
        k_pos = jnp.arange(end)
        mask = k_pos[None, :] <= q_pos[:, None]
        s = jnp.where(mask[None, None], s, -jnp.inf)
        p = jax.nn.softmax(s, axis=-1).astype(vb.dtype)
        outs.append(jnp.einsum('bhqk,bkhd->bqhd', p, vb))
    return jnp.concatenate(outs, axis=1)

def causal_depthwise_conv(a, w, b):
    ch = a.shape[-1]
    out = lax.conv_general_dilated(
        a, w[:, None, :].astype(a.dtype), window_strides=(1,),
        padding=[(CONV_WIDTH - 1, 0)],
        dimension_numbers=('NWC', 'WIO', 'NWC'),
        feature_group_count=ch)
    return out + b

def conv_ffn(h, w_up, conv_w, conv_b, w_down):
    a = h @ w_up
    a = causal_depthwise_conv(a, conv_w, conv_b)
    u, v = jnp.split(a, 2, axis=-1)
    return (jax.nn.silu(u) * v) @ w_down

def setup_inputs(seed: int = 0) -> dict:
    key = jax.random.key(seed)
    ks = jax.random.split(key, 32)
    f32 = jnp.float32
    D, G, P, H, F = D_MODEL, SSM_GROUPS, SSM_STATE, SSM_GROUP, D_FF
    nrm = lambda k, shape, s: jax.random.normal(k, shape, f32) * s
    inp = {}
    inp['x'] = nrm(ks[0], (BATCH, SEQ, D), 1.0)
    inp['c'] = nrm(ks[1], (BATCH, D), 1.0)
    inp['mod_w'] = nrm(ks[2], (DEPTH, D, N_MOD * D), 0.5 * D ** -0.5)
    inp['mod_b'] = nrm(ks[3], (DEPTH, N_MOD * D), 0.01)
    inp['norm_mix_g'] = 1.0 + nrm(ks[4], (DEPTH, D), 0.02)
    inp['norm_ffn_g'] = 1.0 + nrm(ks[5], (DEPTH, D), 0.02)
    inp['ssm_w_in'] = nrm(ks[6], (N_A_LAYERS, D, D), D ** -0.5)
    inp['ssm_log_step'] = jax.random.uniform(ks[7], (N_A_LAYERS, G), f32,
                                             math.log(STEP_MIN), math.log(STEP_MAX))
    inp['ssm_a_re'] = -0.5 + nrm(ks[8], (N_A_LAYERS, G, P), 0.01)
    inp['ssm_a_im'] = (math.pi * jnp.arange(P, dtype=f32))[None, None, :] + nrm(ks[9], (N_A_LAYERS, G, P), 0.01)
    inp['ssm_b_re'] = nrm(ks[10], (N_A_LAYERS, G, P, H), (2 * H) ** -0.5)
    inp['ssm_b_im'] = nrm(ks[11], (N_A_LAYERS, G, P, H), (2 * H) ** -0.5)
    inp['ssm_c_re'] = nrm(ks[12], (N_A_LAYERS, G, H, P), P ** -0.5)
    inp['ssm_c_im'] = nrm(ks[13], (N_A_LAYERS, G, H, P), P ** -0.5)
    inp['ssm_d'] = nrm(ks[14], (N_A_LAYERS, G, H), 1.0)
    inp['ssm_glu_w'] = nrm(ks[15], (N_A_LAYERS, D, D), D ** -0.5)
    inp['ssm_glu_b'] = nrm(ks[16], (N_A_LAYERS, D), 0.01)
    inp['ssm_w_out'] = nrm(ks[17], (N_A_LAYERS, D, D), D ** -0.5)
    inp['kv_mod_w'] = nrm(ks[18], (D, 2 * D), 0.5 * D ** -0.5)
    inp['kv_mod_b'] = nrm(ks[19], (2 * D,), 0.01)
    inp['kv_norm_g'] = 1.0 + nrm(ks[20], (D,), 0.02)
    inp['kv_w'] = nrm(ks[21], (D, 2 * D + N_HEADS), D ** -0.5)
    inp['forget_b'] = FORGET_BIAS_MEAN + nrm(ks[22], (N_HEADS,), 0.5)
    inp['attn_w_q'] = nrm(ks[23], (N_B_LAYERS, D, D), D ** -0.5)
    inp['attn_w_out'] = nrm(ks[24], (N_B_LAYERS, D, D), D ** -0.5)
    inp['ffn_w_up'] = nrm(ks[25], (DEPTH, D, 2 * F), D ** -0.5)
    inp['ffn_conv_w'] = nrm(ks[26], (DEPTH, CONV_WIDTH, 2 * F), CONV_WIDTH ** -0.5)
    inp['ffn_conv_b'] = nrm(ks[27], (DEPTH, 2 * F), 0.01)
    inp['ffn_w_down'] = nrm(ks[28], (DEPTH, F, D), F ** -0.5)
    inp['final_norm_g'] = 1.0 + nrm(ks[29], (D,), 0.02)
    return inp

def reference(x, c, mod_w, mod_b, norm_mix_g, norm_ffn_g,
              ssm_w_in, ssm_log_step, ssm_a_re, ssm_a_im, ssm_b_re, ssm_b_im,
              ssm_c_re, ssm_c_im, ssm_d, ssm_glu_w, ssm_glu_b, ssm_w_out,
              kv_mod_w, kv_mod_b, kv_norm_g, kv_w, forget_b,
              attn_w_q, attn_w_out,
              ffn_w_up, ffn_conv_w, ffn_conv_b, ffn_w_down,
              final_norm_g):
    bsz, seq, _ = x.shape
    c_act = jax.nn.silu(c)
    k_sh = v_sh = f_cum = None
    for i in range(DEPTH):
        mod = c_act @ mod_w[i] + mod_b[i]
        sh_m, sc_m, g_m, sh_f, sc_f, g_f = jnp.split(mod, N_MOD, axis=-1)
        if i == N_A_LAYERS:
            kv_mod = c_act @ kv_mod_w + kv_mod_b
            sh_kv, sc_kv = jnp.split(kv_mod, 2, axis=-1)
            hk = modulate(rms_norm(x, kv_norm_g), sh_kv, sc_kv)
            kvf = hk @ kv_w
            k_sh = kvf[..., :D_MODEL].reshape(bsz, seq, N_HEADS, HEAD_DIM)
            v_sh = kvf[..., D_MODEL:2 * D_MODEL].reshape(bsz, seq, N_HEADS, HEAD_DIM)
            log_f = jax.nn.log_sigmoid(kvf[..., 2 * D_MODEL:].astype(jnp.float32)
                                       + forget_b.astype(jnp.float32))
            f_cum = jnp.transpose(jnp.cumsum(log_f, axis=1), (0, 2, 1))
        h = modulate(rms_norm(x, norm_mix_g[i]), sh_m, sc_m)
        if i < N_A_LAYERS:
            out = s5_mixer(h, ssm_w_in[i], ssm_log_step[i], ssm_a_re[i], ssm_a_im[i],
                           ssm_b_re[i], ssm_b_im[i], ssm_c_re[i], ssm_c_im[i], ssm_d[i],
                           ssm_glu_w[i], ssm_glu_b[i], ssm_w_out[i])
        else:
            j = i - N_A_LAYERS
            q = (h @ attn_w_q[j]).reshape(bsz, seq, N_HEADS, HEAD_DIM)
            o = forgetting_attention(q, k_sh, v_sh, f_cum)
            out = o.reshape(bsz, seq, D_MODEL) @ attn_w_out[j]
        x = x + g_m[:, None, :] * out
        h = modulate(rms_norm(x, norm_ffn_g[i]), sh_f, sc_f)
        out = conv_ffn(h, ffn_w_up[i], ffn_conv_w[i], ffn_conv_b[i], ffn_w_down[i])
        x = x + g_f[:, None, :] * out
    return rms_norm(x, final_norm_g)


_drawn_inputs = setup_inputs


def setup_inputs(seed=0):
    import zlib

    import numpy as np

    out = dict(_drawn_inputs(seed))
    spreads = {}
    factors = {'mod_b': 4.166,
     'norm_mix_g': 8.0,
     'norm_ffn_g': 6.371,
     'ssm_log_step': 47.88,
     'ssm_a_re': 64.0,
     'ssm_a_im': 42.976,
     'ssm_b_re': 59.288,
     'ssm_b_im': 60.016,
     'ssm_c_re': 59.32,
     'ssm_c_im': 60.352,
     'ssm_glu_b': 8.0,
     'kv_mod_b': 8.0,
     'kv_norm_g': 8.0,
     'ffn_conv_b': 8.0,
     'final_norm_g': 7.937}
    for name, (base, spread) in spreads.items():
        noise = np.random.default_rng([zlib.crc32(name.encode()), seed]).standard_normal(out[name].shape)
        drawn = base * np.exp(spread * noise) if base else spread * noise
        out[name] = __import__('jax').numpy.asarray(drawn.astype(out[name].dtype))
    for name, factor in factors.items():
        out[name] = (out[name] * factor).astype(out[name].dtype)
    return out
```

```python
from contextlib import ExitStack

import concourse.bass as bass
from concourse import mybir

F32 = mybir.dt.float32
F32R = mybir.dt.float32r
ALU = mybir.AluOpType
ACT = mybir.ActivationFunctionType
AX_X = mybir.AxisListType.X

P = 128
D = 2048
S = 256
KT = D // P
TB = S // P
FF = 11 * D // 4
FT = FF // P
HEADS = 16
GROUPS, STATE, GW = 128, 64, 16
ST = GROUPS * STATE // P
EPS = 1e-6
PI = 3.141592653589793
TWO_PI_DOWN = 6.2831850
ROUND = 12582912.0
TWO_PI_1 = 6.28125
TWO_PI_2 = 0.0019340515136718750
TWO_PI_3 = 2 * PI - TWO_PI_1 - TWO_PI_2
MASKED = -1.0e30

NRAW, NSPLIT, NMOD = 4, 2, 2
UK = 2
UC = 1024
WF = UK * UC
GU = KT // UK
DU = FT // UK

SH_M0, SC_M0, G_M0, SH_F0, SC_F0, G_F0, SH_KV, SC_KV, SH_M1, SC_M1, G_M1, SH_F1, SC_F1, G_F1 = range(14)

U_IN = 0
U_GLU = U_IN + 2 * GU
U_OUT = U_GLU + 2 * GU
U_UP0 = U_OUT + 2 * GU
U_DOWN0 = U_UP0 + 11 * GU
U_K = U_DOWN0 + 2 * DU
U_V = U_K + 2 * GU
U_Q = U_V + 2 * GU
U_AO = U_Q + 2 * GU
U_UP1 = U_AO + 2 * GU
U_DOWN1 = U_UP1 + 11 * GU
U_END = U_DOWN1 + 2 * DU

XG = KT
XD0 = XG + 2 * GU + KT
XD1 = XD0 + 2 * DU + 3 * KT
XN = (0, XG + 2 * GU, XD0 + 2 * DU, XD0 + 2 * DU + KT, XD0 + 2 * DU + 2 * KT)
BANK_DOWN = (0, 4)
PREP_DVE = 22


def flat(ap):
    return ap.rearrange("p a n -> p (a n)")


def ge(eng, sem, value):
    if not (isinstance(value, int) and value <= 0):
        eng.wait_ge(sem, value)


def steps(eng, n, step, emit):
    with eng.Fori(0, n // step) as i:
        for j in range(step):
            emit(i * step, j)


def trunk(nc, x, c, mod_w, mod_b, norm_mix_g, norm_ffn_g, ssm_w_in, ssm_log_step, ssm_a_re, ssm_a_im,
          ssm_b_re, ssm_b_im, ssm_c_re, ssm_c_im, ssm_d, ssm_glu_w, ssm_glu_b, ssm_w_out, kv_mod_w,
          kv_mod_b, kv_norm_g, kv_w, forget_b, attn_w_q, attn_w_out, ffn_w_up, ffn_conv_w, ffn_conv_b,
          ffn_w_down, final_norm_g, out):
    ctx = ExitStack()
    with ctx:
        top = [16512]

        def sb(name, shape, dt=F32, at=None):
            n = 2 if dt == mybir.dt.bfloat16 else 4
            for d in shape[1:]:
                n *= d
            if at is None:
                at = top[0]
                top[0] += (n + 31) // 32 * 32
            return nc.alloc_sbuf_tensor_at(name, shape, dt, offset=at)

        def sem(name):
            return ctx.enter_context(nc.semaphore(name))

        w_raw = sb("w_raw", [P, NRAW, WF])
        w_hi = sb("w_hi", [P, NSPLIT, WF], F32R)
        w_lo = sb("w_lo", [P, NSPLIT, WF], F32R)
        m_raw = sb("m_raw", [P, NMOD, D])
        xT = sb("xT", [P, KT, S])
        h_at = top[0]
        h = sb("h", [P, 2, KT, S], F32R)
        big_at = top[0]
        big = sb("big", [P, 3, KT, S])
        acc_at = top[0]
        mod_acc = sb("mod_acc", [P, D])
        ones = sb("ones", [P, P])
        ident = sb("ident", [P, P])
        mod_bias = sb("mod_bias", [P, 14 * KT])
        modT = sb("modT", [P, 14, KT])
        gains = sb("gains", [P, 8 * KT])
        convT = sb("convT", [P, 2, 4, 88])
        rstd = sb("rstd", [P, S])
        gs = sb("gs", [P, KT])
        cT = sb("cT", [P, KT])
        half_pi = sb("half_pi", [P, 1])
        eps = sb("eps", [P, 1])
        scr_at = top[0]
        assert scr_at + 16 * 1024 <= 229344, scr_at
        scr = sb("scr", [P, 4096])

        NM0, NM1, NF0, NF1, NKV, NFIN, GLUB, SKIP = range(8)

        def gain(n, kt=None):
            return gains[:, n * KT:(n + 1) * KT] if kt is None else gains[:, n * KT + kt:n * KT + kt + 1]

        u_t = big[:, 0]
        b_t = sb("b_t", [P, 2, KT, P], at=big_at + 16384)
        c_t = sb("c_t", [P, 2, KT, P], at=big_at + 32768)
        v_nat = sb("v_nat", [P, TB, D], at=big_at + 16384)
        ffg = sb("ffg", [P, 48, S], at=big_at)
        x_nat = sb("x_nat", [P, TB, D], at=big_at + 16384)
        out_nat = sb("out_nat", [P, TB, D], at=big_at + 16384)
        c_nat = sb("c_nat", [P, 2, KT, P], at=big_at)
        b_raw = sb("b_raw", [P, 2, ST, GW], at=h_at)
        b_tmp = sb("b_tmp", [P, 2, ST, GW], at=h_at + 8192)
        b_bar = sb("b_bar", [P, 2, ST, 2, GW], at=h_at + 16384)
        nat = sb("nat", [P, 16, P], at=scr_at)
        prep = sb("prep", [64, 14, P], at=scr_at + 8192)
        step = sb("step", [64, 2], at=scr_at + 8192 + 14 * 512)
        tab = sb("tab", [P, 2, 3, 2, S], at=h_at)
        rot = sb("rot", [P, 2, 2, 2, S], at=h_at + 16384)
        tmp = sb("tmp", [P, 2, 2, S], at=h_at + 16384 + 8192)
        prod = sb("prod", [P, 4, 2, S], at=scr_at)
        yb = sb("yb", [P, 2, S], at=scr_at + 8192)
        arg = sb("arg", [P, 2, 2, S], at=scr_at + 10240)
        prm = sb("prm", [P, 4, ST], at=scr_at + 14336)
        iota = sb("iota", [P, S], at=scr_at + 15360)
        conv = sb("conv", [P, 8, S], at=scr_at)
        sel = sb("sel", [P, HEADS, P], at=acc_at)
        mask = sb("mask", [P, 384], at=scr_at)
        fc = sb("fc", [P, 4, S], at=scr_at + 1536)
        fw_raw = sb("fw_raw", [P, KT, HEADS], at=scr_at + 5632)
        fw_hi = sb("fw_hi", [P, KT, HEADS], F32R, at=scr_at + 6656)
        fw_lo = sb("fw_lo", [P, KT, HEADS], F32R, at=scr_at + 7680)
        f_nat = sb("f_nat", [P, TB, HEADS], at=scr_at + 8704)
        att = sb("att", [P, 4, 384], at=scr_at + 5632)
        att_t = sb("att_t", [P, 2, 384], at=scr_at + 5632 + 6144)
        stat = sb("stat", [P, 3, 4, TB], at=scr_at + 5632 + 6144 + 3072)
        fb = sb("fb", [HEADS, 1], at=scr_at + 5632 + 6144 + 3072 + 96)

        psum = ctx.enter_context(nc.psum_tensor("psum_all", [P, 8, 512], F32))

        w_full = [sem(f"w_full{i}") for i in range(NRAW)]
        m_full = [sem(f"m_full{i}") for i in range(NMOD)]
        hi_done, lo_done, w_used = sem("hi_done"), sem("lo_done"), sem("w_used")
        mod_used, acc_ready, sum_ready, mod_ready = sem("mod_used"), sem("acc_ready"), sem("sum_ready"), sem("mod_ready")
        x_loaded, nat_loaded, ab_loaded, bc_loaded, fw_loaded = (
            sem("x_loaded"), sem("nat_loaded"), sem("ab_loaded"), sem("bc_loaded"), sem("fw_loaded"))
        consts, silu_done, rest_loaded, b_loaded, c_loaded = (
            sem("consts"), sem("silu_done"), sem("rest_loaded"), sem("b_loaded"), sem("c_loaded"))
        prep_red, gs_done, fc_zero, iota_done, zhi_done, zlo_done, x_out, copied, f_act = (
            sem("prep_red"), sem("gs_done"), sem("fc_zero"), sem("iota_done"), sem("zhi_done"), sem("zlo_done"), sem("x_out"), sem("copied"), sem("f_act"))
        turned, turned_out = sem("turned"), sem("turned_out")
        prep_act, prep_dve, bar_done = sem("prep_act"), sem("prep_dve"), sem("bar_done")
        c_zero = sem("c_zero")
        sq_done, ss_done, r_done, scaled, xhi_done, xlo_done = (
            sem("sq_done"), sem("ss_done"), sem("r_done"), sem("scaled"), sem("xhi_done"), sem("xlo_done"))
        evac = sem("evac")
        s_v, s_k, s_r, s_abs, s_tab, s_bu = (sem(n) for n in ("s_v", "s_k", "s_r", "s_abs", "s_tab", "s_bu"))
        s_rotm, s_rota, s_z, s_prod, s_y, s_yd, s_g = (
            sem(n) for n in ("s_rotm", "s_rota", "s_z", "s_prod", "s_y", "s_yd", "s_g"))
        s_sg, s_zg = sem("s_sg"), sem("s_zg")
        conv_act, conv_1, conv_2, silu_c, ffg_done = (
            sem("conv_act"), sem("conv_1"), sem("conv_2"), sem("silu_c"), sem("ffg_done"))
        fw_split, f_sum, f_evac, f_turn, f_step, f_cum, sel_done, mask_done = (
            sem(n) for n in ("fw_split", "f_sum", "f_evac", "f_turn", "f_step", "f_cum", "sel_done", "mask_done"))
        a_s, a_masked, a_max, a_neg, a_exp, a_rec, a_p, a_t, a_tc, a_o, a_ohi, a_olo = (
            sem(f"a_{n}") for n in ("s", "masked", "max", "neg", "exp", "rec", "p", "t", "tc", "o", "ohi", "olo"))
        o_scaled, o_turned, o_copied, stored = sem("o_scaled"), sem("o_turned"), sem("o_copied"), sem("stored")

        block = ctx.enter_context(nc.Block())

        def rows(w):
            return w.rearrange("(t p) n -> p t n", p=P)

        w_in_v, glu_v, w_out_v = rows(ssm_w_in[0]), rows(ssm_glu_w[0]), rows(ssm_w_out[0])
        kv_v, q_v, ao_v = rows(kv_w), rows(attn_w_q[0]), rows(attn_w_out[0])
        up_v = [ffn_w_up[i].rearrange("(t p) (a n) -> p t a n", p=P, a=2) for i in range(2)]
        down_v = [rows(ffn_w_down[i]) for i in range(2)]
        mod_v = [rows(mod_w[0]), rows(kv_mod_w), rows(mod_w[1])]

        def mod_section(s):
            return (0, s) if s < SH_KV else (1, s - SH_KV) if s < SH_M1 else (2, s - SH_M1)

        @block.sync
        def _(sp):
            def load_w(src, st, dyn=0):
                if st >= NRAW:
                    sp.wait_ge(lo_done, dyn + (st - NRAW + 1))
                for k in range(UK):
                    sp.dma_start(w_raw[:, st % NRAW, UC * k:UC * (k + 1)], src(k)).then_inc(w_full[st % NRAW], 16)

            def load_m(s, kt, dyn=0, sdyn=0):
                t, ms = mod_section(s)
                st = KT * s + kt
                if st >= NMOD:
                    sp.wait_ge(mod_used, sdyn * KT + dyn + (st - NMOD + 1))
                src = mod_v[t][:, bass.ds(dyn + kt, 1), bass.ds(sdyn * D + ms * D, D)]
                sp.dma_start(m_raw[:, st % NMOD], src).then_inc(m_full[st % NMOD], 16)

            def load_pair(wv, col, base, s=None):
                for g in range(2):
                    def one(k, j):
                        load_w(lambda r: wv[:, bass.ds(k * UK + (j * UK + r), 1), col + UC * g:col + UC * (g + 1)], base + GU * g + j, k)
                        if s is not None:
                            load_m(s, GU * g + j, k)
                    steps(sp, GU, 4, one)

            def load_up(layer, p, base, dyn, groups=2, s=None):
                for j in range(GU * groups):
                    k, g = j % GU, j // GU
                    load_w(lambda r: up_v[layer][:, UK * k + r, :, bass.ds(p * 1024 + 512 * g, 512)], base + j, dyn)
                    if s is not None:
                        load_m(s[0], j, 0, s[1])

            def load_down(layer, base, sections=None):
                for g in range(2):
                    def one(k, j, m):
                        load_w(lambda r: down_v[layer][:, bass.ds(k * UK + (j * UK + r), 1), UC * g:UC * (g + 1)], base + DU * g + j, k)
                        if m:
                            load_m(sections[g], j, k)
                    steps(sp, KT, 4, lambda k, j: one(k, j, sections is not None))
                    for j in range(KT, DU):
                        one(0, j, False)

            for kt in range(NMOD):
                load_m(SH_M0, kt)
            steps(sp, KT - NMOD, 2, lambda k, j: load_m(SH_M0, NMOD + j, k))
            steps(sp, KT, 2, lambda k, j: load_m(SC_M0, j, k))
            for j in range(2 * GU):
                k, g = j % GU, j // GU
                load_w(lambda r: w_in_v[:, UK * k + r, UC * g:UC * g + UC], U_IN + j)
            for j in range(NRAW):
                load_w(lambda r: glu_v[:, UK * j + r, 0:UC], U_GLU + j)
            steps(sp, KT, 2, lambda k, j: load_m(G_M0, j, k))
            for j in range(NRAW, GU):
                load_w(lambda r: glu_v[:, UK * j + r, 0:UC], U_GLU + j)

            def glu_half(k, j):
                load_w(lambda r: glu_v[:, bass.ds(k * UK + (j * UK + r), 1), UC:2 * UC], U_GLU + GU + j, k)
                for e in range(2):
                    load_m(SH_F0, 2 * j + e, k * 2)

            steps(sp, GU, 4, glu_half)
            load_pair(w_out_v, 0, U_OUT, SC_F0)
            load_up(0, 0, U_UP0, 0, s=(G_F0, 0))
            with sp.Fori(0, 2) as i:
                load_up(0, i + 1, U_UP0 + 16, i * 16, s=(SH_KV, i))
            with sp.Fori(0, 2) as i:
                load_up(0, i + 3, U_UP0 + 48, i * 16, s=(SH_M1, i))
            load_up(0, 5, U_UP0 + 80, 0, groups=1)
            load_down(0, U_DOWN0, (G_M1, SH_F1))
            load_pair(kv_v, 0, U_K, SC_F1)
            load_pair(kv_v, D, U_V, G_F1)
            load_pair(q_v, 0, U_Q)
            load_pair(ao_v, 0, U_AO)
            with sp.Fori(0, 5) as i:
                load_up(1, i, U_UP1, i * 16)
            load_up(1, 5, U_UP1 + 80, 0, groups=1)
            load_down(1, U_DOWN1)
            for tb in range(TB):
                sp.wait_ge(o_copied, 4 * (tb + 1))
                sp.dma_start(out[0, P * tb:P * (tb + 1), :], out_nat[:, tb]).then_inc(stored, 16)
            sp.wait_ge(stored, 32)

        B_C, B_BIAS, B_GAIN, B_CONV, B_X, B_PRM, B_CT, B_BT = 0, 1, 2, 3, 5, 13, 14, 22
        N_BATCH = 30

        @block.gpsimd
        def _(pool):
            pool.memset(ident[:, :], 0.0).then_inc(consts, 1)
            pool.memset(ones[:, :], 1.0).then_inc(consts, 1)
            pool.wait_ge(consts, 2)
            pool.affine_select(out=ident[:, :], in_=ident[:, :], compare_op=ALU.not_equal, fill=1.0, base=0,
                               pattern=[[-1, P]], channel_multiplier=1).then_inc(consts, 1)
            pool.memset(c_nat[:, :, :, :], 0.0).then_inc(c_zero, 1)
            pool.memset(b_bar[:, :, :, :, :], 0.0).then_inc(c_zero, 1)
            pool.memset(half_pi[:, :], PI / 2)
            pool.memset(eps[:, :], EPS).then_inc(consts, 1)
            pool.wait_ge(turned_out, B_PRM + 1)
            pool.memset(iota[:, :], 1.0).then_inc(consts, 1)

            def table(m, q):
                ge(pool, s_tab, m * 4 + q)
                j = m * 8 + 2 * q
                f_b = prm[:, 0, bass.ds(j, 2)].unsqueeze(2).to_broadcast([P, 2, S])
                t_b = iota[:, :].unsqueeze(1).to_broadcast([P, 2, S])
                pool.tensor_tensor(arg[:, 0], t_b, f_b, ALU.mult).then_inc(s_v, 1)
                pool.wait_ge(s_k, m * 4 + (q + 1))
                pool.tensor_tensor(arg[:, 0], arg[:, 0], arg[:, 1], ALU.subtract).then_inc(s_r, 1)

            def products(m, q):
                pool.wait_ge(s_z, m * 4 + (q + 1))
                for half in range(2):
                    ge(pool, s_y, m * 8 + (2 * q + half - 1))
                    a, b = ((0, 2), (1, 0))[half]
                    pool.tensor_tensor(prod[:, 2 * half], tab[:, q % 2, a], rot[:, q % 2, 0], ALU.mult)
                    pool.tensor_tensor(prod[:, 2 * half + 1], tab[:, q % 2, b], rot[:, q % 2, 1], ALU.mult).then_inc(s_prod, 1)

            def s5(m):
                table(m, 0)
                for q in range(4):
                    if q < 3:
                        table(m, q + 1)
                    products(m, q)

            pool.wait_ge(iota_done, 1)
            pool.wait_ge(turned_out, N_BATCH)
            s5(0)
            with pool.Fori(1, 8) as m:
                s5(m)

            def gate(g, base):
                pool.wait_ge(silu_c, g + (base + 1))
                pool.tensor_tensor(ffg[:, bass.ds(g * 4, 4)], conv[:, 0:4], conv[:, 4:8], ALU.mult).then_inc(ffg_done, 1)

            with pool.Fori(0, 11) as g:
                gate(g, 0)
            pool.wait_ge(ffg_done, 11)
            pool.memset(fc[:, :, :], 0.0).then_inc(fc_zero, 1)
            pool.memset(mask[:, :], 0.0).then_inc(mask_done, 1)
            pool.wait_ge(mask_done, 1)
            pool.affine_select(out=mask[:, 0:P], in_=mask[:, 0:P], compare_op=ALU.is_ge, fill=MASKED, base=0,
                               pattern=[[-1, P]], channel_multiplier=1).then_inc(mask_done, 1)
            pool.affine_select(out=mask[:, 2 * P:], in_=mask[:, 2 * P:], compare_op=ALU.is_ge, fill=MASKED, base=0,
                               pattern=[[-1, P]], channel_multiplier=1).then_inc(mask_done, 1)
            pool.wait_ge(mod_ready, 14)
            pool.memset(sel[:, :, :], 0.0).then_inc(sel_done, 1)
            pool.wait_ge(sel_done, 1)
            pool.affine_select(out=sel[:, :, :], in_=sel[:, :, :], compare_op=ALU.not_equal, fill=1.0, base=0,
                               pattern=[[-1, HEADS], [0, P]], channel_multiplier=1).then_inc(sel_done, 1)
            with pool.Fori(0, 11) as g:
                gate(g, 11)

        @block.scalar
        def _(act):
            act.dma_start(nat[0:KT, 0, :], c.rearrange("a (t p) -> (a t) p", p=P)).then_inc(nat_loaded, 16)
            nb = 0
            act.dma_start(prep[:, 0, :], ssm_a_re[0].rearrange("(j g) p -> j (g p)", g=2)).then_inc(ab_loaded, 16)
            act.dma_start(prep[:, 1, :], ssm_a_im[0].rearrange("(j g) p -> j (g p)", g=2)).then_inc(ab_loaded, 16)
            act.dma_start(step[:, :], ssm_log_step[0].rearrange("(j g) -> j g", g=2)).then_inc(ab_loaded, 16)
            act.dma_start(nat[0:96, 1, :], mod_b[0].rearrange("(t p) -> t p", p=P)).then_inc(rest_loaded, 16)
            act.dma_start(nat[0:32, 2, :], kv_mod_b.rearrange("(t p) -> t p", p=P)).then_inc(rest_loaded, 16)
            act.dma_start(nat[0:96, 3, :], mod_b[1].rearrange("(t p) -> t p", p=P)).then_inc(rest_loaded, 16)
            for n, g in enumerate((norm_mix_g.rearrange("a (t p) -> (a t) p", p=P), norm_ffn_g.rearrange("a (t p) -> (a t) p", p=P),
                                   kv_norm_g.rearrange("(t p) -> t p", p=P), final_norm_g.rearrange("(t p) -> t p", p=P),
                                   ssm_glu_b.rearrange("a (t p) -> (a t) p", p=P), ssm_d.rearrange("a (t g) h -> (a t) (g h)", g=8))):
                act.dma_start(nat[nb:nb + g.shape[0], 4, :], g).then_inc(rest_loaded, 16)
                nb += g.shape[0]
            for i in range(2):
                for k in range(3):
                    act.dma_start(nat[0:88, 5 + 4 * i + k, :], ffn_conv_w[i, k].rearrange("(t p) -> t p", p=P)).then_inc(rest_loaded, 16)
                act.dma_start(nat[0:88, 8 + 4 * i, :], ffn_conv_b[i].rearrange("(t p) -> t p", p=P)).then_inc(rest_loaded, 16)
            for tb in range(TB):
                act.dma_start(x_nat[:, tb], x[0, P * tb:P * (tb + 1), :]).then_inc(x_loaded, 16)
            for n, w in enumerate((ssm_b_re, ssm_b_im)):
                act.dma_start(b_raw[:, n], w[0].rearrange("(j g) p h -> (g p) j h", g=2)).then_inc(b_loaded, 16)
            act.wait_ge(c_zero, 1)
            for n, w in enumerate((ssm_c_re, ssm_c_im)):
                wv = w[0].rearrange("(n i g) h p -> i g h n p", i=4, g=2)
                for i in range(4):
                    for g in range(2):
                        at = 32 * i + GW * g
                        act.dma_start(c_nat[at:at + GW, n, :, STATE * g:STATE * (g + 1)], wv[i, g]).then_inc(c_loaded, 16)

            def turn_out(b, dst, n=512, scale=1.0):
                act.wait_ge(turned, b + 1)
                act.activation(dst, psum[:, b % 8, 0:n], ACT.Copy, scale=scale).then_inc(turned_out, 1)

            act.wait_ge(nat_loaded, 16)
            act.activation(nat[0:KT, 0, :], nat[0:KT, 0, :], ACT.Silu).then_inc(silu_done, 1)
            turn_out(B_C, cT[:, :], KT)
            act.wait_ge(ab_loaded, 48)
            act.activation(step[:, :], step[:, :], ACT.Exp).then_inc(prep_act, 1)
            act.wait_ge(prep_dve, 2)
            act.activation(prep[:, 4, :], prep[:, 2, :], ACT.Exp).then_inc(prep_act, 1)
            turn_out(B_BIAS, mod_bias[:, :], 14 * KT)
            turn_out(B_GAIN, gains[:, :], P)
            for i in range(2):
                turn_out(B_CONV + i, convT[:, i], 352)
            for b in range(8):
                turn_out(B_X + b, xT[:, 2 * b:2 * b + 2].rearrange("p t s -> p (t s)"))
            act.wait_ge(prep_dve, 7)
            act.activation(prep[:, 6, :], prep[:, 5, :], ACT.Sin, scale=TWO_PI_DOWN).then_inc(prep_act, 1)
            act.activation(prep[:, 7, :], prep[:, 5, :], ACT.Abs).then_inc(prep_act, 1)
            act.wait_ge(prep_act, 4)
            act.wait_ge(consts, 4)
            act.activation(prep[:, 7, :], prep[:, 7, :], ACT.Sin, scale=-TWO_PI_DOWN, bias=half_pi[0:64, :]).then_inc(prep_act, 1)
            turn_out(B_PRM, prm[:, :, :].rearrange("p a j -> p (a j)"), 4 * ST)
            for n in range(2):
                for b in range(4):
                    turn_out(B_CT + 4 * n + b, c_t[:, n, 4 * b:4 * b + 4].rearrange("p t s -> p (t s)"), scale=(1.0, -1.0)[n])
            for n in range(2):
                for b in range(4):
                    turn_out(B_BT + 4 * n + b, b_t[:, n, 4 * b:4 * b + 4].rearrange("p t s -> p (t s)"))

            def hi(st, dyn=0):
                act.wait_ge(w_full[st % NRAW], dyn * (16 * UK // NRAW) + 16 * UK * (st // NRAW + 1))
                ge(act, w_used, dyn + (st - NSPLIT + 1))
                act.activation(w_hi[:, st % NSPLIT], w_raw[:, st % NRAW], ACT.Copy).then_inc(hi_done, 1)

            def squares(buf, ready):
                act.wait_ge(*ready)
                for b in range(4):
                    act.activation(buf[:, 4 * b:4 * b + 4], xT[:, 4 * b:4 * b + 4], ACT.Square).then_inc(sq_done, 1)

            def root(i, bank=7):
                act.wait_ge(ss_done, i + 1)
                act.activation(rstd[:, :], psum[:, bank, 0:S], ACT.Sqrt, scale=1.0 / D, bias=eps[:, :]).then_inc(r_done, 1)

            def norm_hi(buf, shift, n):
                act.wait_ge(mod_ready, shift + 1)
                def one(k, j):
                    act.wait_ge(scaled, k + (KT * n + j + 1))
                    act.activation(h[:, 0, bass.ds(k + j, 1)], buf[:, bass.ds(k + j, 1)], ACT.Identity,
                                   bias=modT[:, shift, bass.ds(k + j, 1)]).then_inc(xhi_done, 1)
                steps(act, KT, 4, one)

            def ring_hi(src, unit0, i, k=0, t0=None):
                ge(act, w_used, k + (unit0 + i - 1))
                t = 2 * i if t0 is None else t0
                act.activation(h[:, 0, 12 + 2 * (i % 2):14 + 2 * (i % 2)], src[:, bass.ds(k * 2 + t, 2)], ACT.Copy).then_inc(xhi_done, 1)

            def plain_pair(base, evac_out=None):
                for g in range(2):
                    for j in range(GU):
                        hi(base + GU * g + j + 2)
                    if evac_out is not None:
                        evac_out(g)

            def copy_out(base, count, dst, scale=1.0):
                def f(g):
                    act.wait_ge(w_used, base + GU * (g + 1))
                    src = psum[:, 4 * g:4 * g + 4]
                    if len(dst(g).shape) == 4:
                        src = src.rearrange("p (t b) n -> p t b n", t=TB)
                    act.activation(dst(g), src, ACT.Copy, scale=scale).then_inc(copied, 1)
                return f

            squares(big[:, 0], (turned_out, N_BATCH))
            hi(U_IN)
            hi(U_IN + 1)
            root(0)
            norm_hi(big[:, 0], SH_M0, 0)
            plain_pair(U_IN, copy_out(U_IN, 0, lambda g: u_t[:, 8 * g:8 * g + 8].rearrange("p (b t) s -> p b (t s)", b=4)))

            def tables(m, q):
                ge(act, s_prod, m * 8 + 2 * (q - 1))
                act.wait_ge(s_r, m * 4 + (q + 1))
                act.activation(tab[:, q % 2, 1], arg[:, 0], ACT.Sin, scale=TWO_PI_DOWN)
                act.activation(tab[:, q % 2, 2], arg[:, 0], ACT.Sin, scale=-TWO_PI_DOWN)
                act.activation(arg[:, 0], arg[:, 0], ACT.Abs).then_inc(s_abs, 1)
                act.wait_ge(s_abs, m * 4 + (q + 1))
                act.activation(tab[:, q % 2, 0], arg[:, 0], ACT.Sin, scale=-TWO_PI_DOWN, bias=half_pi[:, :]).then_inc(s_tab, 1)

            def s5(m):
                for q in range(4):
                    tables(m, q)
                act.wait_ge(s_yd, m * 2 + 2)
                act.activation(u_t[:, bass.ds(m * 2, 2)], yb[:, :], ACT.Gelu_apprx_tanh).then_inc(s_g, 1)

            s5(0)
            with act.Fori(1, 8) as m:
                s5(m)

            for i in range(2):
                ring_hi(u_t, U_GLU, i)
            for g in range(2):
                for j in range(GU):
                    i = GU * g + j + 2
                    hi(U_GLU + i)
                    if i < 2 * GU:
                        ring_hi(u_t, U_GLU, i, t0=2 * (i % GU))
                act.wait_ge(w_used, U_GLU + GU * (g + 1))
                for b in range(2):
                    for j in range(4):
                        t = 4 * b + j
                        act.activation(big[:, 1, 8 * g + t], psum[:, 4 * g + t // 2, S * (t % 2):S * (t % 2 + 1)], ACT.Sigmoid,
                                       bias=gain(GLUB, 8 * g + t)).then_inc(s_sg, 1)
                for b in range(2):
                    act.wait_ge(s_zg, 2 * g + b + 1)
                    t = 8 * g + 4 * b
                    act.activation(h[:, 0, t:t + 4], big[:, 1, t:t + 4], ACT.Copy).then_inc(zhi_done, 1)
            plain_pair(U_OUT)

            def ffn(layer, n, buf, sq, shift, up_base, down_base, gbase, ready):
                squares(sq, ready)
                root(1 if n == 1 else 3)
                norm_hi(sq, shift, n)

                def taps(g, bank):
                    ge(act, ffg_done, g + gbase)
                    act.wait_ge(w_used, g * GU + (up_base + GU))
                    for t in range(8):
                        tile = g * 4 + (t if t < 4 else t - 4 + FT)
                        a = act.activation(conv[:, t], psum[:, bank + t // 2, S * (t % 2):S * (t % 2 + 1)], ACT.Identity,
                                           scale=convT[:, layer, 2, bass.ds(tile, 1)], bias=convT[:, layer, 3, bass.ds(tile, 1)])
                        if t % 2:
                            a.then_inc(conv_act, 1)
                    act.wait_ge(conv_2, g * 4 + (4 * gbase + 4))
                    act.activation(conv[:, 0:4], conv[:, 0:4], ACT.Silu).then_inc(silu_c, 1)

                with act.Fori(0, 5) as p:
                    for g in range(2):
                        for j in range(GU):
                            hi(up_base + GU * g + j + 2, p * 16)
                        taps(p * 2 + g, 4 * g)
                for j in range(GU):
                    hi(up_base + 10 * GU + j + 2)
                taps(10, 0)
                act.wait_ge(ffg_done, gbase + 11)
                for i in range(2):
                    ring_hi(ffg, down_base, i)
                for g in range(2):
                    def one(k, j):
                        i = DU * g + 2 + j
                        hi(down_base + i, k)
                        ring_hi(ffg, down_base, i, k, t0=4 + 2 * j)
                    steps(act, DU - 2, 4, one)
                    for i in (DU * (g + 1), DU * (g + 1) + 1):
                        if down_base + i < U_END:
                            hi(down_base + i)
                        if g == 0:
                            ring_hi(ffg, down_base, i, t0=2 * (i - DU))

            ffn(0, 1, None, big[:, 2], SH_F0, U_UP0, U_DOWN0, 0, (x_out, 2))

            squares(big[:, 0], (x_out, 4))
            act.dma_start(fw_raw[:, :, :], kv_v[:, :, 2 * D:2 * D + HEADS]).then_inc(fw_loaded, 16)
            act.dma_start(fb[:, :], forget_b.rearrange("(h a) -> h a", a=1)).then_inc(fw_loaded, 16)
            root(2)
            norm_hi(big[:, 0], SH_KV, 2)
            act.wait_ge(fw_loaded, 32)
            act.activation(fw_hi[:, :, :], fw_raw[:, :, :], ACT.Copy).then_inc(fw_split, 1)
            plain_pair(U_K, copy_out(U_K, 2, lambda g: big[:, 0, 8 * g:8 * g + 8].rearrange("p (b t) s -> p b (t s)", b=4)))
            plain_pair(U_V, copy_out(U_V, 4, lambda g: v_nat[:, :, UC * g:UC * g + UC].rearrange("p t (b n) -> p t b n", b=2)))
            act.wait_ge(f_step, 1)
            act.activation(fc[0:HEADS, 1], fc[0:HEADS, 0], ACT.Abs).then_inc(f_act, 1)
            act.wait_ge(f_act, 1)
            act.activation(fc[0:HEADS, 1], fc[0:HEADS, 1], ACT.Exp, scale=-1.0).then_inc(f_act, 1)
            act.wait_ge(f_act, 2)
            act.activation(fc[0:HEADS, 1], fc[0:HEADS, 1], ACT.Ln, bias=1.0).then_inc(f_act, 1)

            norm_hi(big[:, 2], SH_M1, 3)
            plain_pair(U_Q, copy_out(U_Q, 6, lambda g: big[:, 2, 8 * g:8 * g + 8].rearrange("p (b t) s -> p b (t s)", b=4), P ** -0.5))

            def heads(i):
                for e in range(4):
                    act.wait_ge(a_max, i * 4 + (e + 1))
                    for tb, (lo_c, hi_c) in enumerate(((0, P), (P, 3 * P))):
                        a = act.activation(att[:, e, lo_c:hi_c], att[:, e, lo_c:hi_c], ACT.Exp, bias=stat[:, 0, e, tb:tb + 1],
                                           accum_out=stat[:, 1, e, tb:tb + 1])
                    a.then_inc(a_exp, 1)
                for e in range(4):
                    act.wait_ge(a_t, i * 4 + (e + 1))
                    ge(act, a_o, i * 4 + (e - 1))
                    act.activation(att_t[:, e % 2], psum[:, 4 + e % 2, 0:384], ACT.Copy).then_inc(a_tc, 1)
                    if e:
                        out_hi(i, e - 1)
                out_hi(i, 3)

            def out_hi(i, e):
                act.wait_ge(a_o, i * 4 + (e + 1))
                act.activation(h[:, 0, bass.ds(i * 4 + e, 1)], psum[:, 6 + e % 2, 0:S].unsqueeze(1), ACT.Copy).then_inc(a_ohi, 1)

            heads(0)
            with act.Fori(1, 4) as i:
                heads(i)
            plain_pair(U_AO)
            ffn(1, 4, None, big[:, 2], SH_F1, U_UP1, U_DOWN1, 11, (x_out, 6))

            squares(big[:, 0], (x_out, 8))
            root(4)
            for b in range(8):
                act.wait_ge(o_turned, b + 1)
                act.activation(out_nat[:, b // 4, 512 * (b % 4):512 * (b % 4 + 1)], psum[:, b % 4, :], ACT.Copy).then_inc(o_copied, 1)

        @block.vector
        def _(dve):
            def lo(st, dyn=0):
                dve.wait_ge(hi_done, dyn + (st + 1))
                ge(dve, w_used, dyn + (st - NSPLIT + 1))
                dve.tensor_tensor(w_lo[:, st % NSPLIT], w_raw[:, st % NRAW], w_hi[:, st % NSPLIT].bitcast(F32),
                                  ALU.subtract).then_inc(lo_done, 1)

            def mod_add(s, kt, dyn=0, sdyn=0):
                st = KT * s + kt
                dve.wait_ge(m_full[st % NMOD], sdyn * 128 + dyn * 8 + 16 * (st // NMOD + 1))
                if isinstance(dyn, int) and kt == 0:
                    ge(dve, sum_ready, sdyn + s)
                    dve.tensor_scalar(mod_acc[:, :], m_raw[:, 0], cT[:, 0:1], None, ALU.mult).then_inc(mod_used, 1)
                    return
                dve.wait_ge(mod_used, sdyn * KT + dyn + st)
                dve.scalar_tensor_tensor(out=mod_acc[:, :], in0=m_raw[:, st % NMOD], scalar=cT[:, bass.ds(dyn + kt, 1)],
                                         in1=mod_acc[:, :], op0=ALU.mult, op1=ALU.add).then_inc(mod_used, 1)

            def mod_out(s, bank, sdyn=0):
                dve.wait_ge(sum_ready, sdyn + (s + 1))
                dve.tensor_tensor(modT[:, bass.ds(sdyn + s, 1)], psum[:, bank, 0:KT].unsqueeze(1),
                                  mod_bias[:, bass.ds(sdyn * KT + s * KT, KT)].unsqueeze(1), ALU.add).then_inc(mod_ready, 1)

            def pair(base, evac, s=None, dyn=0, sdyn=0):
                if s is not None:
                    mod_add(s, 0, 0, sdyn)
                    mod_add(s, 1, 0, sdyn)
                for j in range(2, 2 * GU):
                    lo(base + j, dyn)
                    if j == GU + 1:
                        evac(0)
                    if s is not None:
                        mod_add(s, j, 0, sdyn)
                lo(base + 2 * GU, dyn)
                if s is not None:
                    mod_out(s, 0, sdyn)
                lo(base + 2 * GU + 1, dyn)
                evac(1)

            dve.wait_ge(turned_out, B_C + 1)
            mod_add(SH_M0, 0)
            mod_add(SH_M0, 1)

            RE, IM, DRE, DIM, MAG, TURN, SIN, COS, K1, K2, FR, FI = range(12)
            seen = [0]

            def pd(ins):
                ins.then_inc(prep_dve, 1)
                seen[0] += 1

            def pw():
                dve.wait_ge(prep_dve, seen[0])

            dve.wait_ge(ab_loaded, 48)
            dve.wait_ge(prep_act, 1)
            for src, dst in ((RE, DRE), (IM, DIM)):
                dve.tensor_scalar(prep[:, dst, 0:STATE], prep[:, src, 0:STATE], step[:, 0:1], None, ALU.mult)
                pd(dve.tensor_scalar(prep[:, dst, STATE:], prep[:, src, STATE:], step[:, 1:2], None, ALU.mult))
            mod_add(SH_M0, 2)
            pw()
            pd(dve.tensor_scalar(prep[:, K1, :], prep[:, DIM, :], 1.0 / (2 * PI), ROUND, ALU.mult, ALU.add))
            pw()
            pd(dve.tensor_scalar(prep[:, K1, :], prep[:, K1, :], ROUND, None, ALU.subtract))
            for part in (TWO_PI_1, TWO_PI_2, TWO_PI_3):
                pw()
                ins = dve.scalar_tensor_tensor(out=prep[:, DIM, :], in0=prep[:, K1, :], scalar=-part, in1=prep[:, DIM, :],
                                               op0=ALU.mult, op1=ALU.add)
                if part != TWO_PI_3:
                    pd(ins)
            ins.then_inc(prep_red, 1)
            dve.wait_ge(prep_red, 1)
            dve.tensor_scalar(prep[:, DIM, :], prep[:, DIM, :], 1.0 / (2 * PI), 0.5, ALU.mult, ALU.min).then_inc(prep_red, 1)
            dve.wait_ge(prep_red, 2)
            pd(dve.tensor_scalar(prep[:, TURN, :], prep[:, DIM, :], -0.5, None, ALU.max))
            mod_add(SH_M0, 3)
            dve.wait_ge(prep_act, 5)
            pd(dve.tensor_tensor(prep[:, K1, :], prep[:, MAG, :], prep[:, COS, :], ALU.mult))
            pd(dve.tensor_tensor(prep[:, K2, :], prep[:, MAG, :], prep[:, SIN, :], ALU.mult))
            pd(dve.tensor_tensor(prep[:, FR, :], prep[:, RE, :], prep[:, RE, :], ALU.mult))
            pd(dve.tensor_tensor(prep[:, FI, :], prep[:, IM, :], prep[:, IM, :], ALU.mult))
            pw()
            pd(dve.tensor_scalar(prep[:, K1, :], prep[:, K1, :], -1.0, None, ALU.add))
            pd(dve.tensor_tensor(prep[:, DRE, :], prep[:, FR, :], prep[:, FI, :], ALU.add))
            pw()
            pd(dve.reciprocal(prep[:, DRE, :], prep[:, DRE, :]))
            for dst, (a, b), (e, f), op in ((FR, (K1, RE), (K2, IM), ALU.add), (FI, (K2, RE), (K1, IM), ALU.subtract)):
                pd(dve.tensor_tensor(prep[:, dst, :], prep[:, a, :], prep[:, b, :], ALU.mult))
                pd(dve.tensor_tensor(prep[:, DIM, :], prep[:, e, :], prep[:, f, :], ALU.mult))
                pw()
                pd(dve.tensor_tensor(prep[:, dst, :], prep[:, dst, :], prep[:, DIM, :], op))
                pw()
                pd(dve.tensor_tensor(prep[:, dst, :], prep[:, dst, :], prep[:, DRE, :], ALU.mult))
            pw()
            assert seen[0] == PREP_DVE
            mod_add(SH_M0, 4)
            mod_add(SH_M0, 5)
            dve.wait_ge(turned_out, B_PRM + 1)
            dve.wait_ge(b_loaded, 32)
            dve.wait_ge(c_zero, 2)
            f_r, f_i = (prm[:, n, :].unsqueeze(2).to_broadcast([P, ST, GW]) for n in (2, 3))
            nb = 0
            for n, (a, b, op) in enumerate(((0, 1, ALU.subtract), (1, 0, ALU.add))):
                if n:
                    dve.wait_ge(bar_done, 4)
                dve.tensor_tensor(b_tmp[:, 0], b_raw[:, a], f_r, ALU.mult).then_inc(bar_done, 1)
                dve.tensor_tensor(b_tmp[:, 1], b_raw[:, b], f_i, ALU.mult).then_inc(bar_done, 1)
                dve.wait_ge(bar_done, 4 * n + 2)
                for g in range(2):
                    r = slice(STATE * g, STATE * (g + 1))
                    dve.tensor_tensor(b_bar[r, n, :, g, :], b_tmp[r, 0], b_tmp[r, 1], op).then_inc(bar_done, 1)
                mod_add(SH_M0, 6 + n)
            dve.wait_ge(consts, 5)
            dve.tensor_tensor_scan(out=iota[:, :], data0=iota[:, :], data1=iota[:, :], initial=0.0, op0=ALU.mult,
                                   op1=ALU.add).then_inc(iota_done, 1)
            steps(dve, KT // 2, 2, lambda k, j: mod_add(SH_M0, KT // 2 + j, k))
            mod_add(SC_M0, 0)
            mod_add(SC_M0, 1)
            steps(dve, KT - 2, 2, lambda k, j: mod_add(SC_M0, 2 + j, k))
            mod_out(SH_M0, 0)
            mod_out(SC_M0, 1)

            def norm(n, buf, scale, shift, g, sums=None, free=None):
                if sums is not None:
                    i, bank = sums
                    dve.wait_ge(r_done, 2 * i + 1)
                    dve.reciprocal(rstd[:, :], rstd[:, :]).then_inc(r_done, 1)
                    dve.wait_ge(r_done, 2 * i + 2)
                if scale is None:
                    gain_of = lambda kt: gains[:, bass.ds(g * KT + kt, 1)]
                else:
                    dve.wait_ge(mod_ready, scale + 1)
                    dve.scalar_tensor_tensor(out=gs[:, :], in0=modT[:, scale], scalar=1.0, in1=gain(g), op0=ALU.add,
                                             op1=ALU.mult).then_inc(gs_done, 1)
                    dve.wait_ge(gs_done, n + 1)
                    gain_of = lambda kt: gs[:, bass.ds(kt, 1)]
                if free is not None:
                    dve.wait_ge(*free)

                def scale_x(k, j):
                    dve.scalar_tensor_tensor(out=buf[:, bass.ds(k + j, 1)], in0=xT[:, bass.ds(k + j, 1)], scalar=gain_of(k + j),
                                             in1=rstd[:, :].unsqueeze(1), op0=ALU.mult, op1=ALU.mult).then_inc(scaled, 1)

                def rest(k, j):
                    dve.wait_ge(xhi_done, k + (XN[n] + j + 1))
                    dve.scalar_tensor_tensor(out=h[:, 1, bass.ds(k + j, 1)], in0=buf[:, bass.ds(k + j, 1)],
                                             scalar=modT[:, shift, bass.ds(k + j, 1)], in1=h[:, 0, bass.ds(k + j, 1)].bitcast(F32),
                                             op0=ALU.add, op1=ALU.subtract).then_inc(xlo_done, 1)

                if scale is None:
                    steps(dve, KT, 4, scale_x)
                    return
                for j in range(4):
                    scale_x(0, j)
                with dve.Fori(0, 3) as i:
                    for j in range(4):
                        scale_x(i * 4, j + 4)
                    for j in range(4):
                        rest(i * 4, j)
                for j in range(4):
                    rest(12, j)

            def ring_lo(src, i, count, unit0, k=0, t0=None):
                dve.wait_ge(xhi_done, k + (count + i + 1))
                ge(dve, w_used, k + (unit0 + i - 1))
                t = 2 * i if t0 is None else t0
                r = slice(12 + 2 * (i % 2), 14 + 2 * (i % 2))
                dve.tensor_tensor(h[:, 1, r], src[:, bass.ds(k * 2 + t, 2)], h[:, 0, r].bitcast(F32), ALU.subtract).then_inc(xlo_done, 1)

            def add_to_x(base, units, section, banks=(0, 4)):
                def f(g):
                    dve.wait_ge(w_used, base + units * (g + 1))
                    dve.wait_ge(mod_ready, section + 1)
                    for t in range(8):
                        ins = dve.scalar_tensor_tensor(out=xT[:, 8 * g + t], in0=psum[:, banks[g] + t // 2, S * (t % 2):S * (t % 2 + 1)],
                                                       scalar=modT[:, section, 8 * g + t:8 * g + t + 1], in1=xT[:, 8 * g + t],
                                                       op0=ALU.mult, op1=ALU.add)
                    ins.then_inc(x_out, 1)
                return f

            none = lambda g: None

            lo(U_IN)
            lo(U_IN + 1)
            norm(0, big[:, 0], SC_M0, SH_M0, NM0, (0, 7))
            pair(U_IN, none)

            def round_arg(m, q):
                dve.wait_ge(s_v, m * 4 + (q + 1))
                dve.tensor_scalar(arg[:, 1], arg[:, 0], ROUND, ROUND, ALU.add, ALU.subtract).then_inc(s_k, 1)

            def states(m, q):
                dve.wait_ge(s_bu, m * 4 + (q + 1))
                dve.wait_ge(s_tab, m * 4 + (q + 1))
                ge(dve, s_prod, m * 8 + 2 * (q - 1))
                b = q % 2
                cos, sin, nsin = (tab[:, b, n] for n in range(3))
                r = [rot[:, b, n] for n in range(2)]
                t = [tmp[:, n] for n in range(2)]
                re, im = (psum[:, 4 + 2 * b:6 + 2 * b, S * n:S * (n + 1)] for n in range(2))
                ge(dve, s_rota, m * 4 + q)
                dve.tensor_tensor(r[0], re, cos, ALU.mult)
                dve.tensor_tensor(t[0], im, sin, ALU.mult)
                dve.tensor_tensor(r[1], im, cos, ALU.mult)
                dve.tensor_tensor(t[1], re, nsin, ALU.mult).then_inc(s_rotm, 1)
                dve.wait_ge(s_rotm, m * 4 + (q + 1))
                for n in range(2):
                    ins = dve.tensor_tensor(r[n], r[n], t[n], ALU.add)
                ins.then_inc(s_rota, 1)
                dve.wait_ge(s_rota, m * 4 + (q + 1))
                for e in range(2):
                    decay = prm[:, 1, bass.ds(m * 8 + 2 * q + e, 1)].to_broadcast([P, S])
                    for n in range(2):
                        ins = dve.tensor_tensor_scan(out=rot[:, b, n, e], data0=decay, data1=rot[:, b, n, e], initial=0.0,
                                                     op0=ALU.mult, op1=ALU.add)
                ins.then_inc(s_z, 1)

            def skip(m, e):
                dve.wait_ge(s_y, m * 8 + 4 * (e + 1))
                ge(dve, s_g, m)
                dve.scalar_tensor_tensor(out=yb[:, e:e + 1], in0=u_t[:, bass.ds(m * 2 + e, 1)],
                                         scalar=gains[:, bass.ds(m * 2 + (SKIP * KT + e), 1)],
                                         in1=psum[:, e, 0:S].unsqueeze(1), op0=ALU.mult, op1=ALU.add).then_inc(s_yd, 1)

            def s5(m):
                round_arg(m, 0)
                for q in range(4):
                    if q < 3:
                        round_arg(m, q + 1)
                    states(m, q)
                    if q == 2:
                        skip(m, 0)
                skip(m, 1)
                if isinstance(m, int):
                    mod_add(G_M0, 0)
                    mod_add(G_M0, 1)
                else:
                    for e in range(2):
                        mod_add(G_M0, e, m * 2)

            dve.wait_ge(copied, 2)
            s5(0)
            with dve.Fori(1, 8) as m:
                s5(m)

            for i in range(2):
                if i == 0:
                    dve.wait_ge(s_g, 8)
                ring_lo(u_t, i, XG, U_GLU)

            def sigmoid_gate(g):
                for b in range(2):
                    t = 8 * g + 4 * b
                    dve.wait_ge(s_sg, t + 4)
                    dve.tensor_tensor(big[:, 1, t:t + 4], big[:, 1, t:t + 4], big[:, 0, t:t + 4], ALU.mult).then_inc(s_zg, 1)
                for b in range(2):
                    t = 8 * g + 4 * b
                    dve.wait_ge(zhi_done, 2 * g + b + 1)
                    dve.tensor_tensor(h[:, 1, t:t + 4], big[:, 1, t:t + 4], h[:, 0, t:t + 4].bitcast(F32), ALU.subtract).then_inc(zlo_done, 1)

            for j in range(2, GU + 2):
                lo(U_GLU + j)
                ring_lo(u_t, j, XG, U_GLU, t0=2 * (j % GU))
                if j == GU:
                    mod_out(G_M0, 0 + 4)
            sigmoid_gate(0)
            for j in range(GU + 2, 2 * GU):
                for e in range(2):
                    mod_add(SH_F0, 2 * (j - GU - 2) + e)
                lo(U_GLU + j)
                ring_lo(u_t, j, XG, U_GLU, t0=2 * (j % GU))
            for e in range(4):
                mod_add(SH_F0, 2 * (GU - 2) + e)
            lo(U_OUT)
            mod_out(SH_F0, 0)
            lo(U_OUT + 1)
            sigmoid_gate(1)
            pair(U_OUT, add_to_x(U_OUT, GU, G_M0), SC_F0)

            def ffn(layer, n, sq, scale, shift, gate_s, sums, up_base, down_base, gbase, count, sections):
                norm(n, sq, scale, shift, NF0 + layer, sums)

                def taps(g, bank):
                    for b in range(4):
                        dve.wait_ge(conv_act, g * 4 + (4 * gbase + b + 1))
                        for lag, tap, done in ((1, 1, conv_1), (2, 0, conv_2)):
                            if lag == 2:
                                dve.wait_ge(conv_1, g * 4 + (4 * gbase + b + 1))
                            for t in (2 * b, 2 * b + 1):
                                tile = g * 4 + (t if t < 4 else t - 4 + FT)
                                c0 = S * (t % 2)
                                ins = dve.scalar_tensor_tensor(
                                    out=conv[:, t, lag:], in0=psum[:, bank + b, c0:c0 + S - lag],
                                    scalar=convT[:, layer, tap, bass.ds(tile, 1)], in1=conv[:, t, lag:], op0=ALU.mult, op1=ALU.add)
                            ins.then_inc(done, 1)

                with dve.Fori(0, 5) as p:
                    pair(up_base, lambda g: taps(p * 2 + g, 4 * g), G_F0 if sections else None, p * 16, p)
                for j in range(2, GU + 2):
                    lo(up_base + 10 * GU + j)
                taps(10, 0)
                dve.wait_ge(ffg_done, gbase + 11)
                for i in range(2):
                    ring_lo(ffg, i, count, down_base)
                out = add_to_x(down_base, DU, gate_s, (4, 0))
                for g in range(2):
                    s = sections[g] if sections else None

                    def one(k, j, with_m):
                        i = DU * g + 2 + j
                        lo(down_base + i, k)
                        ring_lo(ffg, i, count, down_base, k, t0=4 + 2 * j)
                        if with_m:
                            mod_add(s, 2 + j, k)
                    if s is not None:
                        mod_add(s, 0)
                        mod_add(s, 1)
                        steps(dve, 12, 4, lambda k, j: one(k, j, True))
                        for j in range(12, DU - 2):
                            one(0, j, j < KT - 2)
                    else:
                        steps(dve, DU - 2, 4, lambda k, j: one(k, j, False))
                    for e in range(2):
                        i = DU * (g + 1) + e
                        if e and s is not None:
                            mod_out(s, BANK_DOWN[g])
                        if down_base + i < U_END:
                            lo(down_base + i)
                        if g == 0:
                            ring_lo(ffg, i, count, down_base, t0=2 * (i - DU))
                    out(g)

            ffn(0, 1, big[:, 2], SC_F0, SH_F0, G_F0, (1, 7), U_UP0, U_DOWN0, 0, XD0, (G_M1, SH_F1))

            norm(2, big[:, 0], SC_KV, SH_KV, NKV, (2, 7))
            dve.wait_ge(fw_split, 1)
            dve.tensor_tensor(fw_lo[:, :, :], fw_raw[:, :, :], fw_hi[:, :, :].bitcast(F32), ALU.subtract).then_inc(fw_split, 1)
            pair(U_K, none, SC_F1)
            pair(U_V, none, G_F1)
            dve.wait_ge(f_sum, 1)
            dve.tensor_copy(f_nat[:, :, :], psum[:, 0, 0:TB * HEADS].rearrange("p (t n) -> p t n", t=TB)).then_inc(f_evac, 1)
            dve.wait_ge(f_turn, 1)
            dve.wait_ge(fc_zero, 1)
            dve.tensor_scalar(fc[0:HEADS, 0], psum[0:HEADS, 1, 0:S], fb[:, :], None, ALU.add).then_inc(f_step, 1)
            dve.wait_ge(f_act, 3)
            dve.tensor_scalar(fc[0:HEADS, 0], fc[0:HEADS, 0], 0.0, None, ALU.min).then_inc(f_step, 1)
            dve.memset(fc[0:HEADS, 2], 1.0).then_inc(f_step, 1)
            dve.wait_ge(f_step, 3)
            dve.tensor_tensor(fc[0:HEADS, 0], fc[0:HEADS, 0], fc[0:HEADS, 1], ALU.subtract).then_inc(f_step, 1)
            dve.wait_ge(f_step, 4)
            dve.tensor_tensor_scan(out=fc[0:HEADS, 3], data0=fc[0:HEADS, 2], data1=fc[0:HEADS, 0], initial=0.0, op0=ALU.mult,
                                   op1=ALU.add).then_inc(f_step, 1)
            dve.wait_ge(f_step, 5)
            dve.tensor_scalar(fc[0:HEADS, 1], fc[0:HEADS, 3], -1.0, None, ALU.mult).then_inc(f_cum, 1)

            norm(3, big[:, 2], SC_M1, SH_M1, NM1, None, (w_used, U_Q))
            pair(U_Q, none)

            def heads(i):
                for e in range(4):
                    dve.wait_ge(a_s, i * 4 + (e + 1))
                    ge(dve, a_t, i * 4 + (e - 3))
                    dve.tensor_tensor(att[:, e], psum[:, e, 0:384], mask[:, :], ALU.add).then_inc(a_masked, 1)
                    dve.wait_ge(a_masked, i * 4 + (e + 1))
                    for tb, (c0, c1) in enumerate(((0, P), (P, 3 * P))):
                        ins = dve.tensor_reduce(stat[:, 0, e, tb:tb + 1], att[:, e, c0:c1], AX_X, ALU.max, negate=True)
                    ins.then_inc(a_max, 1)
                for e in range(4):
                    dve.wait_ge(a_exp, i * 4 + (e + 1))
                    dve.reciprocal(stat[:, 2, e, :], stat[:, 1, e, :]).then_inc(a_rec, 1)
                    dve.wait_ge(a_rec, i * 4 + (e + 1))
                    for tb, (c0, c1) in enumerate(((0, P), (P, 3 * P))):
                        ins = dve.tensor_scalar(att[:, e, c0:c1], att[:, e, c0:c1], stat[:, 2, e, tb:tb + 1], None, ALU.mult)
                    ins.then_inc(a_p, 1)
                for e in range(4):
                    dve.wait_ge(a_ohi, i * 4 + (e + 1))
                    hd = bass.ds(i * 4 + e, 1)
                    dve.tensor_tensor(h[:, 1, hd], psum[:, 6 + e % 2, 0:S].unsqueeze(1), h[:, 0, hd].bitcast(F32),
                                      ALU.subtract).then_inc(a_olo, 1)

            dve.wait_ge(mask_done, 3)
            heads(0)
            with dve.Fori(1, 4) as i:
                heads(i)
            pair(U_AO, add_to_x(U_AO, GU, G_M1))
            ffn(1, 4, big[:, 2], SC_F1, SH_F1, G_F1, (3, 7), U_UP1, U_DOWN1, 11, XD1, None)

            norm(5, big[:, 0], None, None, NFIN, (4, 7))

        @block.tensor
        def _(pe):
            mm = lambda out, a, b, start=False: pe.matmul(out, a, b, start=start, stop=False, skip_group_check=True)

            def turn(b, blocks, ready=None):
                if ready is not None:
                    pe.wait_ge(*ready)
                ge(pe, turned_out, b - 7)
                c0 = 0
                for src in blocks:
                    n = src.shape[0]
                    ins = pe.transpose(psum[0:src.shape[1], b % 8, c0:c0 + n], src, ident[0:n, 0:n])
                    c0 += n
                ins.then_inc(turned, 1)

            def mod_sum(s, bank, sdyn=0):
                pe.wait_ge(mod_used, sdyn * KT + KT * (s + 1))
                for kt in range(KT):
                    ins = mm(psum[:, bank, kt:kt + 1], mod_acc[:, P * kt:P * (kt + 1)], ones[:, 0:1], kt == 0)
                ins.then_inc(sum_ready, 1)

            pe.wait_ge(consts, 3)
            turn(B_C, [nat[0:KT, 0, :]], (silu_done, 1))
            turn(B_BIAS, [nat[0:96, 1, :], nat[0:32, 2, :], nat[0:96, 3, :]], (rest_loaded, 16 * 17))
            turn(B_GAIN, [nat[:, 4, :]])
            for i in range(2):
                turn(B_CONV + i, [nat[0:88, 5 + 4 * i + k, :] for k in range(4)])
            for b in range(8):
                turn(B_X + b, [x_nat[:, tb, P * kt:P * (kt + 1)] for kt in (2 * b, 2 * b + 1) for tb in range(TB)], (x_loaded, 32))
            turn(B_PRM, [prep[:, n, :] for n in (5, 4, 10, 11)], (prep_dve, PREP_DVE))
            for n in range(2):
                for b in range(4):
                    turn(B_CT + 4 * n + b, [c_nat[:, n, 4 * b + i, :] for i in range(4)], (c_loaded, 256))
            for n in range(2):
                for b in range(4):
                    turn(B_BT + 4 * n + b, [b_bar[:, n, 16 * b + 4 * i:16 * b + 4 * i + 4].rearrange("p j g h -> p (j g h)")
                                            for i in range(4)], (bar_done, 4 * n + 4))
            pe.wait_ge(turned_out, N_BATCH)
            mod_sum(SH_M0, 0)
            mod_sum(SC_M0, 1)

            def sums(i, buf, bank):
                for kt in range(KT):
                    if kt % 4 == 0:
                        pe.wait_ge(sq_done, 4 * i + kt // 4 + 1)
                    ins = mm(psum[:, bank, 0:S], ones[:, :], buf[:, kt], kt == 0)
                ins.then_inc(ss_done, 1)

            def unit(st, dyn, bank, xt, x_ready, first=False):
                pe.wait_ge(lo_done, dyn + (st + 1))
                for sem_, value in x_ready:
                    pe.wait_ge(sem_, value)
                sl = st % NSPLIT
                for k in range(UK):
                    x_hi, x_lo = xt(k)
                    for t in range(8):
                        c0 = k * UC + P * t
                        wh, wl = w_hi[:, sl, c0:c0 + P], w_lo[:, sl, c0:c0 + P]
                        acc = psum[:, bank + t // 2, S * (t % 2):S * (t % 2 + 1)]
                        mm(acc, wh, x_hi, first and k == 0 and t % 2 == 0)
                        mm(acc, wh, x_lo)
                        ins = mm(acc, wl, x_hi)
                ins.then_inc(w_used, 1)

            def group(base, n, bank, xt, ready, dyn=0):
                def one(k, j, first=False):
                    unit(base + j, dyn + k, bank, lambda r: xt(k, j, r), ready(k, j), first)

                one(0, 0, True)
                one(0, 1)
                with pe.Fori(0, n // 2 - 1) as i:
                    for j in range(2):
                        one(i * 2, 2 + j)

            def h_group(base, bank, dyn=0, made=None):
                group(base, GU, bank, lambda k, j, r: [flat(h[:, n, bass.ds(k * UK + (j * UK + r), 1)]) for n in range(2)],
                      lambda k, j: [(made[0], k * UK + (made[1] + UK * (j + 1)))] if made else [], dyn)

            def h_pair(base, made=None):
                h_group(base, 0, made=made)
                h_group(base + GU, 4)

            def ring_group(stage, first_unit, n, bank, count):
                def tiles(k, j, r):
                    t = 12 + 2 * ((first_unit + j) % 2) + r
                    return h[:, 0, t], h[:, 1, t]
                group(stage + first_unit, n, bank, tiles, lambda k, j: [(xlo_done, k + (count + first_unit + j + 1))])

            sums(0, big[:, 0], 7)
            pe.wait_ge(mod_ready, 2)
            h_pair(U_IN, (xlo_done, XN[0]))

            def inputs(m, q):
                b = 4 + 2 * (q % 2)
                ge(pe, s_rotm, m * 4 + (q - 1))
                n = m * 2 + q // 2
                for part in range(2):
                    for e in range(2):
                        r = slice(32 * (2 * (q % 2) + e), 32 * (2 * (q % 2) + e) + 32)
                        ins = mm(psum[:, b + e, S * part:S * (part + 1)], b_t[r, part, n], u_t[r, n], part == 0)
                ins.then_inc(s_bu, 1)

            def outputs(m, q):
                n = m * 2 + q // 2
                if q % 2 == 0:
                    ge(pe, s_yd, m * 2 + (q // 2 - 1))
                for half in range(2):
                    pe.wait_ge(s_prod, m * 8 + (2 * q + half + 1))
                    for e in range(2):
                        r = slice(32 * (2 * (q % 2) + e), 32 * (2 * (q % 2) + e) + 32)
                        for i in range(2):
                            ins = mm(psum[r, q // 2, 0:S], c_t[:, half, n, r], prod[:, 2 * half + i, e],
                                     half == 0 and i == 0)
                    ins.then_inc(s_y, 1)

            def s5(m):
                inputs(m, 0)
                for q in range(4):
                    if q < 3:
                        inputs(m, q + 1)
                    outputs(m, q)

            pe.wait_ge(copied, 2)
            for m in range(8):
                s5(m)

            pe.wait_ge(s_yd, 16)
            ring_group(U_GLU, 0, GU, 0, XG)
            mod_sum(G_M0, 4)
            pe.wait_ge(mod_ready, G_M0 + 1)
            ring_group(U_GLU, GU, GU, 4, XG)
            mod_sum(SH_F0, 0)
            pe.wait_ge(mod_ready, SH_F0 + 1)
            pe.wait_ge(zlo_done, 4)
            h_pair(U_OUT)
            mod_sum(SC_F0, 0)
            pe.wait_ge(mod_ready, SC_F0 + 1)

            def ffn(i, sq, up_base, down_base, x0, count, sections):
                sums(i, sq, 7)
                pe.wait_ge(xlo_done, x0 + KT)
                with pe.Fori(0, 5) as p:
                    for g in range(2):
                        h_group(up_base + GU * g, 4 * g, dyn=p * 16)
                    if sections:
                        mod_sum(sections[0], 0, p)
                        pe.wait_ge(mod_ready, p + (sections[0] + 1))
                h_group(up_base + 10 * GU, 0)
                for g in range(2):
                    ring_group(down_base, DU * g, DU, 4 * (1 - g), count)
                    if sections:
                        mod_sum(sections[1 + g], BANK_DOWN[g])
                        pe.wait_ge(mod_ready, sections[1 + g] + 1)

            ffn(1, big[:, 2], U_UP0, U_DOWN0, XN[1], XD0, (G_F0, G_M1, SH_F1))

            sums(2, big[:, 0], 7)
            h_pair(U_K, (xlo_done, XN[2]))
            mod_sum(SC_F1, 0)
            pe.wait_ge(mod_ready, SC_F1 + 1)

            def v_unit(st, bank, kt, first=False):
                pe.wait_ge(lo_done, st + 1)
                sl = st % NSPLIT
                for k in range(UK):
                    for tb in range(TB):
                        x_hi, x_lo = (h[:, n, kt + k, P * tb:P * (tb + 1)] for n in range(2))
                        acc = [psum[:, bank + 2 * tb + e] for e in range(2)]
                        wh, wl = ([w[:, sl, k * UC + 512 * e:k * UC + 512 * (e + 1)] for e in range(2)] for w in (w_hi, w_lo))
                        for e in range(2):
                            mm(acc[e], x_hi, wh[e], first and k == 0)
                        for e in range(2):
                            mm(acc[e], x_hi, wl[e])
                        for e in range(2):
                            ins = mm(acc[e], x_lo, wh[e])
                ins.then_inc(w_used, 1)

            for g in range(2):
                for j in range(GU):
                    v_unit(U_V + GU * g + j, 4 * g, UK * j, j == 0)
            mod_sum(G_F1, 0)
            pe.wait_ge(mod_ready, G_F1 + 1)
            pe.wait_ge(fw_split, 2)
            for tb in range(TB):
                for kt in range(KT):
                    x_hi, x_lo = (h[:, n, kt, P * tb:P * (tb + 1)] for n in range(2))
                    acc = psum[:, 0, HEADS * tb:HEADS * (tb + 1)]
                    mm(acc, x_hi, fw_hi[:, kt], kt == 0 and tb == 0)
                    mm(acc, x_hi, fw_lo[:, kt])
                    ins = mm(acc, x_lo, fw_hi[:, kt])
            ins.then_inc(f_sum, 1)
            pe.wait_ge(f_evac, 1)
            for tb in range(TB):
                ins = pe.transpose(psum[0:HEADS, 1, P * tb:P * (tb + 1)], f_nat[:, tb, :], ident[:, :])
            ins.then_inc(f_turn, 1)

            h_pair(U_Q, (xlo_done, XN[3]))

            def heads(i):
                for e in range(4):
                    q_h, k_h = (flat(big[:, n, bass.ds(i * 4 + e, 1)]) for n in (2, 0))
                    own = flat(sel[:, bass.ds(i * 4 + e, 1)])
                    ge(pe, a_masked, i * 4 + (e - 3))
                    sc = psum[:, e]
                    mm(sc[:, 0:P], q_h[:, 0:P], k_h[:, 0:P], True)
                    mm(sc[:, P:3 * P], q_h[:, P:S], k_h)
                    mm(sc[:, 0:P], fc[:, 3, 0:P], own)
                    for b in range(TB):
                        mm(sc[:, P * (b + 1):P * (b + 2)], fc[:, 3, P:S], own)
                    mm(sc[:, 0:P], own, fc[:, 1, 0:P])
                    mm(sc[:, P:3 * P], own, fc[:, 1, :]).then_inc(a_s, 1)

                def turn_p(e):
                    pe.wait_ge(a_p, i * 4 + (e + 1))
                    ge(pe, a_tc, i * 4 + (e - 1))
                    for b in range(3):
                        ins = pe.transpose(psum[:, 4 + e % 2, P * b:P * (b + 1)], att[:, e, P * b:P * (b + 1)], ident[:, :])
                    ins.then_inc(a_t, 1)

                def values(e):
                    pe.wait_ge(a_tc, i * 4 + (e + 1))
                    ge(pe, a_olo, i * 4 + (e - 1))
                    v_h = [v_nat[:, tb, 512 * i + P * e:512 * i + P * (e + 1)] for tb in range(TB)]
                    mm(psum[:, 6 + e % 2, 0:S], v_h[0], att_t[:, e % 2, 0:S], True)
                    mm(psum[:, 6 + e % 2, P:S], v_h[1], att_t[:, e % 2, S:3 * P]).then_inc(a_o, 1)

                turn_p(0)
                for e in range(1, 4):
                    turn_p(e)
                    values(e - 1)
                values(3)

            pe.wait_ge(copied, 8)
            pe.wait_ge(sel_done, 2)
            pe.wait_ge(f_cum, 1)
            for i in range(4):
                heads(i)
            h_pair(U_AO, (a_olo, 0))
            ffn(3, big[:, 2], U_UP1, U_DOWN1, XN[4], XD1, None)

            sums(4, big[:, 0], 7)
            pe.wait_ge(scaled, 6 * KT)
            for b in range(8):
                ge(pe, o_copied, b - 3)
                for j in range(4):
                    ins = pe.transpose(psum[:, b % 4, P * j:P * (j + 1)], big[:, 0, 4 * (b % 4) + j, P * (b // 4):P * (b // 4 + 1)],
                                       ident[:, :])
                ins.then_inc(o_turned, 1)


_INS = ['x', 'c', 'mod_w', 'mod_b', 'norm_mix_g', 'norm_ffn_g', 'ssm_w_in', 'ssm_log_step', 'ssm_a_re', 'ssm_a_im',
        'ssm_b_re', 'ssm_b_im', 'ssm_c_re', 'ssm_c_im', 'ssm_d', 'ssm_glu_w', 'ssm_glu_b', 'ssm_w_out', 'kv_mod_w',
        'kv_mod_b', 'kv_norm_g', 'kv_w', 'forget_b', 'attn_w_q', 'attn_w_out', 'ffn_w_up', 'ffn_conv_w', 'ffn_conv_b',
        'ffn_w_down', 'final_norm_g']


def kernel(**inputs):
    import numpy as _np
    import concourse.bacc as _bacc
    from concourse import mybir as _mybir
    from concourse.bass_utils import run_bass_kernel_spmd as _run

    nc = _bacc.Bacc("TRN2", target_bir_lowering=False, num_devices=1)
    arrays, args = {}, []
    for name in _INS:
        a = _np.ascontiguousarray(inputs[name])
        arrays[f"in_{name}_dram"] = a
        args.append(nc.dram_tensor(f"in_{name}_dram", a.shape, _mybir.dt.from_np(a.dtype), kind="ExternalInput").ap())
    args.append(nc.dram_tensor("out_0_dram", (1, S, D), _mybir.dt.float32, kind="ExternalOutput").ap())
    trunk(nc, *args)
    r = _run(nc, [arrays], core_ids=[0])
    return r.results[0]["out_0_dram"]
```

```python
from contextlib import ExitStack

import concourse.bass as bass
from concourse import mybir

F32 = mybir.dt.float32
F32R = mybir.dt.float32r
ALU = mybir.AluOpType
ACT = mybir.ActivationFunctionType
AX_X = mybir.AxisListType.X

P = 128
D = 2048
S = 256
KT = D // P
TB = S // P
FF = 11 * D // 4
FT = FF // P
HEADS = 16
GROUPS, STATE, GW = 128, 64, 16
ST = GROUPS * STATE // P
EPS = 1e-6
PI = 3.141592653589793
TWO_PI_DOWN = 6.2831850
ROUND = 12582912.0
TWO_PI_1 = 6.28125
TWO_PI_2 = 0.0019340515136718750
TWO_PI_3 = 2 * PI - TWO_PI_1 - TWO_PI_2
MASKED = -1.0e30

NW, NMOD, LEAD = 4, 2, 3
UK = 2
UC = 1024
WF = UK * UC
GU = KT // UK
DU = FT // UK

SH_M0, SC_M0, G_M0, SH_F0, SC_F0, G_F0, SH_KV, SC_KV, SH_M1, SC_M1, G_M1, SH_F1, SC_F1, G_F1 = range(14)

U_IN = 0
U_GLU = U_IN + 2 * GU
U_OUT = U_GLU + 2 * GU
U_UP0 = U_OUT + 2 * GU
U_DOWN0 = U_UP0 + 11 * GU
U_K = U_DOWN0 + 2 * DU
U_V = U_K + 2 * GU
U_Q = U_V + 2 * GU
U_AO = U_Q + 2 * GU
U_UP1 = U_AO + 2 * GU
U_DOWN1 = U_UP1 + 11 * GU
U_END = U_DOWN1 + 2 * DU

XG = KT
XD0 = XG + 2 * GU + KT
XD1 = XD0 + 2 * DU + 3 * KT
XN = (0, XG + 2 * GU, XD0 + 2 * DU, XD0 + 2 * DU + KT, XD0 + 2 * DU + 2 * KT)
BANK_DOWN = (0, 4)
S5_STEPS = ST // 2
NTAB = 3
S5_UNITS = 6
S5_UNIT = {4 * i + 8: i for i in range(S5_UNITS)}
S5_GELU = {4 * m + 6: m for m in range(8)}
PREP_DVE = 22
FIRST = 2 * KT


def flat(ap):
    return ap.rearrange("p a n -> p (a n)")


def ge(eng, sem, value):
    if not (isinstance(value, int) and value <= 0):
        eng.wait_ge(sem, value)


def ring(slots, i):
    t = (12 if slots == 2 else 0) + 2 * (i % slots)
    return slice(t, t + 2)


def steps(eng, n, step, emit):
    with eng.Fori(0, n // step) as i:
        for j in range(step):
            emit(i * step, j)


def trunk(nc, x, c, mod_w, mod_b, norm_mix_g, norm_ffn_g, ssm_w_in, ssm_log_step, ssm_a_re, ssm_a_im,
          ssm_b_re, ssm_b_im, ssm_c_re, ssm_c_im, ssm_d, ssm_glu_w, ssm_glu_b, ssm_w_out, kv_mod_w,
          kv_mod_b, kv_norm_g, kv_w, forget_b, attn_w_q, attn_w_out, ffn_w_up, ffn_conv_w, ffn_conv_b,
          ffn_w_down, final_norm_g, out):
    ctx = ExitStack()
    with ctx:
        top = [16512]

        def sb(name, shape, dt=F32, at=None):
            n = 2 if dt == mybir.dt.bfloat16 else 4
            for d in shape[1:]:
                n *= d
            if at is None:
                at = top[0]
                top[0] += (n + 31) // 32 * 32
            return nc.alloc_sbuf_tensor_at(name, shape, dt, offset=at)

        def sem(name):
            return ctx.enter_context(nc.semaphore(name))

        raw_at = top[0]
        w_raw = sb("w_raw", [P, NW, WF])
        w_lo = sb("w_lo", [P, NW, WF], F32R, at=raw_at)
        w_hi = sb("w_hi", [P, NW, WF], F32R)
        first = sb("first", [P, NW, 2, D], at=raw_at)
        m_raw = sb("m_raw", [P, NMOD, D])
        xT = sb("xT", [P, KT, S])
        h_at = top[0]
        h = sb("h", [P, 2, KT, S], F32R)
        big_at = top[0]
        big = sb("big", [P, 3, KT, S])
        acc_at = top[0]
        mod_acc = sb("mod_acc", [P, D])
        ones = sb("ones", [P, P])
        ident = sb("ident", [P, P])
        mod_bias = sb("mod_bias", [P, 14 * KT])
        modT = sb("modT", [P, 14, KT])
        gains = sb("gains", [P, 8 * KT])
        convT = sb("convT", [P, 2, 4, 88])
        rstd = sb("rstd", [P, S])
        gs = sb("gs", [P, KT])
        cT = sb("cT", [P, KT])
        half_pi = sb("half_pi", [P, 1])
        eps = sb("eps", [P, 1])
        round_c = sb("round_c", [P, 2])
        scr_at = top[0]
        assert scr_at + 16 * 1024 <= 229344, scr_at
        scr = sb("scr", [P, 4096])

        NM0, NM1, NF0, NF1, NKV, NFIN, GLUB, SKIP = range(8)

        def gain(n, kt=None):
            return gains[:, n * KT:(n + 1) * KT] if kt is None else gains[:, n * KT + kt:n * KT + kt + 1]

        u_t = big[:, 0]
        b_t = sb("b_t", [P, 2, KT, P], at=big_at + 16384)
        c_t = sb("c_t", [P, 2, KT, P], at=big_at + 32768)
        v_nat = sb("v_nat", [P, TB, D], at=big_at + 16384)
        ffg = sb("ffg", [P, 48, S], at=big_at)
        x_nat = sb("x_nat", [P, TB, D], at=big_at + 16384)
        out_nat = sb("out_nat", [P, TB, D], at=big_at + 16384)
        c_nat = sb("c_nat", [P, 2, KT, P], at=big_at)
        b_raw = sb("b_raw", [P, 2, ST, GW], at=h_at)
        b_tmp = sb("b_tmp", [P, 2, ST, GW], at=h_at + 8192)
        b_bar = sb("b_bar", [P, 2, ST, 2, GW], at=h_at + 16384)
        nat = sb("nat", [P, 16, P], at=scr_at)
        prep = sb("prep", [64, 14, P], at=scr_at + 8192)
        step = sb("step", [64, 2], at=scr_at + 8192 + 14 * 512)
        tab = sb("tab", [P, NTAB, 2, 2, S], at=h_at)
        rot = sb("rot", [P, 2, 2, 2, S], at=h_at + 16384)
        tmp = sb("tmp", [P, 2, 2, S], at=h_at + 16384 + 8192)
        prod = sb("prod", [P, 4, 2, S], at=scr_at)
        yb = sb("yb", [P, 2, S], at=scr_at + 8192)
        arg = sb("arg", [P, 2, 2, S], at=scr_at + 10240)
        prm = sb("prm", [P, 4, ST], at=scr_at + 14336)
        iota = sb("iota", [P, S], at=scr_at + 15360)
        sqb = sb("sqb", [P, 8, S], at=scr_at + 8192)
        conv = sb("conv", [P, 8, S], at=scr_at)
        sel = sb("sel", [P, HEADS, P], at=acc_at)
        mask = sb("mask", [P, 384], at=scr_at)
        fc = sb("fc", [P, 4, S], at=scr_at + 1536)
        fw_raw = sb("fw_raw", [P, KT, HEADS], at=scr_at + 5632)
        fw_hi = sb("fw_hi", [P, KT, HEADS], F32R, at=scr_at + 6656)
        fw_lo = sb("fw_lo", [P, KT, HEADS], F32R, at=scr_at + 7680)
        f_nat = sb("f_nat", [P, TB, HEADS], at=scr_at + 8704)
        att = sb("att", [P, 4, 384], at=scr_at + 5632)
        att_t = sb("att_t", [P, 2, 384], at=scr_at + 5632 + 6144)
        stat = sb("stat", [P, 3, 4, TB], at=scr_at + 5632 + 6144 + 3072)
        fb = sb("fb", [HEADS, 1], at=scr_at + 5632 + 6144 + 3072 + 96)

        psum = ctx.enter_context(nc.psum_tensor("psum_all", [P, 8, 512], F32))

        w_full = [sem(f"w_full{i}") for i in range(NW)]
        m_full = [sem(f"m_full{i}") for i in range(NMOD)]
        hi_done, lo_done, w_used = sem("hi_done"), sem("lo_done"), sem("w_used")
        mod_used, acc_ready, sum_ready, mod_ready = sem("mod_used"), sem("acc_ready"), sem("sum_ready"), sem("mod_ready")
        x_loaded, nat_loaded, ab_loaded, bc_loaded, fw_loaded = (
            sem("x_loaded"), sem("nat_loaded"), sem("ab_loaded"), sem("bc_loaded"), sem("fw_loaded"))
        consts, silu_done, rest_loaded, b_loaded, c_loaded = (
            sem("consts"), sem("silu_done"), sem("rest_loaded"), sem("b_loaded"), sem("c_loaded"))
        prep_red, gs_done, fc_zero, iota_done, zhi_done, zlo_done, x_out, copied, f_act = (
            sem("prep_red"), sem("gs_done"), sem("fc_zero"), sem("iota_done"), sem("zhi_done"), sem("zlo_done"), sem("x_out"), sem("copied"), sem("f_act"))
        turned, turned_out = sem("turned"), sem("turned_out")
        prep_act, prep_dve, bar_done = sem("prep_act"), sem("prep_dve"), sem("bar_done")
        c_zero = sem("c_zero")
        sq_done, ss_done, r_done, scaled, xhi_done, xlo_done = (
            sem("sq_done"), sem("ss_done"), sem("r_done"), sem("scaled"), sem("xhi_done"), sem("xlo_done"))
        ss_half = sem("ss_half")
        first_full = [sem(f"first_full{i}") for i in range(NW)]
        s_v, s_t, s_r, s_abs, s_tab, s_bu = (sem(n) for n in ("s_v", "s_t", "s_r", "s_abs", "s_tab", "s_bu"))
        s_rotm, s_rota, s_z, s_prod, s_y, s_yd, s_g = (
            sem(n) for n in ("s_rotm", "s_rota", "s_z", "s_prod", "s_y", "s_yd", "s_g"))
        s_rnd, s_du = sem("s_rnd"), sem("s_du")
        s_sg, s_zg = sem("s_sg"), sem("s_zg")
        conv_act, conv_1, conv_2, silu_c, ffg_done = (
            sem("conv_act"), sem("conv_1"), sem("conv_2"), sem("silu_c"), sem("ffg_done"))
        fw_split, f_sum, f_evac, f_turn, f_step, f_cum, sel_done, mask_done = (
            sem(n) for n in ("fw_split", "f_sum", "f_evac", "f_turn", "f_step", "f_cum", "sel_done", "mask_done"))
        a_s, a_masked, a_max, a_neg, a_exp, a_rec, a_p, a_t, a_tc, a_o, a_ohi, a_olo = (
            sem(f"a_{n}") for n in ("s", "masked", "max", "neg", "exp", "rec", "p", "t", "tc", "o", "ohi", "olo"))
        o_scaled, o_turned, o_copied, stored = sem("o_scaled"), sem("o_turned"), sem("o_copied"), sem("stored")

        block = ctx.enter_context(nc.Block())

        def rows(w):
            return w.rearrange("(t p) n -> p t n", p=P)

        w_in_v, glu_v, w_out_v = rows(ssm_w_in[0]), rows(ssm_glu_w[0]), rows(ssm_w_out[0])
        kv_v, q_v, ao_v = rows(kv_w), rows(attn_w_q[0]), rows(attn_w_out[0])
        up_v = [ffn_w_up[i].rearrange("(t p) (a n) -> p t a n", p=P, a=2) for i in range(2)]
        down_v = [rows(ffn_w_down[i]) for i in range(2)]
        mod_v = [rows(mod_w[0]), rows(kv_mod_w), rows(mod_w[1])]

        def mod_section(s):
            return (0, s) if s < SH_KV else (1, s - SH_KV) if s < SH_M1 else (2, s - SH_M1)

        @block.sync
        def _(sp):
            def load_w(src, st, dyn=0):
                if st < NW:
                    sp.wait_ge(mod_used, FIRST - 2 * (NW - 1 - st // 2))
                else:
                    sp.wait_ge(w_used, dyn + (st - NW + 1))
                for k in range(UK):
                    sp.dma_start(w_raw[:, st % NW, UC * k:UC * (k + 1)], src(k)).then_inc(w_full[st % NW], 16)

            def load_m(s, kt, dyn=0, sdyn=0):
                t, ms = mod_section(s)
                st = KT * s + kt
                if not (isinstance(sdyn, int) and isinstance(dyn, int)) or st >= FIRST + NMOD:
                    sp.wait_ge(mod_used, sdyn * KT + dyn + (st - NMOD + 1))
                src = mod_v[t][:, bass.ds(dyn + kt, 1), bass.ds(sdyn * D + ms * D, D)]
                sp.dma_start(m_raw[:, st % NMOD], src).then_inc(m_full[st % NMOD], 16)

            def load_pair(wv, col, base, s=None):
                for g in range(2):
                    def one(k, j):
                        load_w(lambda r: wv[:, bass.ds(k * UK + (j * UK + r), 1), col + UC * g:col + UC * (g + 1)], base + GU * g + j, k)
                        if s is not None:
                            load_m(s, GU * g + j, k)
                    steps(sp, GU, 4, one)

            def load_up(layer, p, base, dyn, groups=2, s=None):
                for j in range(GU * groups):
                    k, g = j % GU, j // GU
                    load_w(lambda r: up_v[layer][:, UK * k + r, :, bass.ds(p * 1024 + 512 * g, 512)], base + j, dyn)
                    if s is not None:
                        load_m(s[0], j, 0, s[1])

            def load_down(layer, base, sections):
                for g in range(2):
                    def one(k, j, m):
                        load_w(lambda r: down_v[layer][:, bass.ds(k * UK + (j * UK + r), 1), UC * g:UC * (g + 1)], base + DU * g + j, k)
                        if m:
                            load_m(sections[g], j, k)
                    steps(sp, KT, 4, lambda k, j: one(k, j, sections[g] is not None))
                    for j in range(KT, DU):
                        one(0, j, False)

            for n in range(FIRST // 2):
                s, kt = n // (KT // 2), 2 * n % KT
                ge(sp, mod_used, 2 * (n - NW + 1))
                sp.dma_start(first[:, n % NW],
                             mod_v[0][:, kt:kt + 2, D * s:D * (s + 1)]).then_inc(first_full[n % NW], 16)
            for j in range(2 * GU):
                k, g = j % GU, j // GU
                load_w(lambda r: w_in_v[:, UK * k + r, UC * g:UC * g + UC], U_IN + j)
                load_m(G_M0, j)
            load_pair(glu_v, 0, U_GLU, SH_F0)
            load_pair(w_out_v, 0, U_OUT, SC_F0)
            load_up(0, 0, U_UP0, 0, s=(G_F0, 0))
            with sp.Fori(0, 2) as i:
                load_up(0, i + 1, U_UP0 + 16, i * 16, s=(SH_KV, i))
            with sp.Fori(0, 2) as i:
                load_up(0, i + 3, U_UP0 + 48, i * 16)
            load_up(0, 5, U_UP0 + 80, 0, groups=1)
            load_down(0, U_DOWN0, (SH_M1, SC_M1))
            load_pair(kv_v, 0, U_K, G_M1)
            load_pair(kv_v, D, U_V, SH_F1)
            load_pair(q_v, 0, U_Q, SC_F1)
            load_pair(ao_v, 0, U_AO)
            with sp.Fori(0, 5) as i:
                load_up(1, i, U_UP1, i * 16)
            load_up(1, 5, U_UP1 + 80, 0, groups=1)
            load_down(1, U_DOWN1, (G_F1, None))
            for tb in range(TB):
                sp.wait_ge(o_copied, 4 * (tb + 1))
                sp.dma_start(out[0, P * tb:P * (tb + 1), :], out_nat[:, tb]).then_inc(stored, 16)
            sp.wait_ge(stored, 32)

        B_C, B_BIAS, B_GAIN, B_CONV, B_X, B_PRM, B_CT, B_BT = 0, 1, 2, 3, 5, 13, 14, 22
        N_BATCH = 30

        @block.gpsimd
        def _(pool):
            pool.memset(ident[:, :], 0.0).then_inc(consts, 1)
            pool.memset(ones[:, :], 1.0).then_inc(consts, 1)
            pool.wait_ge(consts, 2)
            pool.affine_select(out=ident[:, :], in_=ident[:, :], compare_op=ALU.not_equal, fill=1.0, base=0,
                               pattern=[[-1, P]], channel_multiplier=1).then_inc(consts, 1)
            pool.memset(c_nat[:, :, :, :], 0.0).then_inc(c_zero, 1)
            pool.memset(b_bar[:, :, :, :, :], 0.0).then_inc(c_zero, 1)
            pool.memset(half_pi[:, :], PI / 2)
            pool.memset(round_c[:, 0:1], ROUND)
            pool.memset(round_c[:, 1:2], -ROUND)
            pool.memset(eps[:, :], EPS).then_inc(consts, 1)
            pool.wait_ge(turned_out, B_PRM + 1)
            pool.memset(iota[:, :], 1.0).then_inc(consts, 1)

            def turns(k, dyn=0):
                pool.wait_ge(s_v, dyn + (k + 1))
                pool.tensor_tensor(arg[:, 0], arg[:, 1], arg[:, 0], ALU.subtract).then_inc(s_r, 1)

            def products(k, dyn=0):
                pool.wait_ge(s_z, dyn + (k + 1))
                cos, sin = (tab[:, k % NTAB, n] for n in range(2))
                re, im = (rot[:, k % 2, n] for n in range(2))
                ge(pool, s_y, dyn * 2 + (2 * k - 1))
                pool.tensor_tensor(prod[:, 0], cos, re, ALU.mult)
                pool.tensor_tensor(prod[:, 1], sin, im, ALU.mult).then_inc(s_prod, 1)
                ge(pool, s_y, dyn * 2 + 2 * k)
                pool.tensor_tensor(prod[:, 2], sin, re, ALU.mult)
                pool.tensor_tensor(prod[:, 3], cos, im, ALU.mult).then_inc(s_prod, 1)

            turns(0)
            turns(1)
            for k in range(2, 8):
                turns(k)
                products(k - 2)
            with pool.Fori(0, (S5_STEPS - 8) // 12) as i:
                for k in range(8, 20):
                    turns(k, i * 12)
                    products(k - 2, i * 12)
            products(S5_STEPS - 2)
            products(S5_STEPS - 1)

            def gate(g, base):
                pool.wait_ge(silu_c, g + (base + 1))
                pool.wait_ge(conv_2, g * 4 + (4 * base + 4))
                pool.tensor_tensor(ffg[:, bass.ds(g * 4, 4)], conv[:, 0:4], conv[:, 4:8], ALU.mult).then_inc(ffg_done, 1)

            with pool.Fori(0, 11) as g:
                gate(g, 0)
            pool.wait_ge(ffg_done, 11)
            pool.memset(fc[:, :, :], 0.0).then_inc(fc_zero, 1)
            pool.memset(mask[:, :], 0.0).then_inc(mask_done, 1)
            pool.wait_ge(mask_done, 1)
            pool.affine_select(out=mask[:, 0:P], in_=mask[:, 0:P], compare_op=ALU.is_ge, fill=MASKED, base=0,
                               pattern=[[-1, P]], channel_multiplier=1).then_inc(mask_done, 1)
            pool.affine_select(out=mask[:, 2 * P:], in_=mask[:, 2 * P:], compare_op=ALU.is_ge, fill=MASKED, base=0,
                               pattern=[[-1, P]], channel_multiplier=1).then_inc(mask_done, 1)
            pool.wait_ge(mod_ready, G_F1)
            pool.memset(sel[:, :, :], 0.0).then_inc(sel_done, 1)
            pool.wait_ge(sel_done, 1)
            pool.affine_select(out=sel[:, :, :], in_=sel[:, :, :], compare_op=ALU.not_equal, fill=1.0, base=0,
                               pattern=[[-1, HEADS], [0, P]], channel_multiplier=1).then_inc(sel_done, 1)
            with pool.Fori(0, 11) as g:
                gate(g, 11)

        @block.scalar
        def _(act):
            act.dma_start(nat[0:KT, 0, :], c.rearrange("a (t p) -> (a t) p", p=P)).then_inc(nat_loaded, 16)
            nb = 0
            act.dma_start(prep[:, 0, :], ssm_a_re[0].rearrange("(j g) p -> j (g p)", g=2)).then_inc(ab_loaded, 16)
            act.dma_start(prep[:, 1, :], ssm_a_im[0].rearrange("(j g) p -> j (g p)", g=2)).then_inc(ab_loaded, 16)
            act.dma_start(step[:, :], ssm_log_step[0].rearrange("(j g) -> j g", g=2)).then_inc(ab_loaded, 16)
            act.dma_start(nat[0:96, 1, :], mod_b[0].rearrange("(t p) -> t p", p=P)).then_inc(rest_loaded, 16)
            act.dma_start(nat[0:32, 2, :], kv_mod_b.rearrange("(t p) -> t p", p=P)).then_inc(rest_loaded, 16)
            act.dma_start(nat[0:96, 3, :], mod_b[1].rearrange("(t p) -> t p", p=P)).then_inc(rest_loaded, 16)
            for n, g in enumerate((norm_mix_g.rearrange("a (t p) -> (a t) p", p=P), norm_ffn_g.rearrange("a (t p) -> (a t) p", p=P),
                                   kv_norm_g.rearrange("(t p) -> t p", p=P), final_norm_g.rearrange("(t p) -> t p", p=P),
                                   ssm_glu_b.rearrange("a (t p) -> (a t) p", p=P), ssm_d.rearrange("a (t g) h -> (a t) (g h)", g=8))):
                act.dma_start(nat[nb:nb + g.shape[0], 4, :], g).then_inc(rest_loaded, 16)
                nb += g.shape[0]
            for i in range(2):
                for k in range(3):
                    act.dma_start(nat[0:88, 5 + 4 * i + k, :], ffn_conv_w[i, k].rearrange("(t p) -> t p", p=P)).then_inc(rest_loaded, 16)
                act.dma_start(nat[0:88, 8 + 4 * i, :], ffn_conv_b[i].rearrange("(t p) -> t p", p=P)).then_inc(rest_loaded, 16)
            for tb in range(TB):
                act.dma_start(x_nat[:, tb], x[0, P * tb:P * (tb + 1), :]).then_inc(x_loaded, 16)
            for n, w in enumerate((ssm_b_re, ssm_b_im)):
                act.dma_start(b_raw[:, n], w[0].rearrange("(j g) p h -> (g p) j h", g=2)).then_inc(b_loaded, 16)
            act.wait_ge(c_zero, 1)
            for n, w in enumerate((ssm_c_re, ssm_c_im)):
                wv = w[0].rearrange("(n i g) h p -> i g h n p", i=4, g=2)
                for i in range(4):
                    for g in range(2):
                        at = 32 * i + GW * g
                        act.dma_start(c_nat[at:at + GW, n, :, STATE * g:STATE * (g + 1)], wv[i, g]).then_inc(c_loaded, 16)

            def turn_out(b, dst, n=512, scale=1.0):
                act.wait_ge(turned, b + 1)
                act.activation(dst, psum[:, b % 8, 0:n], ACT.Copy, scale=scale).then_inc(turned_out, 1)

            act.wait_ge(nat_loaded, 16)
            act.activation(nat[0:KT, 0, :], nat[0:KT, 0, :], ACT.Silu).then_inc(silu_done, 1)
            turn_out(B_C, cT[:, :], KT)
            act.wait_ge(ab_loaded, 48)
            act.activation(step[:, :], step[:, :], ACT.Exp).then_inc(prep_act, 1)
            act.wait_ge(prep_dve, 2)
            act.activation(prep[:, 4, :], prep[:, 2, :], ACT.Exp).then_inc(prep_act, 1)
            turn_out(B_BIAS, mod_bias[:, :], 14 * KT)
            turn_out(B_GAIN, gains[:, :], P)
            for i in range(2):
                turn_out(B_CONV + i, convT[:, i], 352)
            for b in range(8):
                turn_out(B_X + b, xT[:, 2 * b:2 * b + 2].rearrange("p t s -> p (t s)"))
            act.wait_ge(prep_dve, 7)
            act.activation(prep[:, 6, :], prep[:, 5, :], ACT.Sin, scale=TWO_PI_DOWN).then_inc(prep_act, 1)
            act.activation(prep[:, 7, :], prep[:, 5, :], ACT.Abs).then_inc(prep_act, 1)
            act.wait_ge(prep_act, 4)
            act.wait_ge(consts, 4)
            act.activation(prep[:, 7, :], prep[:, 7, :], ACT.Sin, scale=-TWO_PI_DOWN, bias=half_pi[0:64, :]).then_inc(prep_act, 1)
            turn_out(B_PRM, prm[:, :, :].rearrange("p a j -> p (a j)"), 4 * ST)
            for n in range(2):
                for b in range(4):
                    turn_out(B_CT + 4 * n + b, c_t[:, n, 4 * b:4 * b + 4].rearrange("p t s -> p (t s)"))
            for n in range(2):
                for b in range(4):
                    turn_out(B_BT + 4 * n + b, b_t[:, n, 4 * b:4 * b + 4].rearrange("p t s -> p (t s)"))

            def hi(st, dyn=0):
                act.wait_ge(w_full[st % NW], dyn * (16 * UK // NW) + 16 * UK * (st // NW + 1))
                if st < NW:
                    act.wait_ge(mod_used, FIRST - 2 * (1 - st // 2))
                act.activation(w_hi[:, st % NW], w_raw[:, st % NW], ACT.Copy).then_inc(hi_done, 1)

            def squares(i, g):
                if g:
                    act.wait_ge(ss_half, i)
                for b in range(4):
                    act.wait_ge(x_out, KT * (i - 1) + 8 * g + 2 * b + 2)
                    act.activation(sqb[:, 2 * b:2 * b + 2], xT[:, 8 * g + 2 * b:8 * g + 2 * b + 2], ACT.Square).then_inc(sq_done, 1)

            def root(i, bank):
                act.wait_ge(ss_done, i + 1)
                act.activation(rstd[:, :], psum[:, bank, 0:S], ACT.Sqrt, scale=1.0 / D, bias=eps[:, :]).then_inc(r_done, 1)

            def norm_hi(buf, shift, n):
                act.wait_ge(mod_ready, shift + 1)
                def one(k, j):
                    act.wait_ge(scaled, k + (KT * n + j + 1))
                    act.activation(h[:, 0, bass.ds(k + j, 1)], buf[:, bass.ds(k + j, 1)], ACT.Identity,
                                   bias=modT[:, shift, bass.ds(k + j, 1)]).then_inc(xhi_done, 1)
                steps(act, KT, 4, one)

            def ring_hi(src, unit0, i, slots, k=0, t0=None):
                ge(act, w_used, k + (unit0 + i - slots + 1))
                t = 2 * i if t0 is None else t0
                act.activation(h[:, 0, ring(slots, i)], src[:, bass.ds(k * 2 + t, 2)], ACT.Copy).then_inc(xhi_done, 1)

            def plain_pair(base, evac_out=None):
                for g in range(2):
                    for j in range(GU):
                        hi(base + GU * g + j + LEAD)
                    if evac_out is not None:
                        evac_out(g)

            def copy_out(base, count, dst, scale=1.0):
                def f(g):
                    act.wait_ge(w_used, base + GU * (g + 1))
                    src = psum[:, 4 * g:4 * g + 4]
                    if len(dst(g).shape) == 4:
                        src = src.rearrange("p (t b) n -> p t b n", t=TB)
                    act.activation(dst(g), src, ACT.Copy, scale=scale).then_inc(copied, 1)
                return f

            act.wait_ge(turned_out, N_BATCH)
            for b in range(8):
                act.activation(big[:, 0, 2 * b:2 * b + 2], xT[:, 2 * b:2 * b + 2], ACT.Square).then_inc(sq_done, 1)
            for j in range(LEAD):
                hi(U_IN + j)
            root(0, 7)
            norm_hi(big[:, 0], SH_M0, 0)
            plain_pair(U_IN, copy_out(U_IN, 0, lambda g: u_t[:, 8 * g:8 * g + 8].rearrange("p (b t) s -> p b (t s)", b=4)))

            def turns(q):
                ge(act, s_tab, q)
                for e in range(2):
                    a = act.activation(arg[:, 0, e], iota[:, :], ACT.Copy, scale=prm[:, 0, 2 * q + e:2 * q + e + 1])
                a.then_inc(s_t, 1)
                act.wait_ge(s_t, q + 1)
                act.activation(arg[:, 1], arg[:, 0], ACT.Identity, bias=round_c[:, 0:1]).then_inc(s_rnd, 1)
                act.wait_ge(s_rnd, q + 1)
                act.activation(arg[:, 1], arg[:, 1], ACT.Identity, bias=round_c[:, 1:2]).then_inc(s_v, 1)

            def tables(q):
                ge(act, s_prod, 2 * (q - NTAB + 1))
                act.wait_ge(s_r, q + 1)
                act.activation(tab[:, q % NTAB, 1], arg[:, 0], ACT.Sin, scale=-TWO_PI_DOWN)
                act.activation(arg[:, 1], arg[:, 0], ACT.Abs).then_inc(s_abs, 1)
                act.wait_ge(s_abs, q + 1)
                act.activation(tab[:, q % NTAB, 0], arg[:, 1], ACT.Sin, scale=-TWO_PI_DOWN, bias=half_pi[:, :]).then_inc(s_tab, 1)

            act.wait_ge(iota_done, 1)
            turns(0)
            for q in range(2):
                tables(q)
                turns(q + 1)
            for q in range(S5_STEPS + 3):
                if q + 2 < S5_STEPS:
                    tables(q + 2)
                if q + 3 < S5_STEPS:
                    turns(q + 3)
                m = S5_GELU.get(q)
                if m is not None:
                    act.wait_ge(s_yd, 2 * m + 2)
                    act.activation(u_t[:, 2 * m:2 * m + 2], yb[:, :], ACT.Gelu_apprx_tanh).then_inc(s_g, 1)
                    act.wait_ge(s_g, m + 1)
                    ring_hi(u_t, U_GLU, m, 2)
                if q in S5_UNIT:
                    hi(U_GLU + S5_UNIT[q] + LEAD)

            for j in range(S5_UNITS, 2 * GU):
                hi(U_GLU + j + LEAD)
                if j + 2 in range(GU, 2 * GU):
                    ring_hi(u_t, U_GLU, j + 2, 2, t0=2 * ((j + 2) % GU))
                if j % GU < GU - 1:
                    continue
                g = j // GU
                act.wait_ge(w_used, U_GLU + GU * (g + 1))
                for b in range(2):
                    for j in range(4):
                        t = 4 * b + j
                        act.activation(big[:, 1, 8 * g + t], psum[:, 4 * (1 - g) + t // 2, S * (t % 2):S * (t % 2 + 1)], ACT.Sigmoid,
                                       bias=gain(GLUB, 8 * g + t)).then_inc(s_sg, 1)
                for b in range(2):
                    act.wait_ge(s_zg, 2 * g + b + 1)
                    t = 8 * g + 4 * b
                    act.activation(h[:, 0, t:t + 4], big[:, 1, t:t + 4], ACT.Copy).then_inc(zhi_done, 1)
            plain_pair(U_OUT, lambda g: squares(1, g))

            def ffn(layer, n, sq, shift, up_base, down_base, gbase, n_sum):
                root(n_sum - 1, 7 if layer == 0 else 3)
                norm_hi(sq, shift, n)

                def taps(g, bank):
                    ge(act, ffg_done, g + gbase)
                    act.wait_ge(w_used, g * GU + (up_base + GU))
                    for t in range(8):
                        tile = g * 4 + (t if t < 4 else t - 4 + FT)
                        a = act.activation(conv[:, t], psum[:, bank + t // 2, S * (t % 2):S * (t % 2 + 1)], ACT.Identity,
                                           scale=convT[:, layer, 2, bass.ds(tile, 1)], bias=convT[:, layer, 3, bass.ds(tile, 1)])
                        if t % 2:
                            a.then_inc(conv_act, 1)
                    act.wait_ge(conv_2, g * 4 + (4 * gbase + 2))
                    act.activation(conv[:, 0:4], conv[:, 0:4], ACT.Silu).then_inc(silu_c, 1)

                with act.Fori(0, 5) as p:
                    for g in range(2):
                        for j in range(GU):
                            hi(up_base + GU * g + j + LEAD, p * 16)
                        taps(p * 2 + g, 4 * g)
                for j in range(GU - LEAD):
                    hi(up_base + 10 * GU + j + LEAD)
                act.wait_ge(ffg_done, gbase + 2)
                for i in range(LEAD):
                    hi(down_base + i)
                    ring_hi(ffg, down_base, i, 4)
                taps(10, 0)
                act.wait_ge(ffg_done, gbase + 11)

                def down(i, k=0):
                    if down_base + i < U_END:
                        hi(down_base + i, k)
                    if i < 2 * DU:
                        ring_hi(ffg, down_base, i, 4, k, t0=2 * (i % DU))

                for g in range(2):
                    steps(act, 16, 4, lambda k, j: down(DU * g + LEAD + j, k))
                    for j in range(16 + LEAD, DU + LEAD):
                        down(DU * g + j)
                    squares(n_sum, g)

            ffn(0, 1, big[:, 2], SH_F0, U_UP0, U_DOWN0, 0, 2)

            root(2, 7)
            act.dma_start(fw_raw[:, :, :], kv_v[:, :, 2 * D:2 * D + HEADS]).then_inc(fw_loaded, 16)
            act.dma_start(fb[:, :], forget_b.rearrange("(h a) -> h a", a=1)).then_inc(fw_loaded, 16)
            norm_hi(big[:, 0], SH_KV, 2)
            act.wait_ge(fw_loaded, 32)
            act.activation(fw_hi[:, :, :], fw_raw[:, :, :], ACT.Copy).then_inc(fw_split, 1)
            plain_pair(U_K, copy_out(U_K, 2, lambda g: big[:, 0, 8 * g:8 * g + 8].rearrange("p (b t) s -> p b (t s)", b=4)))
            plain_pair(U_V, copy_out(U_V, 4, lambda g: v_nat[:, :, UC * g:UC * g + UC].rearrange("p t (b n) -> p t b n", b=2)))
            act.wait_ge(f_step, 1)
            act.activation(fc[0:HEADS, 1], fc[0:HEADS, 0], ACT.Abs).then_inc(f_act, 1)
            act.wait_ge(f_act, 1)
            act.activation(fc[0:HEADS, 1], fc[0:HEADS, 1], ACT.Exp, scale=-1.0).then_inc(f_act, 1)
            act.wait_ge(f_act, 2)
            act.activation(fc[0:HEADS, 1], fc[0:HEADS, 1], ACT.Ln, bias=1.0).then_inc(f_act, 1)

            norm_hi(big[:, 2], SH_M1, 3)
            plain_pair(U_Q, copy_out(U_Q, 6, lambda g: big[:, 2, 8 * g:8 * g + 8].rearrange("p (b t) s -> p b (t s)", b=4), P ** -0.5))

            def heads(i):
                for e in range(4):
                    act.wait_ge(a_max, i * 4 + (e + 1))
                    for tb, (lo_c, hi_c) in enumerate(((0, P), (P, 3 * P))):
                        a = act.activation(att[:, e, lo_c:hi_c], att[:, e, lo_c:hi_c], ACT.Exp, bias=stat[:, 0, e, tb:tb + 1],
                                           accum_out=stat[:, 1, e, tb:tb + 1])
                    a.then_inc(a_exp, 1)
                for e in range(4):
                    act.wait_ge(a_t, i * 4 + (e + 1))
                    ge(act, a_o, i * 4 + (e - 1))
                    act.activation(att_t[:, e % 2], psum[:, 4 + e % 2, 0:384], ACT.Copy).then_inc(a_tc, 1)
                    if e:
                        out_hi(i, e - 1)
                out_hi(i, 3)

            def out_hi(i, e):
                act.wait_ge(a_o, i * 4 + (e + 1))
                act.activation(h[:, 0, bass.ds(i * 4 + e, 1)], psum[:, 6 + e % 2, 0:S].unsqueeze(1), ACT.Copy).then_inc(a_ohi, 1)

            heads(0)
            with act.Fori(1, 4) as i:
                heads(i)
            plain_pair(U_AO, lambda g: squares(3, g))
            ffn(1, 4, big[:, 2], SH_F1, U_UP1, U_DOWN1, 11, 4)

            root(4, 7)
            for b in range(8):
                act.wait_ge(o_turned, b + 1)
                act.activation(out_nat[:, b // 4, 512 * (b % 4):512 * (b % 4 + 1)], psum[:, b % 4, :], ACT.Copy).then_inc(o_copied, 1)

        @block.vector
        def _(dve):
            def lo(st, dyn=0):
                dve.wait_ge(hi_done, dyn + (st + 1))
                dve.tensor_tensor(w_lo[:, st % NW], w_raw[:, st % NW], w_hi[:, st % NW].bitcast(F32),
                                  ALU.subtract).then_inc(lo_done, 1)

            def mod_add(s, kt, dyn=0, sdyn=0):
                st = KT * s + kt
                if s < 2:
                    n = st // 2
                    dve.wait_ge(first_full[n % NW], dyn * 2 + 16 * (n // NW + 1))
                    block = first[:, n % NW, kt % 2]
                else:
                    dve.wait_ge(m_full[st % NMOD], sdyn * 128 + dyn * 8 + 16 * ((st - FIRST) // NMOD + 1))
                    block = m_raw[:, st % NMOD]
                if isinstance(dyn, int) and kt == 0:
                    ge(dve, sum_ready, sdyn + s)
                    dve.tensor_scalar(mod_acc[:, :], block, cT[:, 0:1], None, ALU.mult).then_inc(mod_used, 1)
                    return
                dve.wait_ge(mod_used, sdyn * KT + dyn + st)
                dve.scalar_tensor_tensor(out=mod_acc[:, :], in0=block, scalar=cT[:, bass.ds(dyn + kt, 1)],
                                         in1=mod_acc[:, :], op0=ALU.mult, op1=ALU.add).then_inc(mod_used, 1)

            def mod_out(s, bank, sdyn=0):
                dve.wait_ge(sum_ready, sdyn + (s + 1))
                dve.tensor_tensor(modT[:, bass.ds(sdyn + s, 1)], psum[:, bank, 0:KT].unsqueeze(1),
                                  mod_bias[:, bass.ds(sdyn * KT + s * KT, KT)].unsqueeze(1), ALU.add).then_inc(mod_ready, 1)

            def pair(base, evac, s=None, more=False, dyn=0, sdyn=0, first=False, bank=0):
                if first:
                    for j in range(LEAD):
                        mod_add(s, j, 0, sdyn)
                for j in range(LEAD, 2 * GU):
                    lo(base + j, dyn)
                    if j == GU + LEAD - 1:
                        evac(0)
                    if s is not None:
                        mod_add(s, j, 0, sdyn)
                for j in range(LEAD):
                    lo(base + 2 * GU + j, dyn)
                    if j == 0 and s is not None:
                        mod_out(s, bank, sdyn)
                    if more:
                        mod_add(s + 1, j, 0, sdyn)
                evac(1)

            dve.wait_ge(turned_out, B_C + 1)
            mod_add(SH_M0, 0)
            mod_add(SH_M0, 1)

            RE, IM, DRE, DIM, MAG, TURN, SIN, COS, K1, K2, FR, FI = range(12)
            seen = [0]

            def pd(ins):
                ins.then_inc(prep_dve, 1)
                seen[0] += 1

            def pw():
                dve.wait_ge(prep_dve, seen[0])

            dve.wait_ge(ab_loaded, 48)
            dve.wait_ge(prep_act, 1)
            for src, dst in ((RE, DRE), (IM, DIM)):
                dve.tensor_scalar(prep[:, dst, 0:STATE], prep[:, src, 0:STATE], step[:, 0:1], None, ALU.mult)
                pd(dve.tensor_scalar(prep[:, dst, STATE:], prep[:, src, STATE:], step[:, 1:2], None, ALU.mult))
            mod_add(SH_M0, 2)
            pw()
            pd(dve.tensor_scalar(prep[:, K1, :], prep[:, DIM, :], 1.0 / (2 * PI), ROUND, ALU.mult, ALU.add))
            pw()
            pd(dve.tensor_scalar(prep[:, K1, :], prep[:, K1, :], ROUND, None, ALU.subtract))
            for part in (TWO_PI_1, TWO_PI_2, TWO_PI_3):
                pw()
                ins = dve.scalar_tensor_tensor(out=prep[:, DIM, :], in0=prep[:, K1, :], scalar=-part, in1=prep[:, DIM, :],
                                               op0=ALU.mult, op1=ALU.add)
                if part != TWO_PI_3:
                    pd(ins)
            ins.then_inc(prep_red, 1)
            dve.wait_ge(prep_red, 1)
            dve.tensor_scalar(prep[:, DIM, :], prep[:, DIM, :], 1.0 / (2 * PI), 0.5, ALU.mult, ALU.min).then_inc(prep_red, 1)
            dve.wait_ge(prep_red, 2)
            pd(dve.tensor_scalar(prep[:, TURN, :], prep[:, DIM, :], -0.5, None, ALU.max))
            mod_add(SH_M0, 3)
            dve.wait_ge(prep_act, 5)
            pd(dve.tensor_tensor(prep[:, K1, :], prep[:, MAG, :], prep[:, COS, :], ALU.mult))
            pd(dve.tensor_tensor(prep[:, K2, :], prep[:, MAG, :], prep[:, SIN, :], ALU.mult))
            pd(dve.tensor_tensor(prep[:, FR, :], prep[:, RE, :], prep[:, RE, :], ALU.mult))
            pd(dve.tensor_tensor(prep[:, FI, :], prep[:, IM, :], prep[:, IM, :], ALU.mult))
            pw()
            pd(dve.tensor_scalar(prep[:, K1, :], prep[:, K1, :], -1.0, None, ALU.add))
            pd(dve.tensor_tensor(prep[:, DRE, :], prep[:, FR, :], prep[:, FI, :], ALU.add))
            pw()
            pd(dve.reciprocal(prep[:, DRE, :], prep[:, DRE, :]))
            for dst, (a, b), (e, f), op in ((FR, (K1, RE), (K2, IM), ALU.add), (FI, (K2, RE), (K1, IM), ALU.subtract)):
                pd(dve.tensor_tensor(prep[:, dst, :], prep[:, a, :], prep[:, b, :], ALU.mult))
                pd(dve.tensor_tensor(prep[:, DIM, :], prep[:, e, :], prep[:, f, :], ALU.mult))
                pw()
                pd(dve.tensor_tensor(prep[:, dst, :], prep[:, dst, :], prep[:, DIM, :], op))
                pw()
                pd(dve.tensor_tensor(prep[:, dst, :], prep[:, dst, :], prep[:, DRE, :], ALU.mult))
            pw()
            assert seen[0] == PREP_DVE
            mod_add(SH_M0, 4)
            mod_add(SH_M0, 5)
            dve.wait_ge(turned_out, B_PRM + 1)
            dve.wait_ge(b_loaded, 32)
            dve.wait_ge(c_zero, 2)
            f_r, f_i = (prm[:, n, :].unsqueeze(2).to_broadcast([P, ST, GW]) for n in (2, 3))
            nb = 0
            for n, (a, b, op) in enumerate(((0, 1, ALU.subtract), (1, 0, ALU.add))):
                if n:
                    dve.wait_ge(bar_done, 4)
                dve.tensor_tensor(b_tmp[:, 0], b_raw[:, a], f_r, ALU.mult).then_inc(bar_done, 1)
                dve.tensor_tensor(b_tmp[:, 1], b_raw[:, b], f_i, ALU.mult).then_inc(bar_done, 1)
                dve.wait_ge(bar_done, 4 * n + 2)
                for g in range(2):
                    r = slice(STATE * g, STATE * (g + 1))
                    dve.tensor_tensor(b_bar[r, n, :, g, :], b_tmp[r, 0], b_tmp[r, 1], op).then_inc(bar_done, 1)
                mod_add(SH_M0, 6 + n)
            dve.wait_ge(consts, 5)
            dve.tensor_tensor_scan(out=iota[:, :], data0=iota[:, :], data1=iota[:, :], initial=0.0, op0=ALU.mult,
                                   op1=ALU.add).then_inc(iota_done, 1)
            for kt in range(KT // 2, KT):
                mod_add(SH_M0, kt)
            for kt in range(KT):
                mod_add(SC_M0, kt)
            mod_out(SH_M0, 0)
            mod_out(SC_M0, 1)

            def norm(n, buf, scale, shift, g, sums=None, free=None):
                if sums is not None:
                    i, bank = sums
                    dve.wait_ge(r_done, 2 * i + 1)
                    dve.reciprocal(rstd[:, :], rstd[:, :]).then_inc(r_done, 1)
                    dve.wait_ge(r_done, 2 * i + 2)
                if scale is None:
                    gain_of = lambda kt: gains[:, bass.ds(g * KT + kt, 1)]
                else:
                    dve.wait_ge(mod_ready, scale + 1)
                    dve.scalar_tensor_tensor(out=gs[:, :], in0=modT[:, scale], scalar=1.0, in1=gain(g), op0=ALU.add,
                                             op1=ALU.mult).then_inc(gs_done, 1)
                    dve.wait_ge(gs_done, n + 1)
                    gain_of = lambda kt: gs[:, bass.ds(kt, 1)]
                if free is not None:
                    dve.wait_ge(*free)

                def scale_x(k, j):
                    dve.scalar_tensor_tensor(out=buf[:, bass.ds(k + j, 1)], in0=xT[:, bass.ds(k + j, 1)], scalar=gain_of(k + j),
                                             in1=rstd[:, :].unsqueeze(1), op0=ALU.mult, op1=ALU.mult).then_inc(scaled, 1)

                def rest(k, j):
                    dve.wait_ge(xhi_done, k + (XN[n] + j + 1))
                    dve.scalar_tensor_tensor(out=h[:, 1, bass.ds(k + j, 1)], in0=buf[:, bass.ds(k + j, 1)],
                                             scalar=modT[:, shift, bass.ds(k + j, 1)], in1=h[:, 0, bass.ds(k + j, 1)].bitcast(F32),
                                             op0=ALU.add, op1=ALU.subtract).then_inc(xlo_done, 1)

                if scale is None:
                    steps(dve, KT, 4, scale_x)
                    return
                for j in range(2):
                    scale_x(0, j)
                with dve.Fori(0, KT // 2 - 1) as i:
                    for j in range(2):
                        scale_x(i * 2, j + 2)
                    for j in range(2):
                        rest(i * 2, j)
                for j in range(2):
                    rest(KT - 2, j)

            def ring_lo(src, i, count, slots, k=0, t0=None):
                dve.wait_ge(xhi_done, k + (count + i + 1))
                t = 2 * i if t0 is None else t0
                r = ring(slots, i)
                dve.tensor_tensor(h[:, 1, r], src[:, bass.ds(k * 2 + t, 2)], h[:, 0, r].bitcast(F32), ALU.subtract).then_inc(xlo_done, 1)

            def add_to_x(base, units, section, banks=(0, 4)):
                def f(g):
                    dve.wait_ge(w_used, base + units * (g + 1))
                    dve.wait_ge(mod_ready, section + 1)
                    for t in range(8):
                        ins = dve.scalar_tensor_tensor(out=xT[:, 8 * g + t], in0=psum[:, banks[g] + t // 2, S * (t % 2):S * (t % 2 + 1)],
                                                       scalar=modT[:, section, 8 * g + t:8 * g + t + 1], in1=xT[:, 8 * g + t],
                                                       op0=ALU.mult, op1=ALU.add)
                        ins.then_inc(x_out, 1)
                return f

            none = lambda g: None

            for j in range(LEAD):
                lo(U_IN + j)
            norm(0, big[:, 0], SC_M0, SH_M0, NM0, (0, 7))
            pair(U_IN, none, G_M0, True, first=True)

            def states(q):
                dve.wait_ge(s_bu, q + 1)
                dve.wait_ge(s_tab, q + 1)
                ge(dve, s_prod, 2 * (q - 1))
                b = q % 2
                cos, sin = (tab[:, q % NTAB, n] for n in range(2))
                r = [rot[:, b, n] for n in range(2)]
                t = [tmp[:, n] for n in range(2)]
                re, im = (psum[:, 0:2, S * n:S * (n + 1)] for n in range(2))
                ge(dve, s_rota, q)
                dve.tensor_tensor(r[0], re, cos, ALU.mult)
                dve.tensor_tensor(t[0], im, sin, ALU.mult)
                dve.tensor_tensor(r[1], im, cos, ALU.mult)
                dve.tensor_tensor(t[1], re, sin, ALU.mult).then_inc(s_rotm, 1)
                dve.wait_ge(s_rotm, q + 1)
                for n in range(2):
                    ins = dve.tensor_tensor(r[n], r[n], t[n], (ALU.add, ALU.subtract)[n])
                ins.then_inc(s_rota, 1)
                dve.wait_ge(s_rota, q + 1)
                for e in range(2):
                    decay = prm[:, 1, 2 * q + e:2 * q + e + 1].to_broadcast([P, S])
                    for n in range(2):
                        ins = dve.tensor_tensor_scan(out=rot[:, b, n, e], data0=decay, data1=rot[:, b, n, e], initial=0.0,
                                                     op0=ALU.mult, op1=ALU.add)
                ins.then_inc(s_z, 1)

            def skip(kt):
                dve.wait_ge(s_y, 4 * (kt + 1))
                ge(dve, s_g, kt // 2)
                dve.scalar_tensor_tensor(out=yb[:, kt % 2], in0=u_t[:, kt], scalar=gain(SKIP, kt),
                                         in1=psum[:, 2 + kt % 2, 0:S], op0=ALU.mult, op1=ALU.add).then_inc(s_du, 1)
                dve.wait_ge(s_du, kt + 1)
                dve.tensor_tensor(yb[:, kt % 2], yb[:, kt % 2], psum[:, 2 + kt % 2, S:2 * S], ALU.subtract).then_inc(s_yd, 1)

            dve.wait_ge(copied, 2)
            for q in range(S5_STEPS + 5):
                if q < S5_STEPS:
                    states(q)
                if q % 2 and (q - 3) // 2 in range(KT):
                    skip((q - 3) // 2)
                if q - 2 in S5_GELU:
                    ring_lo(u_t, S5_GELU[q - 2], XG, 2)
                if q - 2 in S5_UNIT:
                    lo(U_GLU + S5_UNIT[q - 2] + LEAD)
                    mod_add(SH_F0, S5_UNIT[q - 2] + LEAD)

            def sigmoid_gate(g):
                for b in range(2):
                    t = 8 * g + 4 * b
                    dve.wait_ge(s_sg, t + 4)
                    dve.tensor_tensor(big[:, 1, t:t + 4], big[:, 1, t:t + 4], big[:, 0, t:t + 4], ALU.mult).then_inc(s_zg, 1)
                for b in range(2):
                    t = 8 * g + 4 * b
                    dve.wait_ge(zhi_done, 2 * g + b + 1)
                    dve.tensor_tensor(h[:, 1, t:t + 4], big[:, 1, t:t + 4], h[:, 0, t:t + 4].bitcast(F32), ALU.subtract).then_inc(zlo_done, 1)

            for j in range(S5_UNITS + LEAD, 2 * GU + LEAD):
                lo(U_GLU + j)
                if j - 1 in range(GU, 2 * GU):
                    ring_lo(u_t, j - 1, XG, 2, t0=2 * ((j - 1) % GU))
                if j == 2 * GU:
                    mod_out(SH_F0, 4)
                if j == GU + LEAD - 1:
                    sigmoid_gate(0)
                mod_add(SH_F0 + j // (2 * GU), j % (2 * GU))
            sigmoid_gate(1)
            pair(U_OUT, add_to_x(U_OUT, GU, G_M0, (4, 0)), SC_F0, True, bank=4)

            def ffn(layer, n, sq, scale, shift, gate_s, sums, up_base, down_base, gbase, count, sections):
                norm(n, sq, scale, shift, NF0 + layer, sums)

                def taps(g, bank):
                    for b in range(4):
                        dve.wait_ge(conv_act, g * 4 + (4 * gbase + b + 1))
                        for lag, tap, done in ((1, 1, conv_1), (2, 0, conv_2)):
                            if lag == 2:
                                dve.wait_ge(conv_1, g * 4 + (4 * gbase + b + 1))
                            for t in (2 * b, 2 * b + 1):
                                tile = g * 4 + (t if t < 4 else t - 4 + FT)
                                c0 = S * (t % 2)
                                ins = dve.scalar_tensor_tensor(
                                    out=conv[:, t, lag:], in0=psum[:, bank + b, c0:c0 + S - lag],
                                    scalar=convT[:, layer, tap, bass.ds(tile, 1)], in1=conv[:, t, lag:], op0=ALU.mult, op1=ALU.add)
                            ins.then_inc(done, 1)

                def up(p, p0=0, s=None, more=False):
                    pair(up_base + 16 * p0, lambda g: taps(p * 2 + (2 * p0 + g), 4 * g), s, more, p * 16, p)

                if layer == 0:
                    with dve.Fori(0, 2) as p:
                        up(p, 0, G_F0, True)
                    up(0, 2, G_F0 + 2)
                    with dve.Fori(0, 2) as p:
                        up(p, 3)
                else:
                    with dve.Fori(0, 5) as p:
                        up(p)
                for j in range(LEAD, GU):
                    lo(up_base + 10 * GU + j)
                for i in range(LEAD):
                    lo(down_base + i)
                    ring_lo(ffg, i, count, 4)
                taps(10, 0)
                out = add_to_x(down_base, DU, gate_s, (4, 0))
                for g in range(2):
                    s = sections[g]
                    more = layer == 0

                    def down(i, k=0, block=None):
                        if down_base + i < U_END:
                            lo(down_base + i, k)
                        if i < 2 * DU:
                            ring_lo(ffg, i, count, 4, k, t0=2 * (i % DU))
                        if block is not None:
                            mod_add(s, block, k)

                    if s is None:
                        steps(dve, 16, 4, lambda k, j: down(DU * g + LEAD + j, k))
                    else:
                        if g == 0:
                            for j in range(LEAD):
                                mod_add(s, j)
                        steps(dve, 12, 4, lambda k, j: down(DU * g + LEAD + j, k, LEAD + j))
                        for j in range(12 + LEAD, 16 + LEAD):
                            down(DU * g + j, 0, j if j < KT else None)
                    for j in range(16 + LEAD, DU + LEAD):
                        down(DU * g + j)
                        if j == DU and s is not None:
                            mod_out(s, BANK_DOWN[g])
                        if j >= DU and more:
                            mod_add(s + 1, j - DU)
                    out(g)

            ffn(0, 1, big[:, 2], SC_F0, SH_F0, G_F0, (1, 3), U_UP0, U_DOWN0, 0, XD0, (SH_M1, SC_M1))

            norm(2, big[:, 0], SC_KV, SH_KV, NKV, (2, 7))
            dve.wait_ge(fw_split, 1)
            dve.tensor_tensor(fw_lo[:, :, :], fw_raw[:, :, :], fw_hi[:, :, :].bitcast(F32), ALU.subtract).then_inc(fw_split, 1)
            pair(U_K, none, G_M1, True)
            pair(U_V, none, SH_F1, True)
            dve.wait_ge(f_sum, 1)
            dve.tensor_copy(f_nat[:, :, :], psum[:, 0, 0:TB * HEADS].rearrange("p (t n) -> p t n", t=TB)).then_inc(f_evac, 1)
            dve.wait_ge(f_turn, 1)
            dve.wait_ge(fc_zero, 1)
            dve.tensor_scalar(fc[0:HEADS, 0], psum[0:HEADS, 1, 0:S], fb[:, :], None, ALU.add).then_inc(f_step, 1)
            dve.wait_ge(f_act, 3)
            dve.tensor_scalar(fc[0:HEADS, 0], fc[0:HEADS, 0], 0.0, None, ALU.min).then_inc(f_step, 1)
            dve.memset(fc[0:HEADS, 2], 1.0).then_inc(f_step, 1)
            dve.wait_ge(f_step, 3)
            dve.tensor_tensor(fc[0:HEADS, 0], fc[0:HEADS, 0], fc[0:HEADS, 1], ALU.subtract).then_inc(f_step, 1)
            dve.wait_ge(f_step, 4)
            dve.tensor_tensor_scan(out=fc[0:HEADS, 3], data0=fc[0:HEADS, 2], data1=fc[0:HEADS, 0], initial=0.0, op0=ALU.mult,
                                   op1=ALU.add).then_inc(f_step, 1)
            dve.wait_ge(f_step, 5)
            dve.tensor_scalar(fc[0:HEADS, 1], fc[0:HEADS, 3], -1.0, None, ALU.mult).then_inc(f_cum, 1)

            norm(3, big[:, 2], SC_M1, SH_M1, NM1, None, (w_used, U_Q))
            pair(U_Q, none, SC_F1)

            def heads(i):
                for e in range(4):
                    dve.wait_ge(a_s, i * 4 + (e + 1))
                    ge(dve, a_t, i * 4 + (e - 3))
                    dve.tensor_tensor(att[:, e], psum[:, e, 0:384], mask[:, :], ALU.add).then_inc(a_masked, 1)
                    dve.wait_ge(a_masked, i * 4 + (e + 1))
                    for tb, (c0, c1) in enumerate(((0, P), (P, 3 * P))):
                        ins = dve.tensor_reduce(stat[:, 0, e, tb:tb + 1], att[:, e, c0:c1], AX_X, ALU.max, negate=True)
                    ins.then_inc(a_max, 1)
                for e in range(4):
                    dve.wait_ge(a_exp, i * 4 + (e + 1))
                    dve.reciprocal(stat[:, 2, e, :], stat[:, 1, e, :]).then_inc(a_rec, 1)
                    dve.wait_ge(a_rec, i * 4 + (e + 1))
                    for tb, (c0, c1) in enumerate(((0, P), (P, 3 * P))):
                        ins = dve.tensor_scalar(att[:, e, c0:c1], att[:, e, c0:c1], stat[:, 2, e, tb:tb + 1], None, ALU.mult)
                    ins.then_inc(a_p, 1)
                for e in range(4):
                    dve.wait_ge(a_ohi, i * 4 + (e + 1))
                    hd = bass.ds(i * 4 + e, 1)
                    dve.tensor_tensor(h[:, 1, hd], psum[:, 6 + e % 2, 0:S].unsqueeze(1), h[:, 0, hd].bitcast(F32),
                                      ALU.subtract).then_inc(a_olo, 1)

            dve.wait_ge(mask_done, 3)
            heads(0)
            with dve.Fori(1, 4) as i:
                heads(i)
            pair(U_AO, add_to_x(U_AO, GU, G_M1))
            ffn(1, 4, big[:, 2], SC_F1, SH_F1, G_F1, (3, 3), U_UP1, U_DOWN1, 11, XD1, (G_F1, None))

            norm(5, big[:, 0], None, None, NFIN, (4, 7))

        @block.tensor
        def _(pe):
            mm = lambda out, a, b, start=False: pe.matmul(out, a, b, start=start, stop=False, skip_group_check=True)

            def turn(b, blocks, ready=None):
                if ready is not None:
                    pe.wait_ge(*ready)
                ge(pe, turned_out, b - 7)
                c0 = 0
                for src in blocks:
                    n = src.shape[0]
                    ins = pe.transpose(psum[0:src.shape[1], b % 8, c0:c0 + n], src, ident[0:n, 0:n])
                    c0 += n
                ins.then_inc(turned, 1)

            def mod_sum(s, bank, sdyn=0):
                pe.wait_ge(mod_used, sdyn * KT + KT * (s + 1))
                for kt in range(KT):
                    ins = mm(psum[:, bank, kt:kt + 1], mod_acc[:, P * kt:P * (kt + 1)], ones[:, 0:1], kt == 0)
                ins.then_inc(sum_ready, 1)

            pe.wait_ge(consts, 3)
            turn(B_C, [nat[0:KT, 0, :]], (silu_done, 1))
            turn(B_BIAS, [nat[0:96, 1, :], nat[0:32, 2, :], nat[0:96, 3, :]], (rest_loaded, 16 * 17))
            turn(B_GAIN, [nat[:, 4, :]])
            for i in range(2):
                turn(B_CONV + i, [nat[0:88, 5 + 4 * i + k, :] for k in range(4)])
            for b in range(8):
                turn(B_X + b, [x_nat[:, tb, P * kt:P * (kt + 1)] for kt in (2 * b, 2 * b + 1) for tb in range(TB)], (x_loaded, 32))
            turn(B_PRM, [prep[:, n, :] for n in (5, 4, 10, 11)], (prep_dve, PREP_DVE))
            for n in range(2):
                for b in range(4):
                    turn(B_CT + 4 * n + b, [c_nat[:, n, 4 * b + i, :] for i in range(4)], (c_loaded, 256))
            for n in range(2):
                for b in range(4):
                    turn(B_BT + 4 * n + b, [b_bar[:, n, 16 * b + 4 * i:16 * b + 4 * i + 4].rearrange("p j g h -> p (j g h)")
                                            for i in range(4)], (bar_done, 4 * n + 4))
            pe.wait_ge(turned_out, N_BATCH)
            mod_sum(SH_M0, 0)
            mod_sum(SC_M0, 1)

            def sums(i, g, buf, bank):
                for kt in range(8):
                    if kt % 2 == 0:
                        pe.wait_ge(sq_done, 8 * i + 4 * g + kt // 2 + 1)
                    ins = mm(psum[:, bank, 0:S], ones[:, :], buf[:, kt], g == 0 and kt == 0)
                ins.then_inc(ss_done if g else ss_half, 1)

            def unit(st, dyn, bank, xt, x_ready, first=False, blocks=range(UK)):
                if 0 in blocks:
                    pe.wait_ge(lo_done, dyn + (st + 1))
                    for sem_, value in x_ready:
                        pe.wait_ge(sem_, value)
                sl = st % NW
                for k in blocks:
                    x_hi, x_lo = xt(k)
                    for t in range(8):
                        c0 = k * UC + P * t
                        wh, wl = w_hi[:, sl, c0:c0 + P], w_lo[:, sl, c0:c0 + P]
                        acc = psum[:, bank + t // 2, S * (t % 2):S * (t % 2 + 1)]
                        mm(acc, wh, x_hi, first and k == 0 and t % 2 == 0)
                        mm(acc, wh, x_lo)
                        ins = mm(acc, wl, x_hi)
                if UK - 1 in blocks:
                    ins.then_inc(w_used, 1)

            def group(base, n, bank, xt, ready, dyn=0, before={}):
                def one(k, j, first=False):
                    unit(base + j, dyn + k, bank, lambda r: xt(k, j, r), ready(k, j), first)

                def straight(units):
                    for j in units:
                        if j in before:
                            before[j]()
                        one(0, j, j == 0)

                if n < 3 * NW:
                    straight(range(n))
                    return
                straight(range(NW))
                if NW in before:
                    before[NW]()
                with pe.Fori(0, n // NW - 1) as i:
                    for j in range(NW):
                        one(i * NW, NW + j)
                straight(range(n // NW * NW, n))

            def h_group(base, bank, dyn=0, made=None, before={}):
                group(base, GU, bank, lambda k, j, r: [flat(h[:, n, bass.ds(k * UK + (j * UK + r), 1)]) for n in range(2)],
                      lambda k, j: [(made[0], k * UK + (made[1] + UK * (j + 1)))] if made else [], dyn, before)

            def h_pair(base, made=None, banks=(0, 4), s=None, dyn=0, sdyn=0, before={}):
                h_group(base, banks[0], dyn, made)
                h_group(base + GU, banks[1], dyn,
                        before={**before, **({} if s is None else {GU - 1: lambda: mod_sum(s, banks[0], sdyn)})})
                if s is not None:
                    pe.wait_ge(mod_ready, sdyn + (s + 1))

            def ring_group(stage, first_unit, n, bank, count, slots, before={}):
                def tiles(k, j, r):
                    t = ring(slots, first_unit + j).start + r
                    return h[:, 0, t], h[:, 1, t]
                group(stage + first_unit, n, bank, tiles, lambda k, j: [(xlo_done, k + (count + first_unit + j + 1))], before=before)

            for g in range(2):
                sums(0, g, big[:, 0, 8 * g:8 * g + 8], 7)
            pe.wait_ge(mod_ready, 2)
            h_pair(U_IN, (xlo_done, XN[0]), s=G_M0)

            def inputs(q):
                ge(pe, s_rotm, q)
                for part in range(2):
                    for e in range(2):
                        r = slice(32 * (2 * (q % 2) + e), 32 * (2 * (q % 2) + e) + 32)
                        ins = mm(psum[:, e, S * part:S * (part + 1)], b_t[r, part, q // 2], u_t[r, q // 2], part == 0)
                ins.then_inc(s_bu, 1)

            def outputs(q):
                if q % 2 == 0:
                    ge(pe, s_yd, q // 2 - 1)
                for half in range(2):
                    pe.wait_ge(s_prod, 2 * q + half + 1)
                    for e in range(2):
                        r = slice(32 * (2 * (q % 2) + e), 32 * (2 * (q % 2) + e) + 32)
                        for i in range(2):
                            n = min(half + i, 1)
                            ins = mm(psum[r, 2 + q // 2 % 2, S * n:S * (n + 1)], c_t[:, half, q // 2, r], prod[:, 2 * half + i, e], half == 0 and i == 0)
                    ins.then_inc(s_y, 1)

            def glu_unit(i, blocks=range(UK)):
                t = ring(2, i).start
                unit(U_GLU + i, 0, 4, lambda k: (h[:, 0, t + k], h[:, 1, t + k]), [(xlo_done, XG + i + 1)], i == 0, blocks)

            pe.wait_ge(copied, 2)
            inputs(0)
            inputs(1)
            for q in range(S5_STEPS):
                if q + 2 < S5_STEPS:
                    inputs(q + 2)
                outputs(q)
                for k in range(UK):
                    if q - k - 1 in S5_UNIT:
                        glu_unit(S5_UNIT[q - k - 1], [k])
            for i in range(S5_UNITS, GU):
                glu_unit(i)
            ring_group(U_GLU, GU, GU, 0, XG, 2, {GU - 1: lambda: mod_sum(SH_F0, 4)})
            pe.wait_ge(mod_ready, SH_F0 + 1)
            pe.wait_ge(zlo_done, 4)
            h_pair(U_OUT, banks=(4, 0), s=SC_F0, before={NW: lambda: sums(1, 0, sqb, 7)})
            sums(1, 1, sqb, 7)

            def ffn(n_sum, up_base, down_base, x0, count, sections):
                pe.wait_ge(xlo_done, x0 + KT)
                if sections[1] is not None:
                    with pe.Fori(0, 3) as p:
                        h_pair(up_base, s=G_F0, dyn=p * 16, sdyn=p)
                with pe.Fori(0, 5 if sections[1] is None else 2) as p:
                    h_pair(up_base + (0 if sections[1] is None else 48), dyn=p * 16)
                h_group(up_base + 10 * GU, 0)
                for g in range(2):
                    before = {NW: lambda: sums(n_sum, 0, sqb, 7)} if g else {}
                    if sections[g] is not None:
                        before[DU // NW * NW] = lambda: mod_sum(sections[g], BANK_DOWN[g])
                    ring_group(down_base, DU * g, DU, 4 * (1 - g), count, 4, before)
                    if sections[g] is not None:
                        pe.wait_ge(mod_ready, sections[g] + 1)
                sums(n_sum, 1, sqb, 7)

            ffn(2, U_UP0, U_DOWN0, XN[1], XD0, (SH_M1, SC_M1))

            h_pair(U_K, (xlo_done, XN[2]), s=G_M1)

            def v_unit(st, bank, kt, first=False):
                pe.wait_ge(lo_done, st + 1)
                sl = st % NW
                for k in range(UK):
                    for tb in range(TB):
                        x_hi, x_lo = (h[:, n, kt + k, P * tb:P * (tb + 1)] for n in range(2))
                        acc = [psum[:, bank + 2 * tb + e] for e in range(2)]
                        wh, wl = ([w[:, sl, k * UC + 512 * e:k * UC + 512 * (e + 1)] for e in range(2)] for w in (w_hi, w_lo))
                        for e in range(2):
                            mm(acc[e], x_hi, wh[e], first and k == 0)
                        for e in range(2):
                            mm(acc[e], x_hi, wl[e])
                        for e in range(2):
                            ins = mm(acc[e], x_lo, wh[e])
                ins.then_inc(w_used, 1)

            for g in range(2):
                for j in range(GU):
                    if g and j == GU - 1:
                        mod_sum(SH_F1, 0)
                    v_unit(U_V + GU * g + j, 4 * g, UK * j, j == 0)
            pe.wait_ge(mod_ready, SH_F1 + 1)
            pe.wait_ge(fw_split, 2)
            for tb in range(TB):
                for kt in range(KT):
                    x_hi, x_lo = (h[:, n, kt, P * tb:P * (tb + 1)] for n in range(2))
                    acc = psum[:, 0, HEADS * tb:HEADS * (tb + 1)]
                    mm(acc, x_hi, fw_hi[:, kt], kt == 0 and tb == 0)
                    mm(acc, x_hi, fw_lo[:, kt])
                    ins = mm(acc, x_lo, fw_hi[:, kt])
            ins.then_inc(f_sum, 1)
            pe.wait_ge(f_evac, 1)
            for tb in range(TB):
                ins = pe.transpose(psum[0:HEADS, 1, P * tb:P * (tb + 1)], f_nat[:, tb, :], ident[:, :])
            ins.then_inc(f_turn, 1)

            h_pair(U_Q, (xlo_done, XN[3]), s=SC_F1)

            def heads(i):
                for e in range(4):
                    q_h, k_h = (flat(big[:, n, bass.ds(i * 4 + e, 1)]) for n in (2, 0))
                    own = flat(sel[:, bass.ds(i * 4 + e, 1)])
                    ge(pe, a_masked, i * 4 + (e - 3))
                    sc = psum[:, e]
                    mm(sc[:, 0:P], q_h[:, 0:P], k_h[:, 0:P], True)
                    mm(sc[:, P:3 * P], q_h[:, P:S], k_h)
                    mm(sc[:, 0:P], fc[:, 3, 0:P], own)
                    for b in range(TB):
                        mm(sc[:, P * (b + 1):P * (b + 2)], fc[:, 3, P:S], own)
                    mm(sc[:, 0:P], own, fc[:, 1, 0:P])
                    mm(sc[:, P:3 * P], own, fc[:, 1, :]).then_inc(a_s, 1)

                def turn_p(e):
                    pe.wait_ge(a_p, i * 4 + (e + 1))
                    ge(pe, a_tc, i * 4 + (e - 1))
                    for b in range(3):
                        ins = pe.transpose(psum[:, 4 + e % 2, P * b:P * (b + 1)], att[:, e, P * b:P * (b + 1)], ident[:, :])
                    ins.then_inc(a_t, 1)

                def values(e):
                    pe.wait_ge(a_tc, i * 4 + (e + 1))
                    ge(pe, a_olo, i * 4 + (e - 1))
                    v_h = [v_nat[:, tb, 512 * i + P * e:512 * i + P * (e + 1)] for tb in range(TB)]
                    mm(psum[:, 6 + e % 2, 0:S], v_h[0], att_t[:, e % 2, 0:S], True)
                    mm(psum[:, 6 + e % 2, P:S], v_h[1], att_t[:, e % 2, S:3 * P]).then_inc(a_o, 1)

                turn_p(0)
                for e in range(1, 4):
                    turn_p(e)
                    values(e - 1)
                values(3)

            pe.wait_ge(copied, 8)
            pe.wait_ge(sel_done, 2)
            pe.wait_ge(f_cum, 1)
            for i in range(4):
                heads(i)
            h_pair(U_AO, (a_olo, 0), before={NW: lambda: sums(3, 0, sqb, 3)})
            sums(3, 1, sqb, 3)
            ffn(4, U_UP1, U_DOWN1, XN[4], XD1, (G_F1, None))

            pe.wait_ge(scaled, 6 * KT)
            for b in range(8):
                ge(pe, o_copied, b - 3)
                for j in range(4):
                    ins = pe.transpose(psum[:, b % 4, P * j:P * (j + 1)], big[:, 0, 4 * (b % 4) + j, P * (b // 4):P * (b // 4 + 1)],
                                       ident[:, :])
                ins.then_inc(o_turned, 1)


_INS = ['x', 'c', 'mod_w', 'mod_b', 'norm_mix_g', 'norm_ffn_g', 'ssm_w_in', 'ssm_log_step', 'ssm_a_re', 'ssm_a_im',
        'ssm_b_re', 'ssm_b_im', 'ssm_c_re', 'ssm_c_im', 'ssm_d', 'ssm_glu_w', 'ssm_glu_b', 'ssm_w_out', 'kv_mod_w',
        'kv_mod_b', 'kv_norm_g', 'kv_w', 'forget_b', 'attn_w_q', 'attn_w_out', 'ffn_w_up', 'ffn_conv_w', 'ffn_conv_b',
        'ffn_w_down', 'final_norm_g']


def kernel(**inputs):
    import numpy as _np
    import concourse.bacc as _bacc
    from concourse import mybir as _mybir
    from concourse.bass_utils import run_bass_kernel_spmd as _run

    nc = _bacc.Bacc("TRN2", target_bir_lowering=False, num_devices=1)
    arrays, args = {}, []
    for name in _INS:
        a = _np.ascontiguousarray(inputs[name])
        arrays[f"in_{name}_dram"] = a
        args.append(nc.dram_tensor(f"in_{name}_dram", a.shape, _mybir.dt.from_np(a.dtype), kind="ExternalInput").ap())
    args.append(nc.dram_tensor("out_0_dram", (1, S, D), _mybir.dt.float32, kind="ExternalOutput").ap())
    trunk(nc, *args)
    r = _run(nc, [arrays], core_ids=[0])
    return r.results[0]["out_0_dram"]
```

```python
from contextlib import ExitStack

import concourse.bass as bass
from concourse import mybir

F32 = mybir.dt.float32
F32R = mybir.dt.float32r
ALU = mybir.AluOpType
ACT = mybir.ActivationFunctionType
AX_X = mybir.AxisListType.X

P = 128
D = 2048
S = 256
KT = D // P
TB = S // P
FF = 11 * D // 4
FT = FF // P
HEADS = 16
GROUPS, STATE, GW = 128, 64, 16
ST = GROUPS * STATE // P
EPS = 1e-6
PI = 3.141592653589793
TWO_PI_DOWN = 6.2831850
ROUND = 12582912.0
TWO_PI_1 = 6.28125
TWO_PI_2 = 0.0019340515136718750
TWO_PI_3 = 2 * PI - TWO_PI_1 - TWO_PI_2
MASKED = -1.0e30

NW, NMOD, LEAD = 4, 2, 3
UK = 2
UC = 1024
WF = UK * UC
GU = KT // UK
DU = FT // UK

SH_M0, SC_M0, G_M0, SH_F0, SC_F0, G_F0, SH_KV, SC_KV, SH_M1, SC_M1, G_M1, SH_F1, SC_F1, G_F1 = range(14)

U_IN = 0
U_GLU = U_IN + 2 * GU
U_OUT = U_GLU + 2 * GU
U_UP0 = U_OUT + 2 * GU
U_DOWN0 = U_UP0 + 11 * GU
U_K = U_DOWN0 + 2 * DU
U_V = U_K + 2 * GU
U_Q = U_V + 2 * GU
U_AO = U_Q + 2 * GU
U_UP1 = U_AO + 2 * GU
U_DOWN1 = U_UP1 + 11 * GU
U_END = U_DOWN1 + 2 * DU

XG = KT
XD0 = XG + 2 * GU + KT
XD1 = XD0 + 2 * DU + 3 * KT
XN = (0, XG + 2 * GU, XD0 + 2 * DU, XD0 + 2 * DU + KT, XD0 + 2 * DU + 2 * KT)
BANK_DOWN = (0, 4)
S5_STEPS = ST // 2
NTAB = 3
S5_UNITS = 6
S5_UNIT = {4 * i + 8: i for i in range(S5_UNITS)}
S5_GELU = {4 * m + 6: m for m in range(8)}
PREP_DVE = 22
FIRST = 2 * KT


def block_of(j):
    return None if j % 4 == 3 or j > 20 else 3 * (j // 4) + j % 4


def flat(ap):
    return ap.rearrange("p a n -> p (a n)")


def ge(eng, sem, value):
    if not (isinstance(value, int) and value <= 0):
        eng.wait_ge(sem, value)


def ring(slots, i):
    t = (12 if slots == 2 else 0) + 2 * (i % slots)
    return slice(t, t + 2)


def steps(eng, n, step, emit):
    with eng.Fori(0, n // step) as i:
        for j in range(step):
            emit(i * step, j)


def trunk(nc, x, c, mod_w, mod_b, norm_mix_g, norm_ffn_g, ssm_w_in, ssm_log_step, ssm_a_re, ssm_a_im,
          ssm_b_re, ssm_b_im, ssm_c_re, ssm_c_im, ssm_d, ssm_glu_w, ssm_glu_b, ssm_w_out, kv_mod_w,
          kv_mod_b, kv_norm_g, kv_w, forget_b, attn_w_q, attn_w_out, ffn_w_up, ffn_conv_w, ffn_conv_b,
          ffn_w_down, final_norm_g, out):
    ctx = ExitStack()
    with ctx:
        top = [16512]

        def sb(name, shape, dt=F32, at=None):
            n = 2 if dt == mybir.dt.bfloat16 else 4
            for d in shape[1:]:
                n *= d
            if at is None:
                at = top[0]
                top[0] += (n + 31) // 32 * 32
            return nc.alloc_sbuf_tensor_at(name, shape, dt, offset=at)

        def sem(name):
            return ctx.enter_context(nc.semaphore(name))

        raw_at = top[0]
        w_raw = sb("w_raw", [P, NW, WF])
        w_lo = sb("w_lo", [P, NW, WF], F32R, at=raw_at)
        w_hi = sb("w_hi", [P, NW, WF], F32R)
        first = sb("first", [P, NW, 2, D], at=raw_at)
        m_raw = sb("m_raw", [P, NMOD, D])
        xT = sb("xT", [P, KT, S])
        h_at = top[0]
        h = sb("h", [P, 2, KT, S], F32R)
        big_at = top[0]
        big = sb("big", [P, 3, KT, S])
        acc_at = top[0]
        mod_acc = sb("mod_acc", [P, D])
        ones = sb("ones", [P, P])
        ident = sb("ident", [P, P])
        mod_bias = sb("mod_bias", [P, 14 * KT])
        modT = sb("modT", [P, 14, KT])
        gains = sb("gains", [P, 8 * KT])
        convT = sb("convT", [P, 2, 4, 88])
        rstd = sb("rstd", [P, S])
        gs = sb("gs", [P, KT])
        cT = sb("cT", [P, KT])
        half_pi = sb("half_pi", [P, 1])
        eps = sb("eps", [P, 1])
        round_c = sb("round_c", [P, 2])
        scr_at = top[0]
        assert scr_at + 16 * 1024 <= 229344, scr_at
        scr = sb("scr", [P, 4096])

        NM0, NM1, NF0, NF1, NKV, NFIN, GLUB, SKIP = range(8)

        def gain(n, kt=None):
            return gains[:, n * KT:(n + 1) * KT] if kt is None else gains[:, n * KT + kt:n * KT + kt + 1]

        u_t = big[:, 0]
        b_t = sb("b_t", [P, 2, KT, P], at=big_at + 16384)
        c_t = sb("c_t", [P, 2, KT, P], at=big_at + 32768)
        v_nat = sb("v_nat", [P, TB, D], at=big_at + 16384)
        ffg = sb("ffg", [P, 48, S], at=big_at)
        x_nat = sb("x_nat", [P, TB, D], at=big_at + 16384)
        out_nat = sb("out_nat", [P, TB, D], at=big_at + 16384)
        c_nat = sb("c_nat", [P, 2, KT, P], at=big_at)
        b_raw = sb("b_raw", [P, 2, ST, GW], at=h_at)
        b_tmp = sb("b_tmp", [P, 2, ST, GW], at=h_at + 8192)
        b_bar = sb("b_bar", [P, 2, ST, 2, GW], at=h_at + 16384)
        nat = sb("nat", [P, 16, P], at=scr_at)
        prep = sb("prep", [64, 14, P], at=scr_at + 8192)
        step = sb("step", [64, 2], at=scr_at + 8192 + 14 * 512)
        tab = sb("tab", [P, NTAB, 2, 2, S], at=h_at)
        rot = sb("rot", [P, 2, 2, 2, S], at=h_at + 16384)
        tmp = sb("tmp", [P, 2, 2, S], at=h_at + 16384 + 8192)
        prod = sb("prod", [P, 4, 2, S], at=scr_at)
        yb = sb("yb", [P, 2, S], at=scr_at + 8192)
        arg = sb("arg", [P, 2, 2, S], at=scr_at + 10240)
        prm = sb("prm", [P, 4, ST], at=scr_at + 14336)
        iota = sb("iota", [P, S], at=scr_at + 15360)
        sqb = sb("sqb", [P, 8, S], at=scr_at + 8192)
        conv = sb("conv", [P, 8, S], at=scr_at)
        sel = sb("sel", [P, HEADS, P], at=acc_at)
        mask = sb("mask", [P, 384], at=scr_at)
        fc = sb("fc", [P, 4, S], at=scr_at + 1536)
        fw_raw = sb("fw_raw", [P, KT * HEADS], at=scr_at + 5632)
        fw = sb("fw", [P, 2 * KT * HEADS + P], F32R, at=scr_at + 6656)
        att = sb("att", [P, 4, 384], at=scr_at + 5632)
        att_t = sb("att_t", [P, 2, 384], at=scr_at + 5632 + 6144)
        stat = sb("stat", [P, 3, 4, TB], at=scr_at + 5632 + 6144 + 3072)
        fq = sb("fq", [P, TB, HEADS], at=scr_at + 5632 + 6144 + 3072 + 128)
        fb = sb("fb", [HEADS, 1], at=scr_at + 5632 + 6144 + 3072 + 96)

        psum = ctx.enter_context(nc.psum_tensor("psum_all", [P, 8, 512], F32))

        w_full = [sem(f"w_full{i}") for i in range(NW)]
        m_full = [sem(f"m_full{i}") for i in range(NMOD)]
        hi_done, lo_done, w_used = sem("hi_done"), sem("lo_done"), sem("w_used")
        mod_used, sum_ready, mod_ready = sem("mod_used"), sem("sum_ready"), sem("mod_ready")
        x_loaded, nat_loaded, ab_loaded, fw_loaded = (
            sem("x_loaded"), sem("nat_loaded"), sem("ab_loaded"), sem("fw_loaded"))
        consts, silu_done, rest_loaded, b_loaded, c_loaded = (
            sem("consts"), sem("silu_done"), sem("rest_loaded"), sem("b_loaded"), sem("c_loaded"))
        prep_red, gs_done, fc_zero, iota_done, zhi_done, zlo_done, x_out, copied, f_act = (
            sem("prep_red"), sem("gs_done"), sem("fc_zero"), sem("iota_done"), sem("zhi_done"), sem("zlo_done"), sem("x_out"), sem("copied"), sem("f_act"))
        turned, turned_out = sem("turned"), sem("turned_out")
        prep_act, prep_dve, bar_done = sem("prep_act"), sem("prep_dve"), sem("bar_done")
        c_zero = sem("c_zero")
        sq_done, ss_done, r_done, scaled, xhi_done, xlo_done = (
            sem("sq_done"), sem("ss_done"), sem("r_done"), sem("scaled"), sem("xhi_done"), sem("xlo_done"))
        ss_half = sem("ss_half")
        first_full = [sem(f"first_full{i}") for i in range(NW)]
        s_v, s_t, s_r, s_abs, s_tab, s_bu = (sem(n) for n in ("s_v", "s_t", "s_r", "s_abs", "s_tab", "s_bu"))
        s_rotm, s_rota, s_z, s_prod, s_y, s_yd, s_g = (
            sem(n) for n in ("s_rotm", "s_rota", "s_z", "s_prod", "s_y", "s_yd", "s_g"))
        s_rnd, s_du = sem("s_rnd"), sem("s_du")
        s_sg, s_zg = sem("s_sg"), sem("s_zg")
        conv_act, conv_1, conv_2, silu_c, conv_free = (
            sem("conv_act"), sem("conv_1"), sem("conv_2"), sem("silu_c"), sem("conv_free"))
        fw_split, f_sum, f_step, f_cum, f_turn, f_query, sel_done, mask_done = (
            sem(n) for n in ("fw_split", "f_sum", "f_step", "f_cum", "f_turn", "f_query", "sel_done", "mask_done"))
        a_s, a_masked, a_max, a_exp, a_rec, a_p, a_t, a_tc, a_o, a_ohi, a_olo = (
            sem(f"a_{n}") for n in ("s", "masked", "max", "exp", "rec", "p", "t", "tc", "o", "ohi", "olo"))
        o_turned, o_copied, stored = sem("o_turned"), sem("o_copied"), sem("stored")

        block = ctx.enter_context(nc.Block())

        def rows(w):
            return w.rearrange("(t p) n -> p t n", p=P)

        w_in_v, glu_v, w_out_v = rows(ssm_w_in[0]), rows(ssm_glu_w[0]), rows(ssm_w_out[0])
        kv_v, q_v, ao_v = rows(kv_w), rows(attn_w_q[0]), rows(attn_w_out[0])
        up_v = [ffn_w_up[i].rearrange("(t p) (a n) -> p t a n", p=P, a=2) for i in range(2)]
        down_v = [rows(ffn_w_down[i]) for i in range(2)]
        mod_v = [rows(mod_w[0]), rows(kv_mod_w), rows(mod_w[1])]

        def mod_section(s):
            return (0, s) if s < SH_KV else (1, s - SH_KV) if s < SH_M1 else (2, s - SH_M1)

        @block.sync
        def _(sp):
            def load_w(src, st, dyn=0):
                if st < NW:
                    sp.wait_ge(mod_used, FIRST - 2 * (NW - 1 - st // 2))
                else:
                    sp.wait_ge(w_used, dyn + (st - NW + 1))
                for k in range(UK):
                    sp.dma_start(w_raw[:, st % NW, UC * k:UC * (k + 1)], src(k)).then_inc(w_full[st % NW], 16)

            def load_m(s, kt, dyn=0, sdyn=0):
                t, ms = mod_section(s)
                st = KT * s + kt
                if not (isinstance(sdyn, int) and isinstance(dyn, int)) or st >= FIRST + NMOD:
                    sp.wait_ge(mod_used, sdyn * KT + dyn + (st - NMOD + 1))
                src = mod_v[t][:, bass.ds(dyn + kt, 1), bass.ds(sdyn * D + ms * D, D)]
                sp.dma_start(m_raw[:, st % NMOD], src).then_inc(m_full[st % NMOD], 16)

            def load_pair(wv, col, base, s=None):
                for g in range(2):
                    def one(k, j):
                        load_w(lambda r: wv[:, bass.ds(k * UK + (j * UK + r), 1), col + UC * g:col + UC * (g + 1)], base + GU * g + j, k)
                        if s is not None:
                            load_m(s, GU * g + j, k)
                    steps(sp, GU, 4, one)

            def load_up(layer, p, base, dyn, groups=2, s=None):
                every = groups // 2
                for j in range(GU * groups):
                    k, g = j % GU, j // GU
                    load_w(lambda r: up_v[layer][:, UK * k + r, :, bass.ds(p * 1024 + 512 * g, 512)], base + j, dyn)
                    if s is not None and j % every == every - 1:
                        load_m(s[0], j // every, 0, s[1])

            def load_down(layer, base, sections):
                for g in range(2):
                    s = sections[g]

                    def one(k, j, dyn=0):
                        load_w(lambda r: down_v[layer][:, bass.ds(k * UK + (j * UK + r), 1), UC * g:UC * (g + 1)], base + DU * g + j, k)
                        if s is not None and block_of(j) is not None:
                            load_m(s, block_of(j), dyn)

                    with sp.Fori(0, 2) as i:
                        for j in range(8):
                            one(i * 8, j, i * 6)
                    for j in range(16, DU):
                        one(0, j)

            for n in range(FIRST // 2):
                s, kt = n // (KT // 2), 2 * n % KT
                ge(sp, mod_used, 2 * (n - NW + 1))
                sp.dma_start(first[:, n % NW],
                             mod_v[0][:, kt:kt + 2, D * s:D * (s + 1)]).then_inc(first_full[n % NW], 16)
            for j in range(2 * GU):
                k, g = j % GU, j // GU
                load_w(lambda r: w_in_v[:, UK * k + r, UC * g:UC * g + UC], U_IN + j)
                load_m(G_M0, j)
            load_pair(glu_v, 0, U_GLU, SH_F0)
            load_pair(w_out_v, 0, U_OUT, SC_F0)
            load_up(0, 0, U_UP0, 0, 4, (G_F0, 0))
            load_up(0, 2, U_UP0 + 32, 0, 4, (SH_KV, 0))
            load_up(0, 4, U_UP0 + 64, 0, s=(SC_KV, 0))
            load_up(0, 5, U_UP0 + 80, 0, groups=1)
            load_down(0, U_DOWN0, (SH_M1, SC_M1))
            load_pair(kv_v, 0, U_K, G_M1)
            load_pair(kv_v, D, U_V, SH_F1)
            load_pair(q_v, 0, U_Q, SC_F1)
            load_pair(ao_v, 0, U_AO)
            load_up(1, 0, U_UP1, 0, 4, (G_F1, 0))
            with sp.Fori(0, 3) as i:
                load_up(1, i + 2, U_UP1 + 32, i * 16)
            load_up(1, 5, U_UP1 + 80, 0, groups=1)
            load_down(1, U_DOWN1, (None, None))
            for n in range(2):
                sp.wait_ge(o_copied, 4 * (n + 1))
                for tb in range(TB):
                    sp.dma_start(out[0, P * tb:P * (tb + 1), UC * n:UC * (n + 1)], out_nat[:, tb, UC * n:UC * (n + 1)]).then_inc(stored, 16)
            sp.wait_ge(stored, 64)

        B_C, B_BIAS, B_GAIN, B_CONV, B_X, B_PRM, B_CT, B_BT = 0, 1, 2, 3, 5, 13, 14, 22
        N_BATCH = 30

        @block.gpsimd
        def _(pool):
            pool.memset(ident[:, :], 0.0).then_inc(consts, 1)
            pool.memset(ones[:, :], 1.0).then_inc(consts, 1)
            pool.wait_ge(consts, 2)
            pool.affine_select(out=ident[:, :], in_=ident[:, :], compare_op=ALU.not_equal, fill=1.0, base=0,
                               pattern=[[-1, P]], channel_multiplier=1).then_inc(consts, 1)
            pool.memset(c_nat[:, :, :, :], 0.0).then_inc(c_zero, 1)
            pool.memset(b_bar[:, :, :, :, :], 0.0).then_inc(c_zero, 1)
            pool.memset(half_pi[:, :], PI / 2)
            pool.memset(round_c[:, 0:1], ROUND).then_inc(conv_free, 1)
            pool.memset(round_c[:, 1:2], -ROUND)
            pool.memset(eps[:, :], EPS).then_inc(consts, 1)
            pool.wait_ge(turned_out, B_PRM + 1)
            pool.memset(iota[:, :], 1.0).then_inc(consts, 1)

            def turns(k, dyn=0):
                pool.wait_ge(s_v, dyn + (k + 1))
                pool.tensor_tensor(arg[:, 0], arg[:, 1], arg[:, 0], ALU.subtract).then_inc(s_r, 1)

            def products(k, dyn=0):
                pool.wait_ge(s_z, dyn + (k + 1))
                cos, sin = (tab[:, k % NTAB, n] for n in range(2))
                re, im = (rot[:, k % 2, n] for n in range(2))
                ge(pool, s_y, dyn * 2 + (2 * k - 1))
                pool.tensor_tensor(prod[:, 0], cos, re, ALU.mult)
                pool.tensor_tensor(prod[:, 1], sin, im, ALU.mult).then_inc(s_prod, 1)
                ge(pool, s_y, dyn * 2 + 2 * k)
                pool.tensor_tensor(prod[:, 2], sin, re, ALU.mult)
                pool.tensor_tensor(prod[:, 3], cos, im, ALU.mult).then_inc(s_prod, 1)

            turns(0)
            turns(1)
            for k in range(2, 8):
                turns(k)
                products(k - 2)
            with pool.Fori(0, (S5_STEPS - 8) // 12) as i:
                for k in range(8, 20):
                    turns(k, i * 12)
                    products(k - 2, i * 12)
            products(S5_STEPS - 2)
            products(S5_STEPS - 1)

            def gate(g, base):
                pool.wait_ge(silu_c, g + (base + 1))
                pool.wait_ge(conv_2, g * 4 + (4 * base + 4))
                pool.tensor_tensor(ffg[:, bass.ds(g * 4, 4)], conv[:, 0:4], conv[:, 4:8], ALU.mult).then_inc(conv_free, 1)

            with pool.Fori(0, 11) as g:
                gate(g, 0)
            pool.wait_ge(conv_free, 12)
            pool.memset(fc[:, :, :], 0.0).then_inc(fc_zero, 1)
            pool.memset(mask[:, :], 0.0).then_inc(mask_done, 1)
            pool.wait_ge(mask_done, 1)
            pool.affine_select(out=mask[:, 0:P], in_=mask[:, 0:P], compare_op=ALU.is_ge, fill=MASKED, base=0,
                               pattern=[[-1, P]], channel_multiplier=1).then_inc(mask_done, 1)
            pool.affine_select(out=mask[:, 2 * P:], in_=mask[:, 2 * P:], compare_op=ALU.is_ge, fill=MASKED, base=0,
                               pattern=[[-1, P]], channel_multiplier=1).then_inc(mask_done, 1)
            pool.wait_ge(mod_ready, G_F1)
            pool.memset(sel[:, :, :], 0.0).then_inc(sel_done, 1)
            pool.wait_ge(sel_done, 1)
            pool.affine_select(out=sel[:, :, :], in_=sel[:, :, :], compare_op=ALU.not_equal, fill=1.0, base=0,
                               pattern=[[-1, HEADS], [0, P]], channel_multiplier=1).then_inc(sel_done, 1)
            with pool.Fori(0, 11) as g:
                gate(g, 11)

        @block.scalar
        def _(act):
            act.dma_start(nat[0:KT, 0, :], c.rearrange("a (t p) -> (a t) p", p=P)).then_inc(nat_loaded, 16)
            nb = 0
            act.dma_start(prep[:, 0, :], ssm_a_re[0].rearrange("(j g) p -> j (g p)", g=2)).then_inc(ab_loaded, 16)
            act.dma_start(prep[:, 1, :], ssm_a_im[0].rearrange("(j g) p -> j (g p)", g=2)).then_inc(ab_loaded, 16)
            act.dma_start(step[:, :], ssm_log_step[0].rearrange("(j g) -> j g", g=2)).then_inc(ab_loaded, 16)
            def turn_out(b, dst, n=512):
                act.wait_ge(turned, b + 1)
                act.activation(dst, psum[:, b % 8, 0:n], ACT.Copy).then_inc(turned_out, 1)

            act.wait_ge(nat_loaded, 16)
            act.activation(nat[0:KT, 0, :], nat[0:KT, 0, :], ACT.Silu).then_inc(silu_done, 1)
            act.dma_start(nat[0:96, 1, :], mod_b[0].rearrange("(t p) -> t p", p=P)).then_inc(rest_loaded, 16)
            act.dma_start(nat[0:32, 2, :], kv_mod_b.rearrange("(t p) -> t p", p=P)).then_inc(rest_loaded, 16)
            act.dma_start(nat[0:96, 3, :], mod_b[1].rearrange("(t p) -> t p", p=P)).then_inc(rest_loaded, 16)
            for n, g in enumerate((norm_mix_g.rearrange("a (t p) -> (a t) p", p=P), norm_ffn_g.rearrange("a (t p) -> (a t) p", p=P),
                                   kv_norm_g.rearrange("(t p) -> t p", p=P), final_norm_g.rearrange("(t p) -> t p", p=P),
                                   ssm_glu_b.rearrange("a (t p) -> (a t) p", p=P), ssm_d.rearrange("a (t g) h -> (a t) (g h)", g=8))):
                act.dma_start(nat[nb:nb + g.shape[0], 4, :], g).then_inc(rest_loaded, 16)
                nb += g.shape[0]
            turn_out(B_C, cT[:, :], KT)
            for i in range(2):
                for k in range(3):
                    act.dma_start(nat[0:88, 5 + 4 * i + k, :], ffn_conv_w[i, k].rearrange("(t p) -> t p", p=P)).then_inc(rest_loaded, 16)
                act.dma_start(nat[0:88, 8 + 4 * i, :], ffn_conv_b[i].rearrange("(t p) -> t p", p=P)).then_inc(rest_loaded, 16)
            for tb in range(TB):
                act.dma_start(x_nat[:, tb], x[0, P * tb:P * (tb + 1), :]).then_inc(x_loaded, 16)
            for n, w in enumerate((ssm_b_re, ssm_b_im)):
                act.dma_start(b_raw[:, n], w[0].rearrange("(j g) p h -> (g p) j h", g=2)).then_inc(b_loaded, 16)
            act.wait_ge(c_zero, 1)
            for n, w in enumerate((ssm_c_re, ssm_c_im)):
                wv = w[0].rearrange("(n i g) h p -> i g h n p", i=4, g=2)
                for i in range(4):
                    for g in range(2):
                        at = 32 * i + GW * g
                        act.dma_start(c_nat[at:at + GW, n, :, STATE * g:STATE * (g + 1)], wv[i, g]).then_inc(c_loaded, 16)

            act.wait_ge(ab_loaded, 48)
            act.activation(step[:, :], step[:, :], ACT.Exp).then_inc(prep_act, 1)
            act.wait_ge(prep_dve, 2)
            act.activation(prep[:, 4, :], prep[:, 2, :], ACT.Exp).then_inc(prep_act, 1)
            turn_out(B_BIAS, mod_bias[:, :], 14 * KT)
            turn_out(B_GAIN, gains[:, :], P)
            for i in range(2):
                turn_out(B_CONV + i, convT[:, i], 352)
            for b in range(8):
                turn_out(B_X + b, xT[:, 2 * b:2 * b + 2].rearrange("p t s -> p (t s)"))
            act.wait_ge(prep_dve, 7)
            act.activation(prep[:, 6, :], prep[:, 5, :], ACT.Sin, scale=TWO_PI_DOWN).then_inc(prep_act, 1)
            act.activation(prep[:, 7, :], prep[:, 5, :], ACT.Abs).then_inc(prep_act, 1)
            act.wait_ge(prep_act, 4)
            act.wait_ge(consts, 4)
            act.activation(prep[:, 7, :], prep[:, 7, :], ACT.Sin, scale=-TWO_PI_DOWN, bias=half_pi[0:64, :]).then_inc(prep_act, 1)
            turn_out(B_PRM, prm[:, :, :].rearrange("p a j -> p (a j)"), 4 * ST)
            for n in range(2):
                for b in range(4):
                    turn_out(B_CT + 4 * n + b, c_t[:, n, 4 * b:4 * b + 4].rearrange("p t s -> p (t s)"))
            for n in range(2):
                for b in range(4):
                    turn_out(B_BT + 4 * n + b, b_t[:, n, 4 * b:4 * b + 4].rearrange("p t s -> p (t s)"))

            def hi(st, dyn=0):
                act.wait_ge(w_full[st % NW], dyn * (16 * UK // NW) + 16 * UK * (st // NW + 1))
                if st < NW:
                    act.wait_ge(mod_used, FIRST - 2 * (1 - st // 2))
                act.activation(w_hi[:, st % NW], w_raw[:, st % NW], ACT.Copy).then_inc(hi_done, 1)

            def squares(i, g):
                if g:
                    act.wait_ge(ss_half, i)
                for b in range(4):
                    act.wait_ge(x_out, KT * (i - 1) + 8 * g + 2 * b + 2)
                    act.activation(sqb[:, 2 * b:2 * b + 2], xT[:, 8 * g + 2 * b:8 * g + 2 * b + 2], ACT.Square).then_inc(sq_done, 1)

            def root(i, bank, ahead=None):
                if ahead is not None:
                    hi(ahead)
                    hi(ahead + 1)
                act.wait_ge(ss_done, i + 1)
                act.activation(rstd[:, :], psum[:, bank, 0:S], ACT.Sqrt, scale=1.0 / D, bias=eps[:, :]).then_inc(r_done, 1)

            def norm_hi(buf, shift, n, ahead=None):
                act.wait_ge(mod_ready, shift + 1)
                def one(k, j):
                    act.wait_ge(scaled, k + (KT * n + j + 1))
                    act.activation(h[:, 0, bass.ds(k + j, 1)], buf[:, bass.ds(k + j, 1)], ACT.Identity,
                                   bias=modT[:, shift, bass.ds(k + j, 1)]).then_inc(xhi_done, 1)
                for half in range(2):
                    with act.Fori(2 * half, 2 * half + 2) as i:
                        for j in range(4):
                            one(i * 4, j)
                    if half == 0 and ahead is not None:
                        hi(ahead + 2)

            def ring_hi(src, unit0, i, slots, k=0, t0=None):
                ge(act, w_used, k + (unit0 + i - slots + 1))
                t = 2 * i if t0 is None else t0
                act.activation(h[:, 0, ring(slots, i)], src[:, bass.ds(k * 2 + t, 2)], ACT.Copy).then_inc(xhi_done, 1)

            def plain_pair(base, evac_out=None, norm_next=False):
                for g in range(2):
                    for j in range(GU - LEAD if g and norm_next else GU):
                        hi(base + GU * g + j + LEAD)
                    if evac_out is not None:
                        evac_out(g)

            def copy_out(base, count, dst, scale=1.0, banks=(0, 4)):
                def f(g):
                    act.wait_ge(w_used, base + GU * (g + 1))
                    src = psum[:, banks[g]:banks[g] + 4]
                    if len(dst(g).shape) == 4:
                        src = src.rearrange("p (t b) n -> p t b n", t=TB)
                    act.activation(dst(g), src, ACT.Copy, scale=scale).then_inc(copied, 1)
                return f

            act.wait_ge(turned_out, N_BATCH)
            for b in range(8):
                act.activation(big[:, 0, 2 * b:2 * b + 2], xT[:, 2 * b:2 * b + 2], ACT.Square).then_inc(sq_done, 1)
            root(0, 7)
            for j in range(LEAD):
                hi(U_IN + j)
            norm_hi(big[:, 0], SH_M0, 0)
            plain_pair(U_IN, copy_out(U_IN, 0, lambda g: u_t[:, 8 * g:8 * g + 8].rearrange("p (b t) s -> p b (t s)", b=4)))

            def turns(q):
                ge(act, s_tab, q)
                for e in range(2):
                    a = act.activation(arg[:, 0, e], iota[:, :], ACT.Copy, scale=prm[:, 0, 2 * q + e:2 * q + e + 1])
                a.then_inc(s_t, 1)
                act.wait_ge(s_t, q + 1)
                act.activation(arg[:, 1], arg[:, 0], ACT.Identity, bias=round_c[:, 0:1]).then_inc(s_rnd, 1)
                act.wait_ge(s_rnd, q + 1)
                act.activation(arg[:, 1], arg[:, 1], ACT.Identity, bias=round_c[:, 1:2]).then_inc(s_v, 1)

            def tables(q):
                ge(act, s_prod, 2 * (q - NTAB + 1))
                act.wait_ge(s_r, q + 1)
                act.activation(tab[:, q % NTAB, 1], arg[:, 0], ACT.Sin, scale=-TWO_PI_DOWN)
                act.activation(arg[:, 1], arg[:, 0], ACT.Abs).then_inc(s_abs, 1)
                act.wait_ge(s_abs, q + 1)
                act.activation(tab[:, q % NTAB, 0], arg[:, 1], ACT.Sin, scale=-TWO_PI_DOWN, bias=half_pi[:, :]).then_inc(s_tab, 1)

            act.wait_ge(iota_done, 1)
            turns(0)
            for q in range(2):
                tables(q)
                turns(q + 1)
            for q in range(S5_STEPS + 3):
                if q + 2 < S5_STEPS:
                    tables(q + 2)
                if q + 3 < S5_STEPS:
                    turns(q + 3)
                m = S5_GELU.get(q)
                if m is not None:
                    act.wait_ge(s_yd, 2 * m + 2)
                    act.activation(u_t[:, 2 * m:2 * m + 2], yb[:, :], ACT.Gelu_apprx_tanh).then_inc(s_g, 1)
                    act.wait_ge(s_g, m + 1)
                    ring_hi(u_t, U_GLU, m, 2)
                if q in S5_UNIT:
                    hi(U_GLU + S5_UNIT[q] + LEAD)

            for j in range(S5_UNITS, 2 * GU):
                hi(U_GLU + j + LEAD)
                if j + 2 in range(GU, 2 * GU):
                    ring_hi(u_t, U_GLU, j + 2, 2, t0=2 * ((j + 2) % GU))
                if j % GU < GU - 1:
                    continue
                g = j // GU
                act.wait_ge(w_used, U_GLU + GU * (g + 1))
                for b in range(2):
                    for j in range(4):
                        t = 4 * b + j
                        act.activation(big[:, 1, 8 * g + t], psum[:, 4 * (1 - g) + t // 2, S * (t % 2):S * (t % 2 + 1)], ACT.Sigmoid,
                                       bias=gain(GLUB, 8 * g + t)).then_inc(s_sg, 1)
                for b in range(2):
                    act.wait_ge(s_zg, 2 * g + b + 1)
                    t = 8 * g + 4 * b
                    act.activation(h[:, 0, t:t + 4], big[:, 1, t:t + 4], ACT.Copy).then_inc(zhi_done, 1)
            plain_pair(U_OUT, lambda g: squares(1, g), True)

            def ffn(layer, n, sq, shift, up_base, down_base, gbase, n_sum):
                root(n_sum - 1, 7 if layer == 0 else 3, up_base)
                norm_hi(sq, shift, n, up_base)

                def taps(g, bank):
                    act.wait_ge(conv_free, g + (gbase + 1))
                    act.wait_ge(w_used, g * GU + (up_base + GU))
                    for t in range(8):
                        tile = g * 4 + (t if t < 4 else t - 4 + FT)
                        a = act.activation(conv[:, t], psum[:, bank + t // 2, S * (t % 2):S * (t % 2 + 1)], ACT.Identity,
                                           scale=convT[:, layer, 2, bass.ds(tile, 1)], bias=convT[:, layer, 3, bass.ds(tile, 1)])
                        if t % 2:
                            a.then_inc(conv_act, 1)
                    act.wait_ge(conv_2, g * 4 + (4 * gbase + 2))
                    act.activation(conv[:, 0:4], conv[:, 0:4], ACT.Silu).then_inc(silu_c, 1)

                with act.Fori(0, 5) as p:
                    for g in range(2):
                        for j in range(GU):
                            hi(up_base + GU * g + j + LEAD, p * 16)
                        taps(p * 2 + g, 4 * g)
                for j in range(GU - LEAD):
                    hi(up_base + 10 * GU + j + LEAD)
                act.wait_ge(conv_free, gbase + 3)
                for i in range(LEAD):
                    hi(down_base + i)
                    ring_hi(ffg, down_base, i, 4)
                taps(10, 0)
                act.wait_ge(conv_free, gbase + 12)

                def down(i, k=0):
                    hi(down_base + i, k)
                    ring_hi(ffg, down_base, i, 4, k, t0=2 * (i % DU))

                for g in range(2):
                    steps(act, 16, 4, lambda k, j: down(DU * g + LEAD + j, k))
                    for j in range(16 + LEAD, DU if g else DU + LEAD):
                        down(DU * g + j)
                    squares(n_sum, g)

            ffn(0, 1, big[:, 2], SH_F0, U_UP0, U_DOWN0, 0, 2)

            root(2, 7, U_K)
            act.dma_start(fw_raw[:, :].rearrange("p (t n) -> p t n", t=KT), kv_v[:, :, 2 * D:2 * D + HEADS]).then_inc(fw_loaded, 16)
            act.dma_start(fb[:, :], forget_b.rearrange("(h a) -> h a", a=1)).then_inc(fw_loaded, 16)
            norm_hi(big[:, 0], SH_KV, 2, U_K)
            act.wait_ge(fw_loaded, 32)
            act.activation(fw[:, 0:KT * HEADS], fw_raw[:, :], ACT.Copy).then_inc(fw_split, 1)
            plain_pair(U_K, copy_out(U_K, 2, lambda g: big[:, 0, 8 * g:8 * g + 8].rearrange("p (b t) s -> p b (t s)", b=4)))
            plain_pair(U_V, copy_out(U_V, 4, lambda g: v_nat[:, :, UC * g:UC * g + UC].rearrange("p t (b n) -> p t b n", b=2)))
            norm_hi(big[:, 2], SH_M1, 3)
            copy_q = copy_out(U_Q, 6, lambda g: big[:, 2, 8 * g:8 * g + 8].rearrange("p (b t) s -> p b (t s)", b=4), P ** -0.5, (4, 0))

            def log_f():
                act.wait_ge(f_step, 1)
                act.activation(fc[0:HEADS, 1], fc[0:HEADS, 0], ACT.Abs).then_inc(f_act, 1)
                act.wait_ge(f_act, 1)
                act.activation(fc[0:HEADS, 1], fc[0:HEADS, 1], ACT.Exp, scale=-1.0).then_inc(f_act, 1)
                act.wait_ge(f_act, 2)
                act.activation(fc[0:HEADS, 1], fc[0:HEADS, 1], ACT.Ln, bias=1.0).then_inc(f_act, 1)

            def after_q(g):
                copy_q(g)
                if g == 0:
                    log_f()

            plain_pair(U_Q, after_q)

            def heads(i):
                for e in range(4):
                    act.wait_ge(a_max, i * 4 + (e + 1))
                    for tb, (lo_c, hi_c) in enumerate(((0, P), (P, 3 * P))):
                        a = act.activation(att[:, e, lo_c:hi_c], att[:, e, lo_c:hi_c], ACT.Exp, bias=stat[:, 0, e, tb:tb + 1],
                                           accum_out=stat[:, 1, e, tb:tb + 1])
                    a.then_inc(a_exp, 1)
                for e in range(4):
                    act.wait_ge(a_t, i * 4 + (e + 1))
                    ge(act, a_o, i * 4 + (e - 1))
                    act.activation(att_t[:, e % 2], psum[:, 4 + e % 2, 0:384], ACT.Copy).then_inc(a_tc, 1)
                    if e:
                        out_hi(i, e - 1)
                out_hi(i, 3)

            def out_hi(i, e):
                act.wait_ge(a_o, i * 4 + (e + 1))
                act.activation(h[:, 0, bass.ds(i * 4 + e, 1)], psum[:, 6 + e % 2, 0:S].unsqueeze(1), ACT.Copy).then_inc(a_ohi, 1)

            heads(0)
            with act.Fori(1, 4) as i:
                heads(i)
            plain_pair(U_AO, lambda g: squares(3, g), True)
            ffn(1, 4, big[:, 2], SH_F1, U_UP1, U_DOWN1, 11, 4)

            root(4, 7)
            for b in range(8):
                act.wait_ge(o_turned, b + 1)
                act.activation(out_nat[:, b % TB, 512 * (b // TB):512 * (b // TB + 1)], psum[:, b % 4, :], ACT.Copy).then_inc(o_copied, 1)

        @block.vector
        def _(dve):
            def lo(st, dyn=0):
                dve.wait_ge(hi_done, dyn + (st + 1))
                dve.tensor_tensor(w_lo[:, st % NW], w_raw[:, st % NW], w_hi[:, st % NW].bitcast(F32),
                                  ALU.subtract).then_inc(lo_done, 1)

            def mod_add(s, kt, dyn=0, sdyn=0):
                st = KT * s + kt
                if s < 2:
                    n = st // 2
                    dve.wait_ge(first_full[n % NW], dyn * 2 + 16 * (n // NW + 1))
                    block = first[:, n % NW, kt % 2]
                else:
                    dve.wait_ge(m_full[st % NMOD], sdyn * 128 + dyn * 8 + 16 * ((st - FIRST) // NMOD + 1))
                    block = m_raw[:, st % NMOD]
                if isinstance(dyn, int) and kt == 0:
                    ge(dve, sum_ready, sdyn + s)
                    dve.tensor_scalar(mod_acc[:, :], block, cT[:, 0:1], None, ALU.mult).then_inc(mod_used, 1)
                    return
                dve.wait_ge(mod_used, sdyn * KT + dyn + st)
                dve.scalar_tensor_tensor(out=mod_acc[:, :], in0=block, scalar=cT[:, bass.ds(dyn + kt, 1)],
                                         in1=mod_acc[:, :], op0=ALU.mult, op1=ALU.add).then_inc(mod_used, 1)

            def mod_out(s, bank, sdyn=0):
                dve.wait_ge(sum_ready, sdyn + (s + 1))
                dve.tensor_tensor(modT[:, bass.ds(sdyn + s, 1)], psum[:, bank, 0:KT].unsqueeze(1),
                                  mod_bias[:, bass.ds(sdyn * KT + s * KT, KT)].unsqueeze(1), ALU.add).then_inc(mod_ready, 1)

            def pair(base, evac, s=None, more=False, dyn=0, sdyn=0, first=False, bank=0, norm_next=False):
                if first:
                    for j in range(LEAD):
                        mod_add(s, j, 0, sdyn)
                for j in range(LEAD, 2 * GU):
                    lo(base + j, dyn)
                    if j == GU + LEAD - 1:
                        evac(0)
                    if s is not None:
                        mod_add(s, j, 0, sdyn)
                if norm_next and s is not None:
                    mod_out(s, bank, sdyn)
                for j in range(0 if norm_next else LEAD):
                    lo(base + 2 * GU + j, dyn)
                    if j == 0 and s is not None:
                        mod_out(s, bank, sdyn)
                    if more:
                        mod_add(s + 1, j, 0, sdyn)
                evac(1)

            dve.wait_ge(turned_out, B_C + 1)
            for kt in range(6):
                mod_add(SH_M0, kt)

            RE, IM, DRE, DIM, MAG, TURN, SIN, COS, K1, K2, FR, FI = range(12)
            seen = [0]

            def pd(ins):
                ins.then_inc(prep_dve, 1)
                seen[0] += 1

            def pw():
                dve.wait_ge(prep_dve, seen[0])

            dve.wait_ge(ab_loaded, 48)
            dve.wait_ge(prep_act, 1)
            for src, dst in ((RE, DRE), (IM, DIM)):
                dve.tensor_scalar(prep[:, dst, 0:STATE], prep[:, src, 0:STATE], step[:, 0:1], None, ALU.mult)
                pd(dve.tensor_scalar(prep[:, dst, STATE:], prep[:, src, STATE:], step[:, 1:2], None, ALU.mult))
            mod_add(SH_M0, 6)
            pw()
            pd(dve.tensor_scalar(prep[:, K1, :], prep[:, DIM, :], 1.0 / (2 * PI), ROUND, ALU.mult, ALU.add))
            pw()
            pd(dve.tensor_scalar(prep[:, K1, :], prep[:, K1, :], ROUND, None, ALU.subtract))
            for part in (TWO_PI_1, TWO_PI_2, TWO_PI_3):
                pw()
                ins = dve.scalar_tensor_tensor(out=prep[:, DIM, :], in0=prep[:, K1, :], scalar=-part, in1=prep[:, DIM, :],
                                               op0=ALU.mult, op1=ALU.add)
                if part != TWO_PI_3:
                    pd(ins)
            ins.then_inc(prep_red, 1)
            dve.wait_ge(prep_red, 1)
            dve.tensor_scalar(prep[:, DIM, :], prep[:, DIM, :], 1.0 / (2 * PI), 0.5, ALU.mult, ALU.min).then_inc(prep_red, 1)
            dve.wait_ge(prep_red, 2)
            pd(dve.tensor_scalar(prep[:, TURN, :], prep[:, DIM, :], -0.5, None, ALU.max))
            mod_add(SH_M0, 7)
            dve.wait_ge(prep_act, 5)
            pd(dve.tensor_tensor(prep[:, K1, :], prep[:, MAG, :], prep[:, COS, :], ALU.mult))
            pd(dve.tensor_tensor(prep[:, K2, :], prep[:, MAG, :], prep[:, SIN, :], ALU.mult))
            pd(dve.tensor_tensor(prep[:, FR, :], prep[:, RE, :], prep[:, RE, :], ALU.mult))
            pd(dve.tensor_tensor(prep[:, FI, :], prep[:, IM, :], prep[:, IM, :], ALU.mult))
            pw()
            pd(dve.tensor_scalar(prep[:, K1, :], prep[:, K1, :], -1.0, None, ALU.add))
            pd(dve.tensor_tensor(prep[:, DRE, :], prep[:, FR, :], prep[:, FI, :], ALU.add))
            pw()
            pd(dve.reciprocal(prep[:, DRE, :], prep[:, DRE, :]))
            for dst, (a, b), (e, f), op in ((FR, (K1, RE), (K2, IM), ALU.add), (FI, (K2, RE), (K1, IM), ALU.subtract)):
                pd(dve.tensor_tensor(prep[:, dst, :], prep[:, a, :], prep[:, b, :], ALU.mult))
                pd(dve.tensor_tensor(prep[:, DIM, :], prep[:, e, :], prep[:, f, :], ALU.mult))
                pw()
                pd(dve.tensor_tensor(prep[:, dst, :], prep[:, dst, :], prep[:, DIM, :], op))
                pw()
                pd(dve.tensor_tensor(prep[:, dst, :], prep[:, dst, :], prep[:, DRE, :], ALU.mult))
            pw()
            assert seen[0] == PREP_DVE
            mod_add(SH_M0, 8)
            mod_add(SH_M0, 9)
            dve.wait_ge(turned_out, B_PRM + 1)
            dve.wait_ge(b_loaded, 32)
            dve.wait_ge(c_zero, 2)
            f_r, f_i = (prm[:, n, :].unsqueeze(2).to_broadcast([P, ST, GW]) for n in (2, 3))
            for n, (a, b, op) in enumerate(((0, 1, ALU.subtract), (1, 0, ALU.add))):
                if n:
                    dve.wait_ge(bar_done, 4)
                dve.tensor_tensor(b_tmp[:, 0], b_raw[:, a], f_r, ALU.mult).then_inc(bar_done, 1)
                dve.tensor_tensor(b_tmp[:, 1], b_raw[:, b], f_i, ALU.mult).then_inc(bar_done, 1)
                dve.wait_ge(bar_done, 4 * n + 2)
                for g in range(2):
                    r = slice(STATE * g, STATE * (g + 1))
                    dve.tensor_tensor(b_bar[r, n, :, g, :], b_tmp[r, 0], b_tmp[r, 1], op).then_inc(bar_done, 1)
                mod_add(SH_M0, 10 + n)
            dve.wait_ge(consts, 5)
            dve.tensor_tensor_scan(out=iota[:, :], data0=iota[:, :], data1=iota[:, :], initial=0.0, op0=ALU.mult,
                                   op1=ALU.add).then_inc(iota_done, 1)
            for kt in range(12, KT):
                mod_add(SH_M0, kt)
            for kt in range(KT):
                mod_add(SC_M0, kt)

            def inverse(i):
                dve.wait_ge(r_done, 2 * i + 1)
                dve.reciprocal(rstd[:, :], rstd[:, :]).then_inc(r_done, 1)
                dve.wait_ge(r_done, 2 * i + 2)

            def norm(n, buf, scale, shift, g, sums=None, ahead=None):
                if ahead is not None:
                    lo(ahead[0])
                    lo(ahead[0] + 1)
                if sums is not None:
                    inverse(sums)
                if scale is None:
                    gain_of = lambda kt: gains[:, bass.ds(g * KT + kt, 1)]
                else:
                    dve.wait_ge(mod_ready, scale + 1)
                    dve.scalar_tensor_tensor(out=gs[:, :], in0=modT[:, scale], scalar=1.0, in1=gain(g), op0=ALU.add,
                                             op1=ALU.mult).then_inc(gs_done, 1)
                    dve.wait_ge(gs_done, n + 1)
                    gain_of = lambda kt: gs[:, bass.ds(kt, 1)]

                def scale_x(k, j):
                    dve.scalar_tensor_tensor(out=buf[:, bass.ds(k + j, 1)], in0=xT[:, bass.ds(k + j, 1)], scalar=gain_of(k + j),
                                             in1=rstd[:, :].unsqueeze(1), op0=ALU.mult, op1=ALU.mult).then_inc(scaled, 1)

                def rest(k, j):
                    dve.wait_ge(xhi_done, k + (XN[n] + j + 1))
                    dve.scalar_tensor_tensor(out=h[:, 1, bass.ds(k + j, 1)], in0=buf[:, bass.ds(k + j, 1)],
                                             scalar=modT[:, shift, bass.ds(k + j, 1)], in1=h[:, 0, bass.ds(k + j, 1)].bitcast(F32),
                                             op0=ALU.add, op1=ALU.subtract).then_inc(xlo_done, 1)

                if scale is None:
                    steps(dve, KT, 4, scale_x)
                    return
                def four(k):
                    for j in range(4):
                        scale_x(k, j)
                    for j in range(4):
                        rest(k, j)

                with dve.Fori(0, 2) as i:
                    four(i * 4)
                if ahead is not None:
                    lo(ahead[0] + 2)
                    if ahead[1] is not None:
                        mod_add(ahead[1], 0)
                with dve.Fori(2, 4) as i:
                    four(i * 4)
                if ahead is not None and ahead[1] is not None:
                    for j in range(1, LEAD):
                        mod_add(ahead[1], j)

            def ring_lo(src, i, count, slots, k=0, t0=None):
                dve.wait_ge(xhi_done, k + (count + i + 1))
                t = 2 * i if t0 is None else t0
                r = ring(slots, i)
                dve.tensor_tensor(h[:, 1, r], src[:, bass.ds(k * 2 + t, 2)], h[:, 0, r].bitcast(F32), ALU.subtract).then_inc(xlo_done, 1)

            def add_to_x(base, units, section, banks=(0, 4)):
                def f(g):
                    dve.wait_ge(w_used, base + units * (g + 1))
                    dve.wait_ge(mod_ready, section + 1)
                    for t in range(8):
                        ins = dve.scalar_tensor_tensor(out=xT[:, 8 * g + t], in0=psum[:, banks[g] + t // 2, S * (t % 2):S * (t % 2 + 1)],
                                                       scalar=modT[:, section, 8 * g + t:8 * g + t + 1], in1=xT[:, 8 * g + t],
                                                       op0=ALU.mult, op1=ALU.add)
                        ins.then_inc(x_out, 1)
                return f

            none = lambda g: None

            inverse(0)
            for j in range(LEAD):
                lo(U_IN + j)
            mod_out(SH_M0, 0)
            mod_out(SC_M0, 1)
            norm(0, big[:, 0], SC_M0, SH_M0, NM0)
            pair(U_IN, none, G_M0, True, first=True)

            def states(q):
                dve.wait_ge(s_bu, q + 1)
                dve.wait_ge(s_tab, q + 1)
                ge(dve, s_prod, 2 * (q - 1))
                b = q % 2
                cos, sin = (tab[:, q % NTAB, n] for n in range(2))
                r = [rot[:, b, n] for n in range(2)]
                t = [tmp[:, n] for n in range(2)]
                re, im = (psum[:, 0:2, S * n:S * (n + 1)] for n in range(2))
                ge(dve, s_rota, q)
                dve.tensor_tensor(r[0], re, cos, ALU.mult)
                dve.tensor_tensor(t[0], im, sin, ALU.mult)
                dve.tensor_tensor(r[1], im, cos, ALU.mult)
                dve.tensor_tensor(t[1], re, sin, ALU.mult).then_inc(s_rotm, 1)
                dve.wait_ge(s_rotm, q + 1)
                for n in range(2):
                    ins = dve.tensor_tensor(r[n], r[n], t[n], (ALU.add, ALU.subtract)[n])
                ins.then_inc(s_rota, 1)
                dve.wait_ge(s_rota, q + 1)
                for e in range(2):
                    decay = prm[:, 1, 2 * q + e:2 * q + e + 1].to_broadcast([P, S])
                    for n in range(2):
                        ins = dve.tensor_tensor_scan(out=rot[:, b, n, e], data0=decay, data1=rot[:, b, n, e], initial=0.0,
                                                     op0=ALU.mult, op1=ALU.add)
                ins.then_inc(s_z, 1)

            def skip(kt):
                dve.wait_ge(s_y, 4 * (kt + 1))
                ge(dve, s_g, kt // 2)
                dve.scalar_tensor_tensor(out=yb[:, kt % 2], in0=u_t[:, kt], scalar=gain(SKIP, kt),
                                         in1=psum[:, 2 + kt % 2, 0:S], op0=ALU.mult, op1=ALU.add).then_inc(s_du, 1)
                dve.wait_ge(s_du, kt + 1)
                dve.tensor_tensor(yb[:, kt % 2], yb[:, kt % 2], psum[:, 2 + kt % 2, S:2 * S], ALU.subtract).then_inc(s_yd, 1)

            dve.wait_ge(copied, 2)
            for q in range(S5_STEPS + 5):
                if q < S5_STEPS:
                    states(q)
                if q % 2 and (q - 3) // 2 in range(KT):
                    skip((q - 3) // 2)
                if q - 2 in S5_GELU:
                    ring_lo(u_t, S5_GELU[q - 2], XG, 2)
                if q - 2 in S5_UNIT:
                    lo(U_GLU + S5_UNIT[q - 2] + LEAD)
                    mod_add(SH_F0, S5_UNIT[q - 2] + LEAD)

            def sigmoid_gate(g):
                for b in range(2):
                    t = 8 * g + 4 * b
                    dve.wait_ge(s_sg, t + 4)
                    dve.tensor_tensor(big[:, 1, t:t + 4], big[:, 1, t:t + 4], big[:, 0, t:t + 4], ALU.mult).then_inc(s_zg, 1)
                for b in range(2):
                    t = 8 * g + 4 * b
                    dve.wait_ge(zhi_done, 2 * g + b + 1)
                    dve.tensor_tensor(h[:, 1, t:t + 4], big[:, 1, t:t + 4], h[:, 0, t:t + 4].bitcast(F32), ALU.subtract).then_inc(zlo_done, 1)

            for j in range(S5_UNITS + LEAD, 2 * GU + LEAD):
                lo(U_GLU + j)
                if j - 1 in range(GU, 2 * GU):
                    ring_lo(u_t, j - 1, XG, 2, t0=2 * ((j - 1) % GU))
                if j == 2 * GU:
                    mod_out(SH_F0, 4)
                if j == GU + LEAD - 1:
                    sigmoid_gate(0)
                mod_add(SH_F0 + j // (2 * GU), j % (2 * GU))
            sigmoid_gate(1)
            pair(U_OUT, add_to_x(U_OUT, GU, G_M0, (4, 0)), SC_F0, bank=4, norm_next=True)

            def ffn(layer, n, sq, scale, shift, gate_s, sums, up_base, down_base, gbase, count, sections):
                norm(n, sq, scale, shift, NF0 + layer, sums, ahead=(up_base, None))

                def taps(g, bank):
                    for b in range(4):
                        dve.wait_ge(conv_act, g * 4 + (4 * gbase + b + 1))
                        for lag, tap, done in ((1, 1, conv_1), (2, 0, conv_2)):
                            if lag == 2:
                                dve.wait_ge(conv_1, g * 4 + (4 * gbase + b + 1))
                            for t in (2 * b, 2 * b + 1):
                                tile = g * 4 + (t if t < 4 else t - 4 + FT)
                                c0 = S * (t % 2)
                                ins = dve.scalar_tensor_tensor(
                                    out=conv[:, t, lag:], in0=psum[:, bank + b, c0:c0 + S - lag],
                                    scalar=convT[:, layer, tap, bass.ds(tile, 1)], in1=conv[:, t, lag:], op0=ALU.mult, op1=ALU.add)
                            ins.then_inc(done, 1)

                def two_pairs(base, i, g0, s):
                    for j in range(LEAD, 4 * GU + LEAD):
                        lo(base + j, i * 32)
                        if j == LEAD:
                            mod_add(s, 0, 0, i)
                            mod_add(s, 1, 0, i)
                        if j == 4 * GU:
                            mod_out(s, 0, i)
                        if j >= GU and j % GU == LEAD - 1:
                            g = j // GU - 1
                            taps(i * 4 + (g0 + g), 4 * (g % 2))
                        if j % 2 and LEAD < j < 4 * GU:
                            mod_add(s, j // 2, 0, i)

                if layer == 0:
                    with dve.Fori(0, 2) as i:
                        two_pairs(up_base, i, 0, G_F0)
                    pair(up_base + 64, lambda g: taps(8 + g, 4 * g), SC_KV, first=True)
                else:
                    two_pairs(up_base, 0, 0, G_F1)
                    with dve.Fori(0, 3) as p:
                        pair(up_base + 32, lambda g: taps(p * 2 + (4 + g), 4 * g), dyn=p * 16)
                for j in range(LEAD, GU):
                    lo(up_base + 10 * GU + j)
                for i in range(LEAD):
                    lo(down_base + i)
                    ring_lo(ffg, i, count, 4)
                taps(10, 0)
                out = add_to_x(down_base, DU, gate_s, (4, 0))
                for g in range(2):
                    s = sections[g]
                    more = layer == 0

                    def down(j, k=0, dyn=0):
                        lo(down_base + DU * g + j, k)
                        ring_lo(ffg, DU * g + j, count, 4, k, t0=2 * (j % DU))
                        if s is not None and j < DU and block_of(j) is not None:
                            mod_add(s, block_of(j), dyn)

                    if s is not None and g == 0:
                        for j in range(LEAD):
                            mod_add(s, j)
                    with dve.Fori(0, 2) as i:
                        for j in range(LEAD, LEAD + 8):
                            down(j, i * 8, i * 6)
                    for j in range(16 + LEAD, DU if g else DU + LEAD):
                        down(j)
                        if j == DU and s is not None:
                            mod_out(s, BANK_DOWN[g])
                        if j >= DU and more:
                            mod_add(s + 1, j - DU)
                    if g and s is not None:
                        mod_out(s, BANK_DOWN[g])
                    out(g)

            ffn(0, 1, big[:, 2], SC_F0, SH_F0, G_F0, 1, U_UP0, U_DOWN0, 0, XD0, (SH_M1, SC_M1))

            norm(2, big[:, 0], SC_KV, SH_KV, NKV, 2, ahead=(U_K, G_M1))
            dve.wait_ge(fw_split, 1)
            dve.memset(fw[:, 2 * KT * HEADS:].bitcast(F32), 0.0)
            dve.tensor_tensor(fw[:, KT * HEADS:2 * KT * HEADS], fw_raw[:, :], fw[:, 0:KT * HEADS].bitcast(F32),
                              ALU.subtract).then_inc(fw_split, 1)
            pair(U_K, none, G_M1, True)
            pair(U_V, none, SH_F1, True)
            dve.wait_ge(f_sum, 1)

            norm(3, big[:, 2], SC_M1, SH_M1, NM1)

            def f_sums(g):
                if g:
                    return
                dve.wait_ge(fc_zero, 1)
                dve.tensor_scalar(fc[0:HEADS, 0], psum[0:HEADS, 1, 0:S], fb[:, :], None, ALU.add).then_inc(f_step, 1)
                dve.wait_ge(f_act, 3)
                dve.tensor_scalar(fc[0:HEADS, 0], fc[0:HEADS, 0], 0.0, None, ALU.min).then_inc(f_step, 1)
                dve.memset(fc[0:HEADS, 2], 1.0).then_inc(f_step, 1)
                dve.wait_ge(f_step, 3)
                dve.tensor_tensor(fc[0:HEADS, 0], fc[0:HEADS, 0], fc[0:HEADS, 1], ALU.subtract).then_inc(f_step, 1)
                dve.wait_ge(f_step, 4)
                dve.tensor_tensor_scan(out=fc[0:HEADS, 3], data0=fc[0:HEADS, 2], data1=fc[0:HEADS, 0], initial=0.0, op0=ALU.mult,
                                       op1=ALU.add).then_inc(f_step, 1)
                dve.wait_ge(f_step, 5)
                dve.tensor_scalar(fc[0:HEADS, 1], fc[0:HEADS, 3], -1.0, None, ALU.mult).then_inc(f_cum, 1)

            pair(U_Q, f_sums, SC_F1, bank=4)

            def heads(i):
                for e in range(4):
                    dve.wait_ge(a_s, i * 4 + (e + 1))
                    ge(dve, a_t, i * 4 + (e - 3))
                    for tb, (c0, c1) in enumerate(((0, P), (P, 3 * P))):
                        ins = dve.scalar_tensor_tensor(out=att[:, e, c0:c1], in0=psum[:, e, c0:c1], scalar=fq[:, tb, bass.ds(i * 4 + e, 1)],
                                                       in1=mask[:, c0:c1], op0=ALU.add, op1=ALU.add)
                    ins.then_inc(a_masked, 1)
                    dve.wait_ge(a_masked, i * 4 + (e + 1))
                    for tb, (c0, c1) in enumerate(((0, P), (P, 3 * P))):
                        ins = dve.tensor_reduce(stat[:, 0, e, tb:tb + 1], att[:, e, c0:c1], AX_X, ALU.max, negate=True)
                    ins.then_inc(a_max, 1)
                for e in range(4):
                    dve.wait_ge(a_exp, i * 4 + (e + 1))
                    dve.reciprocal(stat[:, 2, e, :], stat[:, 1, e, :]).then_inc(a_rec, 1)
                    dve.wait_ge(a_rec, i * 4 + (e + 1))
                    for tb, (c0, c1) in enumerate(((0, P), (P, 3 * P))):
                        ins = dve.tensor_scalar(att[:, e, c0:c1], att[:, e, c0:c1], stat[:, 2, e, tb:tb + 1], None, ALU.mult)
                    ins.then_inc(a_p, 1)
                for e in range(4):
                    dve.wait_ge(a_ohi, i * 4 + (e + 1))
                    hd = bass.ds(i * 4 + e, 1)
                    dve.tensor_tensor(h[:, 1, hd], psum[:, 6 + e % 2, 0:S].unsqueeze(1), h[:, 0, hd].bitcast(F32),
                                      ALU.subtract).then_inc(a_olo, 1)

            dve.wait_ge(mask_done, 3)
            dve.wait_ge(f_turn, 1)
            dve.tensor_copy(fq[:, :, :], psum[:, 7, 0:TB * HEADS].rearrange("p (t n) -> p t n", t=TB)).then_inc(f_query, 1)
            dve.wait_ge(f_query, 1)
            heads(0)
            with dve.Fori(1, 4) as i:
                heads(i)
            pair(U_AO, add_to_x(U_AO, GU, G_M1), norm_next=True)
            ffn(1, 4, big[:, 2], SC_F1, SH_F1, G_F1, 3, U_UP1, U_DOWN1, 11, XD1, (None, None))

            norm(5, big[:, 0], None, None, NFIN, 4)

        @block.tensor
        def _(pe):
            mm = lambda out, a, b, start=False: pe.matmul(out, a, b, start=start, stop=False, skip_group_check=True)

            def turn(b, blocks, ready=None):
                if ready is not None:
                    pe.wait_ge(*ready)
                ge(pe, turned_out, b - 7)
                c0 = 0
                for src in blocks:
                    n = src.shape[0]
                    ins = pe.transpose(psum[0:src.shape[1], b % 8, c0:c0 + n], src, ident[0:n, 0:n])
                    c0 += n
                ins.then_inc(turned, 1)

            def mod_sum(s, bank, sdyn=0):
                pe.wait_ge(mod_used, sdyn * KT + KT * (s + 1))
                for kt in range(KT):
                    ins = mm(psum[:, bank, kt:kt + 1], mod_acc[:, P * kt:P * (kt + 1)], ones[:, 0:1], kt == 0)
                ins.then_inc(sum_ready, 1)

            pe.wait_ge(consts, 3)
            turn(B_C, [nat[0:KT, 0, :]], (silu_done, 1))
            turn(B_BIAS, [nat[0:96, 1, :], nat[0:32, 2, :], nat[0:96, 3, :]], (rest_loaded, 16 * 17))
            turn(B_GAIN, [nat[:, 4, :]])
            for i in range(2):
                turn(B_CONV + i, [nat[0:88, 5 + 4 * i + k, :] for k in range(4)])
            for b in range(8):
                turn(B_X + b, [x_nat[:, tb, P * kt:P * (kt + 1)] for kt in (2 * b, 2 * b + 1) for tb in range(TB)], (x_loaded, 32))
            turn(B_PRM, [prep[:, n, :] for n in (5, 4, 10, 11)], (prep_dve, PREP_DVE))
            for n in range(2):
                for b in range(4):
                    turn(B_CT + 4 * n + b, [c_nat[:, n, 4 * b + i, :] for i in range(4)], (c_loaded, 256))
            for n in range(2):
                for b in range(4):
                    turn(B_BT + 4 * n + b, [b_bar[:, n, 16 * b + 4 * i:16 * b + 4 * i + 4].rearrange("p j g h -> p (j g h)")
                                            for i in range(4)], (bar_done, 4 * n + 4))
            pe.wait_ge(turned_out, N_BATCH)

            def sums(i, g, buf, bank):
                for kt in range(8):
                    if kt % 2 == 0:
                        pe.wait_ge(sq_done, 8 * i + 4 * g + kt // 2 + 1)
                    ins = mm(psum[:, bank, 0:S], ones[:, :], buf[:, kt], g == 0 and kt == 0)
                ins.then_inc(ss_done if g else ss_half, 1)

            def unit(st, dyn, bank, xt, x_ready, first=False, blocks=range(UK)):
                if 0 in blocks:
                    pe.wait_ge(lo_done, dyn + (st + 1))
                    for sem_, value in x_ready:
                        pe.wait_ge(sem_, value)
                sl = st % NW
                for k in blocks:
                    x_hi, x_lo = xt(k)
                    for t in range(8):
                        c0 = k * UC + P * t
                        wh, wl = w_hi[:, sl, c0:c0 + P], w_lo[:, sl, c0:c0 + P]
                        acc = psum[:, bank + t // 2, S * (t % 2):S * (t % 2 + 1)]
                        mm(acc, wh, x_hi, first and k == 0 and t % 2 == 0)
                        mm(acc, wh, x_lo)
                        ins = mm(acc, wl, x_hi)
                if UK - 1 in blocks:
                    ins.then_inc(w_used, 1)

            def group(base, n, bank, xt, ready, dyn=0, before={}):
                def one(k, j, first=False):
                    unit(base + j, dyn + k, bank, lambda r: xt(k, j, r), ready(k, j), first)

                def straight(units):
                    for j in units:
                        if j in before:
                            before[j]()
                        one(0, j, j == 0)

                if n < 3 * NW:
                    straight(range(n))
                    return
                straight(range(NW))
                if NW in before:
                    before[NW]()
                with pe.Fori(0, n // NW - 1) as i:
                    for j in range(NW):
                        one(i * NW, NW + j)
                straight(range(n // NW * NW, n))

            def h_group(base, bank, dyn=0, made=None, before={}):
                group(base, GU, bank, lambda k, j, r: [flat(h[:, n, bass.ds(k * UK + (j * UK + r), 1)]) for n in range(2)],
                      lambda k, j: [(made[0], k * UK + (made[1] + UK * (j + 1)))] if made else [], dyn, before)

            def h_pair(base, made=None, banks=(0, 4), s=None, dyn=0, sdyn=0, before={}):
                h_group(base, banks[0], dyn, made)
                h_group(base + GU, banks[1], dyn,
                        before={**before, **({} if s is None else {GU - 1: lambda: mod_sum(s, banks[0], sdyn)})})
                if s is not None:
                    pe.wait_ge(mod_ready, sdyn + (s + 1))

            def ring_group(stage, first_unit, n, bank, count, slots, before={}):
                def tiles(k, j, r):
                    t = ring(slots, first_unit + j).start + r
                    return h[:, 0, t], h[:, 1, t]
                group(stage + first_unit, n, bank, tiles, lambda k, j: [(xlo_done, k + (count + first_unit + j + 1))], before=before)

            for g in range(2):
                sums(0, g, big[:, 0, 8 * g:8 * g + 8], 7)
            mod_sum(SH_M0, 0)
            mod_sum(SC_M0, 1)
            pe.wait_ge(mod_ready, 2)
            h_pair(U_IN, (xlo_done, XN[0]), s=G_M0)

            def inputs(q):
                ge(pe, s_rotm, q)
                for part in range(2):
                    for e in range(2):
                        r = slice(32 * (2 * (q % 2) + e), 32 * (2 * (q % 2) + e) + 32)
                        ins = mm(psum[:, e, S * part:S * (part + 1)], b_t[r, part, q // 2], u_t[r, q // 2], part == 0)
                ins.then_inc(s_bu, 1)

            def outputs(q):
                if q % 2 == 0:
                    ge(pe, s_yd, q // 2 - 1)
                for half in range(2):
                    pe.wait_ge(s_prod, 2 * q + half + 1)
                    for e in range(2):
                        r = slice(32 * (2 * (q % 2) + e), 32 * (2 * (q % 2) + e) + 32)
                        for i in range(2):
                            n = min(half + i, 1)
                            ins = mm(psum[r, 2 + q // 2 % 2, S * n:S * (n + 1)], c_t[:, half, q // 2, r], prod[:, 2 * half + i, e], half == 0 and i == 0)
                    ins.then_inc(s_y, 1)

            def glu_unit(i, blocks=range(UK)):
                t = ring(2, i).start
                unit(U_GLU + i, 0, 4, lambda k: (h[:, 0, t + k], h[:, 1, t + k]), [(xlo_done, XG + i + 1)], i == 0, blocks)

            pe.wait_ge(copied, 2)
            inputs(0)
            inputs(1)
            for q in range(S5_STEPS):
                if q + 2 < S5_STEPS:
                    inputs(q + 2)
                outputs(q)
                for k in range(UK):
                    if q - k - 1 in S5_UNIT:
                        glu_unit(S5_UNIT[q - k - 1], [k])
            for i in range(S5_UNITS, GU):
                glu_unit(i)
            ring_group(U_GLU, GU, GU, 0, XG, 2, {GU - 1: lambda: mod_sum(SH_F0, 4)})
            pe.wait_ge(mod_ready, SH_F0 + 1)
            pe.wait_ge(zlo_done, 4)
            h_pair(U_OUT, banks=(4, 0), s=SC_F0, before={NW: lambda: sums(1, 0, sqb, 7)})
            sums(1, 1, sqb, 7)

            def ffn(n_sum, up_base, down_base, x0, count, sections):
                def two_pairs(i, s):
                    h_pair(up_base, (xlo_done, x0), dyn=i * 32)
                    h_pair(up_base + 16, s=s, dyn=i * 32, sdyn=i)

                if sections[0] is not None:
                    with pe.Fori(0, 2) as i:
                        two_pairs(i, G_F0)
                    h_pair(up_base + 64, s=SC_KV)
                else:
                    two_pairs(0, G_F1)
                    with pe.Fori(0, 3) as p:
                        h_pair(up_base + 32, dyn=p * 16)
                h_group(up_base + 10 * GU, 0)
                for g in range(2):
                    before = {NW: lambda: sums(n_sum, 0, sqb, 7)} if g else {}
                    if sections[g] is not None:
                        before[DU - 1] = lambda: mod_sum(sections[g], BANK_DOWN[g])
                    ring_group(down_base, DU * g, DU, 4 * (1 - g), count, 4, before)
                    if sections[g] is not None:
                        pe.wait_ge(mod_ready, sections[g] + 1)
                sums(n_sum, 1, sqb, 7)

            ffn(2, U_UP0, U_DOWN0, XN[1], XD0, (SH_M1, SC_M1))

            h_pair(U_K, (xlo_done, XN[2]), s=G_M1)

            def v_unit(st, bank, kt, first=False):
                pe.wait_ge(lo_done, st + 1)
                sl = st % NW
                for k in range(UK):
                    for tb in range(TB):
                        x_hi, x_lo = (h[:, n, kt + k, P * tb:P * (tb + 1)] for n in range(2))
                        acc = [psum[:, bank + 2 * tb + e] for e in range(2)]
                        wh, wl = ([w[:, sl, k * UC + 512 * e:k * UC + 512 * (e + 1)] for e in range(2)] for w in (w_hi, w_lo))
                        for e in range(2):
                            mm(acc[e], x_hi, wh[e], first and k == 0)
                        for e in range(2):
                            mm(acc[e], x_hi, wl[e])
                        for e in range(2):
                            ins = mm(acc[e], x_lo, wh[e])
                ins.then_inc(w_used, 1)

            for g in range(2):
                for j in range(GU):
                    if g and j == GU - 1:
                        mod_sum(SH_F1, 0)
                    v_unit(U_V + GU * g + j, 4 * g, UK * j, j == 0)
            pe.wait_ge(mod_ready, SH_F1 + 1)
            pe.wait_ge(fw_split, 2)
            for kt in range(KT):
                wh, wl = (fw[:, HEADS * (KT * n + kt):HEADS * (KT * n + kt) + P] for n in range(2))
                mm(psum[:, 1, 0:S], wh, h[:, 0, kt], kt == 0)
                mm(psum[:, 1, 0:S], wh, h[:, 1, kt])
                ins = mm(psum[:, 1, 0:S], wl, h[:, 0, kt])
            ins.then_inc(f_sum, 1)

            h_group(U_Q, 4, made=(xlo_done, XN[3]))
            pe.wait_ge(f_step, 1)
            h_group(U_Q + GU, 0, before={GU - 1: lambda: mod_sum(SC_F1, 4)})
            pe.wait_ge(mod_ready, SC_F1 + 1)

            def scores(i, e):
                n = 4 * i + e
                ge(pe, a_masked, n - 3)
                sc, q_h, k_h = psum[:, e], big[:, 2, n], big[:, 0, n]
                mm(sc[:, 0:P], q_h[:, 0:P], k_h[:, 0:P], True)
                mm(sc[:, P:3 * P], q_h[:, P:S], k_h)
                mm(sc[:, 0:P], sel[:, n], fc[:, 1, 0:P])
                mm(sc[:, P:3 * P], sel[:, n], fc[:, 1, :]).then_inc(a_s, 1)

            def heads(i):
                def turn_p(e):
                    pe.wait_ge(a_p, i * 4 + (e + 1))
                    ge(pe, a_tc, i * 4 + (e - 1))
                    for b in range(3):
                        ins = pe.transpose(psum[:, 4 + e % 2, P * b:P * (b + 1)], att[:, e, P * b:P * (b + 1)], ident[:, :])
                    ins.then_inc(a_t, 1)

                def values(e):
                    pe.wait_ge(a_tc, i * 4 + (e + 1))
                    ge(pe, a_olo, i * 4 + (e - 1))
                    v_h = [v_nat[:, tb, 512 * i + P * e:512 * i + P * (e + 1)] for tb in range(TB)]
                    mm(psum[:, 6 + e % 2, 0:S], v_h[0], att_t[:, e % 2, 0:S], True)
                    mm(psum[:, 6 + e % 2, P:S], v_h[1], att_t[:, e % 2, S:3 * P]).then_inc(a_o, 1)

                for e in range(4):
                    scores(i, e)
                for e in range(4):
                    turn_p(e)
                    if e:
                        values(e - 1)
                values(3)

            pe.wait_ge(copied, 8)
            pe.wait_ge(sel_done, 2)
            pe.wait_ge(f_cum, 1)
            for tb in range(TB):
                ins = pe.transpose(psum[:, 7, HEADS * tb:HEADS * (tb + 1)], fc[0:HEADS, 3, P * tb:P * (tb + 1)], ident[0:HEADS, 0:HEADS])
            ins.then_inc(f_turn, 1)
            for i in range(4):
                heads(i)
            h_pair(U_AO, (a_olo, 0), before={NW: lambda: sums(3, 0, sqb, 3)})
            sums(3, 1, sqb, 3)
            ffn(4, U_UP1, U_DOWN1, XN[4], XD1, (None, None))

            for b in range(8):
                pe.wait_ge(scaled, 5 * KT + 4 * (b // TB + 1))
                ge(pe, o_copied, b - 3)
                for j in range(4):
                    ins = pe.transpose(psum[:, b % 4, P * j:P * (j + 1)],
                                       big[:, 0, 4 * (b // TB) + j, P * (b % TB):P * (b % TB + 1)], ident[:, :])
                ins.then_inc(o_turned, 1)


_INS = ['x', 'c', 'mod_w', 'mod_b', 'norm_mix_g', 'norm_ffn_g', 'ssm_w_in', 'ssm_log_step', 'ssm_a_re', 'ssm_a_im',
        'ssm_b_re', 'ssm_b_im', 'ssm_c_re', 'ssm_c_im', 'ssm_d', 'ssm_glu_w', 'ssm_glu_b', 'ssm_w_out', 'kv_mod_w',
        'kv_mod_b', 'kv_norm_g', 'kv_w', 'forget_b', 'attn_w_q', 'attn_w_out', 'ffn_w_up', 'ffn_conv_w', 'ffn_conv_b',
        'ffn_w_down', 'final_norm_g']


def kernel(**inputs):
    import numpy as _np
    import concourse.bacc as _bacc
    from concourse import mybir as _mybir
    from concourse.bass_utils import run_bass_kernel_spmd as _run

    nc = _bacc.Bacc("TRN2", target_bir_lowering=False, num_devices=1)
    arrays, args = {}, []
    for name in _INS:
        a = _np.ascontiguousarray(inputs[name])
        arrays[f"in_{name}_dram"] = a
        args.append(nc.dram_tensor(f"in_{name}_dram", a.shape, _mybir.dt.from_np(a.dtype), kind="ExternalInput").ap())
    args.append(nc.dram_tensor("out_0_dram", (1, S, D), _mybir.dt.float32, kind="ExternalOutput").ap())
    trunk(nc, *args)
    r = _run(nc, [arrays], core_ids=[0])
    return r.results[0]["out_0_dram"]
```
